# Optimizing a Trainium2 kernel written in Bass

```python
import math
import jax
import jax.numpy as jnp
from jax import lax
import numpy as np
import math, functools
import jax, jax.numpy as jnp

D_MODEL = 1024
BATCH = 1
SEQ = 512
DEPTH = 1

ATT_HEADS = 8
ATT_HEAD_DIM = 64
ATT_QK_WIDTH = ATT_HEADS * 2 * ATT_HEAD_DIM
ATT_V_WIDTH = ATT_HEADS * 2 * ATT_HEAD_DIM
ROPE_THETA = 10000.0
Q_BLOCK = 128
SSD_EXPAND = 2
SSD_INNER = SSD_EXPAND * D_MODEL
SSD_HEAD_DIM = 64
SSD_HEADS = SSD_INNER // SSD_HEAD_DIM
SSD_GROUPS = 8
SSD_HEADS_PER_GROUP = SSD_HEADS // SSD_GROUPS
SSD_STATE = 128
SSD_CONV = 4
SSD_CONV_CH = SSD_INNER + 2 * SSD_GROUPS * SSD_STATE
SSD_CHUNK = 128
IN_SPLITS = (ATT_QK_WIDTH, ATT_QK_WIDTH, ATT_V_WIDTH, SSD_INNER, SSD_CONV_CH, SSD_HEADS, D_MODEL, D_MODEL)
IN_COLS = sum(IN_SPLITS)
MOE_GROUPS = 8
MOE_EXPERTS_PER_GROUP = 8
MOE_EXPERTS = MOE_GROUPS * MOE_EXPERTS_PER_GROUP
MOE_TOP_K = 2
MOE_HIDDEN = 512
MOE_BLOCK = 128
NORM_EPS = 1e-6
SUBLN_EPS = 1e-5
SSD_NORM_EPS = 1e-5


def rms_norm(x, w, eps):
    xf = x.astype(jnp.float32)
    y = xf * lax.rsqrt(jnp.mean(xf * xf, axis=-1, keepdims=True) + eps)
    return (y * w.astype(jnp.float32)).astype(x.dtype)

def rotary_tables(positions):
    inv_freq = 1.0 / (ROPE_THETA ** (jnp.arange(0, ATT_HEAD_DIM, 2, dtype=jnp.float32) / ATT_HEAD_DIM))
    ang = positions.astype(jnp.float32)[..., None] * inv_freq
    return jnp.cos(ang), jnp.sin(ang)

def apply_rotary(t, cos, sin):
    c = cos[:, :, None, None, :]
    sn = sin[:, :, None, None, :]
    tf = t.astype(jnp.float32)
    t1, t2 = jnp.split(tf, 2, axis=-1)
    return jnp.concatenate([t1 * c - t2 * sn, t2 * c + t1 * sn], axis=-1).astype(t.dtype)

def diff_attention(q, k, v, lam):
    s = q.shape[1]
    scale = ATT_HEAD_DIM ** -0.5
    outs = []
    for blk in range(s // Q_BLOCK):
        q_lo = blk * Q_BLOCK
        q_hi = q_lo + Q_BLOCK
        scores = jnp.einsum('bqhcd,bkhcd->bhcqk', q[:, q_lo:q_hi], k[:, :q_hi],
                            preferred_element_type=jnp.float32) * scale
        causal = (q_lo + jnp.arange(Q_BLOCK))[:, None] >= jnp.arange(q_hi)[None, :]
        probs = jax.nn.softmax(jnp.where(causal, scores, -jnp.inf), axis=-1)
        weights = probs[:, :, 0] - lam * probs[:, :, 1]
        outs.append(jnp.einsum('bhqk,bkhe->bqhe', weights.astype(v.dtype), v[:, :q_hi]))
    return jnp.concatenate(outs, axis=1)

def causal_depthwise_conv(u, w, bias):
    out = lax.conv_general_dilated(u, w[:, None, :], window_strides=(1,), padding=[(SSD_CONV - 1, 0)],
                                   dimension_numbers=('NWC', 'WIO', 'NWC'),
                                   feature_group_count=u.shape[-1])
    return out + bias

def ssd_chunked_scan(xdt, a, bm, cm):
    b, s, g, r, p = xdt.shape
    n = bm.shape[-1]
    nc = s // SSD_CHUNK

    def to_chunks(t):
        return jnp.moveaxis(t.reshape(b, nc, SSD_CHUNK, *t.shape[2:]), 1, 0)

    causal = jnp.tril(jnp.ones((SSD_CHUNK, SSD_CHUNK), dtype=bool))

    def step(state, inp):
        xc, ac, bc, cc = inp
        cum = jnp.cumsum(ac, axis=1)
        cum_t = jnp.moveaxis(cum, 1, -1)
        seg = cum_t[..., :, None] - cum_t[..., None, :]
        decay = jnp.exp(jnp.where(causal, seg, -jnp.inf))
        cb = jnp.einsum('bign,bjgn->bgij', cc, bc)
        y_diag = jnp.einsum('bgij,bgrij,bjgrp->bigrp', cb, decay, xc)
        y_off = jnp.einsum('bign,bgrpn->bigrp', cc, state) * jnp.exp(cum)[..., None]
        total = cum[:, -1]
        w_tail = jnp.exp(total[:, None] - cum)
        new_state = state * jnp.exp(total)[..., None, None] + jnp.einsum('bjgn,bjgr,bjgrp->bgrpn', bc, w_tail, xc)
        return new_state, y_diag + y_off

    init = jnp.zeros((b, g, r, p, n), jnp.float32)
    _, ys = lax.scan(step, init, (to_chunks(xdt), to_chunks(a), to_chunks(bm), to_chunks(cm)))
    return jnp.moveaxis(ys, 0, 1).reshape(b, s, g, r, p)

def ssd_branch(z, xbc, dt_raw, conv_w, conv_b, dt_bias, a_log, d_skip, norm_w):
    b, s, _ = z.shape
    xbc = jax.nn.silu(causal_depthwise_conv(xbc, conv_w, conv_b))
    xs, bm, cm = jnp.split(xbc, [SSD_INNER, SSD_INNER + SSD_GROUPS * SSD_STATE], axis=-1)
    xs = xs.reshape(b, s, SSD_GROUPS, SSD_HEADS_PER_GROUP, SSD_HEAD_DIM).astype(jnp.float32)
    bm = bm.reshape(b, s, SSD_GROUPS, SSD_STATE).astype(jnp.float32)
    cm = cm.reshape(b, s, SSD_GROUPS, SSD_STATE).astype(jnp.float32)
    dt = jax.nn.softplus(dt_raw.astype(jnp.float32) + dt_bias.astype(jnp.float32))
    dt = dt.reshape(b, s, SSD_GROUPS, SSD_HEADS_PER_GROUP)
    a = -jnp.exp(a_log.astype(jnp.float32)).reshape(SSD_GROUPS, SSD_HEADS_PER_GROUP)
    dsk = d_skip.astype(jnp.float32).reshape(SSD_GROUPS, SSD_HEADS_PER_GROUP)
    y = ssd_chunked_scan(xs * dt[..., None], dt * a, bm, cm) + dsk[..., None] * xs
    y = y.reshape(b, s, SSD_INNER) * jax.nn.silu(z.astype(jnp.float32))
    yg = y.reshape(b, s, SSD_GROUPS, SSD_INNER // SSD_GROUPS)
    yg = yg * lax.rsqrt(jnp.mean(yg * yg, axis=-1, keepdims=True) + SSD_NORM_EPS)
    return (yg.reshape(b, s, SSD_INNER) * norm_w.astype(jnp.float32)).astype(z.dtype)

def hierarchical_moe(h, w_gr, b_gr, w_er, b_er, w_gate, w_up, w_down):
    b, s, d = h.shape
    t = h.reshape(-1, d)
    n_tok = t.shape[0]
    g_logits = jnp.matmul(t, w_gr).astype(jnp.float32) + b_gr.astype(jnp.float32)
    g_prob = jax.nn.softmax(g_logits, axis=-1)
    g_sel = jnp.argmax(g_logits, axis=-1)
    g_gate = jnp.take_along_axis(g_prob, g_sel[:, None], axis=-1)[:, 0]
    e_logits = (jnp.matmul(t, w_er).astype(jnp.float32) + b_er.astype(jnp.float32))
    e_logits = e_logits.reshape(n_tok, MOE_GROUPS, MOE_EXPERTS_PER_GROUP)
    e_sel_logits = jnp.take_along_axis(e_logits, g_sel[:, None, None], axis=1)[:, 0]
    top_v, top_i = lax.top_k(e_sel_logits, MOE_TOP_K)
    weights = g_gate[:, None] * jax.nn.softmax(top_v, axis=-1)
    eid = g_sel[:, None].astype(jnp.int32) * MOE_EXPERTS_PER_GROUP + top_i.astype(jnp.int32)
    n_assign = n_tok * MOE_TOP_K
    flat_e = eid.reshape(-1)
    flat_tok = jnp.repeat(jnp.arange(n_tok, dtype=jnp.int32), MOE_TOP_K)
    flat_w = weights.reshape(-1)
    order = jnp.argsort(flat_e)
    se, st, sw = flat_e[order], flat_tok[order], flat_w[order]
    counts = jnp.bincount(flat_e, length=MOE_EXPERTS)
    starts = jnp.cumsum(counts) - counts
    padded = ((counts + MOE_BLOCK - 1) // MOE_BLOCK) * MOE_BLOCK
    pad_end = jnp.cumsum(padded)
    pad_start = pad_end - padded
    dest = pad_start[se] + (jnp.arange(n_assign, dtype=jnp.int32) - starts[se])
    n_buf = n_assign + MOE_EXPERTS * MOE_BLOCK
    n_blocks = n_buf // MOE_BLOCK
    buf_tok = jnp.zeros((n_buf,), jnp.int32).at[dest].set(st)
    buf_w = jnp.zeros((n_buf,), jnp.float32).at[dest].set(sw)
    blk_expert = jnp.minimum(jnp.searchsorted(pad_end, jnp.arange(n_blocks) * MOE_BLOCK, side='right'),
                             MOE_EXPERTS - 1)
    xb = t[buf_tok].reshape(n_blocks, MOE_BLOCK, d)

    def expert_block(args):
        xblk, e = args
        hid = jax.nn.silu(xblk @ w_gate[e]) * (xblk @ w_up[e])
        return hid @ w_down[e]

    yb = lax.map(expert_block, (xb, blk_expert)).reshape(n_buf, d)
    out = jnp.zeros((n_tok, d), jnp.float32).at[buf_tok].add(yb.astype(jnp.float32) * buf_w[:, None])
    return out.astype(h.dtype).reshape(b, s, d)

def first_inputs(seed: int = 0) -> dict:
    key = jax.random.key(seed)
    ks = jax.random.split(key, 28)
    f32 = jnp.float32

    def normal(k, shape, scale):
        return jax.random.normal(k, shape, f32) * scale

    x = normal(ks[0], (BATCH, SEQ, D_MODEL), 1.0)
    positions = (jnp.arange(SEQ, dtype=jnp.int32)[None, :]
                 + jax.random.randint(ks[1], (BATCH, 1), 0, SEQ, dtype=jnp.int32))
    norm_mix_w = 1.0 + normal(ks[2], (DEPTH, D_MODEL), 0.02)
    w_in = normal(ks[3], (DEPTH, D_MODEL, IN_COLS), D_MODEL ** -0.5)
    conv_w = normal(ks[4], (DEPTH, SSD_CONV, SSD_CONV_CH), SSD_CONV ** -0.5)
    conv_b = normal(ks[5], (DEPTH, SSD_CONV_CH), 0.02)
    dt0 = jnp.exp(jax.random.uniform(ks[6], (DEPTH, SSD_HEADS), f32, math.log(1e-3), math.log(1e-1)))
    dt_bias = dt0 + jnp.log(-jnp.expm1(-dt0))
    a_log = jnp.log(jax.random.uniform(ks[7], (DEPTH, SSD_HEADS), f32, 1.0, 16.0))
    d_skip = 1.0 + normal(ks[8], (DEPTH, SSD_HEADS), 0.1)
    ssd_norm_w = 1.0 + normal(ks[9], (DEPTH, SSD_INNER), 0.02)
    lambda_q1 = normal(ks[10], (DEPTH, ATT_HEAD_DIM), 0.1)
    lambda_k1 = normal(ks[11], (DEPTH, ATT_HEAD_DIM), 0.1)
    lambda_q2 = normal(ks[12], (DEPTH, ATT_HEAD_DIM), 0.1)
    lambda_k2 = normal(ks[13], (DEPTH, ATT_HEAD_DIM), 0.1)
    subln_w = 1.0 + normal(ks[14], (DEPTH, 2 * ATT_HEAD_DIM), 0.02)
    w_branch_attn = normal(ks[15], (DEPTH, ATT_V_WIDTH, D_MODEL), ATT_V_WIDTH ** -0.5)
    w_branch_ssd = normal(ks[16], (DEPTH, SSD_INNER, D_MODEL), SSD_INNER ** -0.5)
    w_out = normal(ks[17], (DEPTH, D_MODEL, D_MODEL), D_MODEL ** -0.5)
    norm_ffn_w = 1.0 + normal(ks[18], (DEPTH, D_MODEL), 0.02)
    w_group_router = normal(ks[19], (DEPTH, D_MODEL, MOE_GROUPS), D_MODEL ** -0.5)
    b_group_router = normal(ks[20], (DEPTH, MOE_GROUPS), 0.01)
    w_expert_router = normal(ks[21], (DEPTH, D_MODEL, MOE_EXPERTS), D_MODEL ** -0.5)
    b_expert_router = normal(ks[22], (DEPTH, MOE_EXPERTS), 0.01)
    w_expert_gate = normal(ks[23], (DEPTH, MOE_EXPERTS, D_MODEL, MOE_HIDDEN), D_MODEL ** -0.5)
    w_expert_up = normal(ks[24], (DEPTH, MOE_EXPERTS, D_MODEL, MOE_HIDDEN), D_MODEL ** -0.5)
    w_expert_down = normal(ks[25], (DEPTH, MOE_EXPERTS, MOE_HIDDEN, D_MODEL), MOE_HIDDEN ** -0.5)
    final_norm_w = 1.0 + normal(ks[26], (D_MODEL,), 0.02)
    return {'x': x, 'positions': positions, 'norm_mix_w': norm_mix_w, 'w_in': w_in,
            'conv_w': conv_w, 'conv_b': conv_b, 'dt_bias': dt_bias, 'a_log': a_log, 'd_skip': d_skip,
            'ssd_norm_w': ssd_norm_w, 'lambda_q1': lambda_q1, 'lambda_k1': lambda_k1,
            'lambda_q2': lambda_q2, 'lambda_k2': lambda_k2, 'subln_w': subln_w,
            'w_branch_attn': w_branch_attn, 'w_branch_ssd': w_branch_ssd, 'w_out': w_out,
            'norm_ffn_w': norm_ffn_w, 'w_group_router': w_group_router, 'b_group_router': b_group_router,
            'w_expert_router': w_expert_router, 'b_expert_router': b_expert_router,
            'w_expert_gate': w_expert_gate, 'w_expert_up': w_expert_up, 'w_expert_down': w_expert_down,
            'final_norm_w': final_norm_w}

def first_block(x, positions, norm_mix_w, w_in, conv_w, conv_b, dt_bias, a_log, d_skip, ssd_norm_w,
              lambda_q1, lambda_k1, lambda_q2, lambda_k2, subln_w, w_branch_attn, w_branch_ssd, w_out,
              norm_ffn_w, w_group_router, b_group_router, w_expert_router, b_expert_router,
              w_expert_gate, w_expert_up, w_expert_down, final_norm_w):
    b, s, _ = x.shape
    cos, sin = rotary_tables(positions)
    split_at = [int(o) for o in np.cumsum(IN_SPLITS)[:-1]]
    for l in range(DEPTH):
        lam_init = 0.8 - 0.6 * math.exp(-0.3 * l)
        h = rms_norm(x, norm_mix_w[l], NORM_EPS)
        proj = h @ w_in[l]
        q, k, v, z, xbc, dt_raw, gate_a, gate_s = jnp.split(proj, split_at, axis=-1)
        q = apply_rotary(q.reshape(b, s, ATT_HEADS, 2, ATT_HEAD_DIM), cos, sin)
        k = apply_rotary(k.reshape(b, s, ATT_HEADS, 2, ATT_HEAD_DIM), cos, sin)
        v = v.reshape(b, s, ATT_HEADS, 2 * ATT_HEAD_DIM)
        lam = (jnp.exp(jnp.sum(lambda_q1[l].astype(jnp.float32) * lambda_k1[l].astype(jnp.float32)))
               - jnp.exp(jnp.sum(lambda_q2[l].astype(jnp.float32) * lambda_k2[l].astype(jnp.float32)))
               + lam_init)
        att = diff_attention(q, k, v, lam)
        att = (rms_norm(att, subln_w[l], SUBLN_EPS) * (1.0 - lam_init)).reshape(b, s, ATT_V_WIDTH)
        ssd = ssd_branch(z, xbc, dt_raw, conv_w[l], conv_b[l], dt_bias[l], a_log[l], d_skip[l], ssd_norm_w[l])
        merged = (jax.nn.sigmoid(gate_a) * (att @ w_branch_attn[l])
                  + jax.nn.sigmoid(gate_s) * (ssd @ w_branch_ssd[l]))
        x = x + merged @ w_out[l]
        h2 = rms_norm(x, norm_ffn_w[l], NORM_EPS)
        x = x + hierarchical_moe(h2, w_group_router[l], b_group_router[l], w_expert_router[l],
                                 b_expert_router[l], w_expert_gate[l], w_expert_up[l], w_expert_down[l])
    return rms_norm(x, final_norm_w, NORM_EPS)


HEAD_DIM = 64
N_MIX_HEADS = D_MODEL // HEAD_DIM
HEADS_PER_MIXER = N_MIX_HEADS // 4
GROUP_WIDTH = HEADS_PER_MIXER * HEAD_DIM
MOBA_BLOCK = 256
MOBA_TOPK = 3
MLA_Q_RANK = D_MODEL // 4
MLA_KV_RANK = D_MODEL // 8
MLA_NOPE = HEAD_DIM
MLA_ROPE = HEAD_DIM // 2
MLA_V = HEAD_DIM
DILATED_BRANCHES = ((128, 1), (512, 4), (2048, 16))
SWA_WINDOW = 128
SWA_KV_HEADS = 2
SWA_KV_WIDTH = SWA_KV_HEADS * HEAD_DIM
D_FF = 4 * D_MODEL
EPS = 1e-6
NEG = -1e30
COL_WIDTHS = (GROUP_WIDTH, GROUP_WIDTH, GROUP_WIDTH,
              MLA_Q_RANK, MLA_KV_RANK, MLA_ROPE,
              GROUP_WIDTH, GROUP_WIDTH, GROUP_WIDTH,
              GROUP_WIDTH, SWA_KV_WIDTH, SWA_KV_WIDTH)
IN_COLS_2 = sum(COL_WIDTHS)


def rms_norm_2(x, g):
    xf = x.astype(jnp.float32)
    y = xf * lax.rsqrt(jnp.mean(xf * xf, axis=-1, keepdims=True) + EPS)
    return (y * g.astype(jnp.float32)).astype(x.dtype)

def split_columns(h):
    parts, off = [], 0
    for wdt in COL_WIDTHS:
        parts.append(h[..., off:off + wdt])
        off += wdt
    return parts

def alibi_slopes():
    n = 3 * HEADS_PER_MIXER
    idx = np.arange(1, n + 1, dtype=np.float32).reshape(HEADS_PER_MIXER, 3)
    s = jnp.asarray(np.exp2(-8.0 * idx / n), dtype=jnp.float32)
    return s[:, 0], s[:, 1], s[:, 2]

def rope_tables(S):
    inv = 1.0 / (ROPE_THETA ** (jnp.arange(0, MLA_ROPE, 2, dtype=jnp.float32) / MLA_ROPE))
    ang = jnp.arange(S, dtype=jnp.float32)[:, None] * inv[None, :]
    return jnp.cos(ang), jnp.sin(ang)

def apply_rope(x, cos, sin):
    x1, x2 = jnp.split(x.astype(jnp.float32), 2, axis=-1)
    c, s = cos[None, :, None, :], sin[None, :, None, :]
    return jnp.concatenate([x1 * c - x2 * s, x1 * s + x2 * c], axis=-1).astype(x.dtype)

def moba_attention(q, k, v, slopes):
    B, H, S, dh = q.shape
    nb = -(-S // MOBA_BLOCK)
    Sp = nb * MOBA_BLOCK
    topk = min(MOBA_TOPK, nb)
    pad = ((0, 0), (0, 0), (0, Sp - S), (0, 0))
    qp, kp, vp = jnp.pad(q, pad), jnp.pad(k, pad), jnp.pad(v, pad)
    kb = kp.reshape(B, H, nb, MOBA_BLOCK, dh)
    vb = vp.reshape(B, H, nb, MOBA_BLOCK, dh)
    kmean = jnp.mean(kb.astype(jnp.float32), axis=3)
    scale = dh ** -0.5
    bi = jnp.arange(B)[:, None, None, None]
    hi = jnp.arange(H)[None, :, None, None]
    slope_b = slopes.astype(jnp.float32)

    def chunk(c):
        t0 = c * Q_BLOCK
        qc = lax.dynamic_slice_in_dim(qp, t0, Q_BLOCK, axis=2)
        tpos = t0 + jnp.arange(Q_BLOCK)
        qblk = tpos // MOBA_BLOCK
        own = t0 // MOBA_BLOCK
        gate = jnp.einsum('bhqd,bhnd->bhqn', qc.astype(jnp.float32), kmean)
        past = jnp.arange(nb)[None, :] < qblk[:, None]
        gate = jnp.where(past, gate, NEG)
        _, sel = lax.top_k(gate, topk)
        sel_ok = sel < qblk[:, None]
        ksel = kb[bi, hi, sel]
        vsel = vb[bi, hi, sel]
        kpos_sel = sel[..., None] * MOBA_BLOCK + jnp.arange(MOBA_BLOCK)
        dist_sel = (tpos[:, None, None] - kpos_sel).astype(jnp.float32)
        s_sel = (jnp.einsum('bhqd,bhqjkd->bhqjk', qc, ksel).astype(jnp.float32) * scale
                 - slope_b[None, :, None, None, None] * dist_sel)
        s_sel = jnp.where(sel_ok[..., None], s_sel, NEG).reshape(B, H, Q_BLOCK, topk * MOBA_BLOCK)
        kown = lax.dynamic_slice_in_dim(kb, own, 1, axis=2)[:, :, 0]
        vown = lax.dynamic_slice_in_dim(vb, own, 1, axis=2)[:, :, 0]
        dist_own = tpos[:, None] - (own * MOBA_BLOCK + jnp.arange(MOBA_BLOCK))[None, :]
        s_own = (jnp.einsum('bhqd,bhkd->bhqk', qc, kown).astype(jnp.float32) * scale
                 - slope_b[None, :, None, None] * dist_own.astype(jnp.float32))
        s_own = jnp.where(dist_own >= 0, s_own, NEG)
        p = jax.nn.softmax(jnp.concatenate([s_sel, s_own], axis=-1), axis=-1)
        p_sel = p[..., :topk * MOBA_BLOCK].reshape(B, H, Q_BLOCK, topk, MOBA_BLOCK)
        p_own = p[..., topk * MOBA_BLOCK:]
        return (jnp.einsum('bhqjk,bhqjkd->bhqd', p_sel.astype(v.dtype), vsel)
                + jnp.einsum('bhqk,bhkd->bhqd', p_own.astype(v.dtype), vown))

    out = lax.map(chunk, jnp.arange(Sp // Q_BLOCK))
    return out.transpose(1, 2, 0, 3, 4).reshape(B, H, Sp, dh)[:, :, :S]

def causal_dense_attention(q, k, v, scale):
    B, H, S, _ = q.shape
    kpos = jnp.arange(S)

    def blk(c):
        qc = lax.dynamic_slice_in_dim(q, c * Q_BLOCK, Q_BLOCK, axis=2)
        s = jnp.einsum('bhqd,bhkd->bhqk', qc, k).astype(jnp.float32) * scale
        tpos = c * Q_BLOCK + jnp.arange(Q_BLOCK)
        s = jnp.where(kpos[None, :] <= tpos[:, None], s, NEG)
        p = jax.nn.softmax(s, axis=-1)
        return jnp.einsum('bhqk,bhkd->bhqd', p.astype(v.dtype), v)

    out = lax.map(blk, jnp.arange(S // Q_BLOCK))
    return out.transpose(1, 2, 0, 3, 4).reshape(B, H, S, -1)

def mla_attention(q_lat, kv_lat, k_rope, g_qlat, g_kvlat, w_uq, w_ukv, g_q, g_k):
    B, S, _ = q_lat.shape
    H = HEADS_PER_MIXER
    qk_dim = MLA_NOPE + MLA_ROPE
    q = (rms_norm_2(q_lat, g_qlat) @ w_uq).reshape(B, S, H, qk_dim)
    kv = (rms_norm_2(kv_lat, g_kvlat) @ w_ukv).reshape(B, S, H, MLA_NOPE + MLA_V)
    k_nope, v = kv[..., :MLA_NOPE], kv[..., MLA_NOPE:]
    k = jnp.concatenate([k_nope, jnp.broadcast_to(k_rope[:, :, None, :], (B, S, H, MLA_ROPE))], axis=-1)
    q, k = rms_norm_2(q, g_q), rms_norm_2(k, g_k)
    cos, sin = rope_tables(S)
    q = jnp.concatenate([q[..., :MLA_NOPE], apply_rope(q[..., MLA_NOPE:], cos, sin)], axis=-1)
    k = jnp.concatenate([k[..., :MLA_NOPE], apply_rope(k[..., MLA_NOPE:], cos, sin)], axis=-1)
    t = lambda a: a.transpose(0, 2, 1, 3)
    return causal_dense_attention(t(q), t(k), t(v), qk_dim ** -0.5)

def dilated_branch(q, k, v, slopes, window, dilation):
    B, H, S, dh = q.shape
    span = dilation * Q_BLOCK
    Sp = -(-S // span) * span
    L = Sp // dilation
    nb = L // Q_BLOCK
    steps = window // dilation

    def to_sub(t):
        t = jnp.pad(t, ((0, 0), (0, 0), (0, Sp - S), (0, 0)))
        return t.reshape(B, H, L, dilation, dh).transpose(0, 1, 3, 2, 4).reshape(B, H, dilation, nb, Q_BLOCK, dh)

    def with_prev(t):
        prev = jnp.pad(t, ((0, 0), (0, 0), (0, 0), (1, 0), (0, 0), (0, 0)))[:, :, :, :-1]
        return jnp.concatenate([prev, t], axis=4)

    qs = to_sub(q)
    kk, vv = with_prev(to_sub(k)), with_prev(to_sub(v))
    qi = jnp.arange(Q_BLOCK)[:, None]
    kidx = jnp.arange(2 * Q_BLOCK)[None, :]
    rel = qi + Q_BLOCK - kidx
    blk = jnp.arange(nb)[:, None, None]
    valid = (rel >= 0) & (rel <= steps) & (blk * Q_BLOCK + kidx[None] - Q_BLOCK >= 0)
    s = (jnp.einsum('bhrnqd,bhrnkd->bhrnqk', qs, kk).astype(jnp.float32) * (dh ** -0.5)
         - slopes.astype(jnp.float32)[None, :, None, None, None, None] * (dilation * rel).astype(jnp.float32))
    s = jnp.where(valid, s, NEG)
    m = jnp.max(s, axis=-1, keepdims=True)
    e = jnp.exp(s - m)
    l = jnp.sum(e, axis=-1, keepdims=True)
    o = jnp.einsum('bhrnqk,bhrnkd->bhrnqd', e, vv.astype(jnp.float32))
    back = lambda t: t.reshape(B, H, dilation, L, -1).transpose(0, 1, 3, 2, 4).reshape(B, H, Sp, -1)[:, :, :S]
    return back(o), back(m), back(l)

def dilated_mixture(q, k, v, slopes):
    branches = [dilated_branch(q, k, v, slopes, w, d) for (w, d) in DILATED_BRANCHES]
    M = functools.reduce(jnp.maximum, [b[1] for b in branches])
    num = jnp.zeros(q.shape, jnp.float32)
    den = jnp.zeros(q.shape[:-1] + (1,), jnp.float32)
    for o, m, l in branches:
        w = jnp.exp(m - M)
        num = num + w * o
        den = den + w * l
    return (num / den).astype(q.dtype)

def swa_sink_attention(q, k, v, sinks, slopes):
    B, H, S, dh = q.shape
    G = H // SWA_KV_HEADS
    nb = S // Q_BLOCK
    qb = q.reshape(B, SWA_KV_HEADS, G, nb, Q_BLOCK, dh)

    def with_prev(t):
        t = t.reshape(B, SWA_KV_HEADS, nb, Q_BLOCK, dh)
        prev = jnp.pad(t, ((0, 0), (0, 0), (1, 0), (0, 0), (0, 0)))[:, :, :-1]
        return jnp.concatenate([prev, t], axis=3)

    kk, vv = with_prev(k), with_prev(v)
    qi = jnp.arange(Q_BLOCK)[:, None]
    kidx = jnp.arange(2 * Q_BLOCK)[None, :]
    rel = qi + Q_BLOCK - kidx
    blk = jnp.arange(nb)[:, None, None]
    valid = (rel >= 0) & (rel < SWA_WINDOW) & (blk * Q_BLOCK + kidx[None] - Q_BLOCK >= 0)
    sl = slopes.astype(jnp.float32).reshape(SWA_KV_HEADS, G)[None, :, :, None, None, None]
    s = jnp.einsum('bkgnqd,bkncd->bkgnqc', qb, kk).astype(jnp.float32) * (dh ** -0.5) - sl * rel.astype(jnp.float32)
    s = jnp.where(valid, s, NEG)
    sink = jnp.broadcast_to(sinks.astype(jnp.float32).reshape(SWA_KV_HEADS, G)[None, :, :, None, None, None],
                            s.shape[:-1] + (1,))
    p = jax.nn.softmax(jnp.concatenate([s, sink], axis=-1), axis=-1)[..., :-1]
    o = jnp.einsum('bkgnqc,bkncd->bkgnqd', p.astype(v.dtype), vv)
    return o.reshape(B, H, S, dh)

def hybrid_layer(x, attn_norm_g, w_in, moba_q_g, moba_k_g, mla_qlat_g, mla_kvlat_g,
                 mla_w_uq, mla_w_ukv, mla_q_g, mla_k_g, dil_q_g, dil_k_g, swa_q_g, swa_k_g,
                 swa_sinks, group_out_g, w_o, mlp_norm_g, w_up, w_down):
    B, S, _ = x.shape
    H = HEADS_PER_MIXER
    slope_a, slope_c, slope_d = alibi_slopes()
    h = rms_norm_2(x, attn_norm_g) @ w_in
    a_q, a_k, a_v, b_ql, b_kvl, b_kr, c_q, c_k, c_v, d_q, d_k, d_v = split_columns(h)
    heads = lambda t, n: t.reshape(B, S, n, HEAD_DIM)
    tr = lambda t: t.transpose(0, 2, 1, 3)
    oa = moba_attention(tr(rms_norm_2(heads(a_q, H), moba_q_g)), tr(rms_norm_2(heads(a_k, H), moba_k_g)),
                        tr(heads(a_v, H)), slope_a)
    ob = mla_attention(b_ql, b_kvl, b_kr, mla_qlat_g, mla_kvlat_g, mla_w_uq, mla_w_ukv, mla_q_g, mla_k_g)
    oc = dilated_mixture(tr(rms_norm_2(heads(c_q, H), dil_q_g)), tr(rms_norm_2(heads(c_k, H), dil_k_g)),
                         tr(heads(c_v, H)), slope_c)
    od = swa_sink_attention(tr(rms_norm_2(heads(d_q, H), swa_q_g)),
                            tr(rms_norm_2(heads(d_k, SWA_KV_HEADS), swa_k_g)),
                            tr(heads(d_v, SWA_KV_HEADS)), swa_sinks, slope_d)
    groups = [tr(o).reshape(B, S, GROUP_WIDTH) for o in (oa, ob, oc, od)]
    mixed = jnp.concatenate([rms_norm_2(gr, group_out_g[i]) for i, gr in enumerate(groups)], axis=-1)
    x = x + mixed @ w_o
    u = jax.nn.relu(rms_norm_2(x, mlp_norm_g) @ w_up)
    return x + (u * u) @ w_down

def second_inputs(seed: int = 0) -> dict:
    key = jax.random.key(seed)
    ks = jax.random.split(key, 24)
    f = jnp.float32
    H = HEADS_PER_MIXER
    w = lambda k, shape, fan_in: jax.random.normal(k, shape, f) * (fan_in ** -0.5)
    g = lambda k, shape: 1.0 + 0.02 * jax.random.normal(k, shape, f)
    return {
        "x": jax.random.normal(ks[0], (BATCH, SEQ, D_MODEL), f),
        "attn_norm_g": g(ks[1], (DEPTH, D_MODEL)),
        "w_in": w(ks[2], (DEPTH, D_MODEL, IN_COLS_2), D_MODEL),
        "moba_q_g": g(ks[3], (DEPTH, HEAD_DIM)),
        "moba_k_g": g(ks[4], (DEPTH, HEAD_DIM)),
        "mla_qlat_g": g(ks[5], (DEPTH, MLA_Q_RANK)),
        "mla_kvlat_g": g(ks[6], (DEPTH, MLA_KV_RANK)),
        "mla_w_uq": w(ks[7], (DEPTH, MLA_Q_RANK, H * (MLA_NOPE + MLA_ROPE)), MLA_Q_RANK),
        "mla_w_ukv": w(ks[8], (DEPTH, MLA_KV_RANK, H * (MLA_NOPE + MLA_V)), MLA_KV_RANK),
        "mla_q_g": g(ks[9], (DEPTH, MLA_NOPE + MLA_ROPE)),
        "mla_k_g": g(ks[10], (DEPTH, MLA_NOPE + MLA_ROPE)),
        "dil_q_g": g(ks[11], (DEPTH, HEAD_DIM)),
        "dil_k_g": g(ks[12], (DEPTH, HEAD_DIM)),
        "swa_q_g": g(ks[13], (DEPTH, HEAD_DIM)),
        "swa_k_g": g(ks[14], (DEPTH, HEAD_DIM)),
        "swa_sinks": 0.5 * jax.random.normal(ks[15], (DEPTH, H), f),
        "group_out_g": g(ks[16], (DEPTH, 4, GROUP_WIDTH)),
        "w_o": w(ks[17], (DEPTH, D_MODEL, D_MODEL), D_MODEL),
        "mlp_norm_g": g(ks[18], (DEPTH, D_MODEL)),
        "w_up": w(ks[19], (DEPTH, D_MODEL, D_FF), D_MODEL),
        "w_down": w(ks[20], (DEPTH, D_FF, D_MODEL), D_FF),
    }

def second_block(x, attn_norm_g, w_in, moba_q_g, moba_k_g, mla_qlat_g, mla_kvlat_g, mla_w_uq,
              mla_w_ukv, mla_q_g, mla_k_g, dil_q_g, dil_k_g, swa_q_g, swa_k_g, swa_sinks,
              group_out_g, w_o, mlp_norm_g, w_up, w_down):
    for l in range(DEPTH):
        x = hybrid_layer(x, attn_norm_g[l], w_in[l], moba_q_g[l], moba_k_g[l], mla_qlat_g[l],
                         mla_kvlat_g[l], mla_w_uq[l], mla_w_ukv[l], mla_q_g[l], mla_k_g[l],
                         dil_q_g[l], dil_k_g[l], swa_q_g[l], swa_k_g[l], swa_sinks[l],
                         group_out_g[l], w_o[l], mlp_norm_g[l], w_up[l], w_down[l])
    return x


def setup_inputs(seed=0):
    out = dict(first_inputs(seed))
    for name, value in second_inputs(seed + 1).items():
        if name != "x":
            out[name + "_2"] = value
    return out


def reference(
    x, positions, norm_mix_w, w_in, conv_w, conv_b, dt_bias, a_log, d_skip, ssd_norm_w,
    lambda_q1, lambda_k1, lambda_q2, lambda_k2, subln_w, w_branch_attn, w_branch_ssd, w_out,
    norm_ffn_w, w_group_router, b_group_router, w_expert_router, b_expert_router, w_expert_gate,
    w_expert_up, w_expert_down, final_norm_w, attn_norm_g_2, w_in_2, moba_q_g_2, moba_k_g_2,
    mla_qlat_g_2, mla_kvlat_g_2, mla_w_uq_2, mla_w_ukv_2, mla_q_g_2, mla_k_g_2, dil_q_g_2,
    dil_k_g_2, swa_q_g_2, swa_k_g_2, swa_sinks_2, group_out_g_2, w_o_2, mlp_norm_g_2, w_up_2,
    w_down_2,
):
    x = first_block(
        x, positions, norm_mix_w, w_in, conv_w, conv_b, dt_bias, a_log, d_skip, ssd_norm_w,
        lambda_q1, lambda_k1, lambda_q2, lambda_k2, subln_w, w_branch_attn, w_branch_ssd, w_out,
        norm_ffn_w, w_group_router, b_group_router, w_expert_router, b_expert_router,
        w_expert_gate, w_expert_up, w_expert_down, final_norm_w,
    )
    return second_block(
        x, attn_norm_g_2, w_in_2, moba_q_g_2, moba_k_g_2, mla_qlat_g_2, mla_kvlat_g_2,
        mla_w_uq_2, mla_w_ukv_2, mla_q_g_2, mla_k_g_2, dil_q_g_2, dil_k_g_2, swa_q_g_2,
        swa_k_g_2, swa_sinks_2, group_out_g_2, w_o_2, mlp_norm_g_2, w_up_2, w_down_2,
    )


_drawn_inputs = setup_inputs


def setup_inputs(seed=0):
    import zlib

    import numpy as np

    out = dict(_drawn_inputs(seed))
    spreads = {}
    factors = {'ssd_norm_w': 3.169,
     'lambda_q1': 6.254,
     'subln_w': 3.484,
     'b_group_router': 4.834,
     'b_expert_router': 6.423,
     'attn_norm_g_2': 2.747,
     'moba_q_g_2': 8.0,
     'moba_k_g_2': 8.0,
     'mla_qlat_g_2': 8.0,
     'mla_kvlat_g_2': 5.728,
     'mla_q_g_2': 8.0,
     'mla_k_g_2': 8.0,
     'dil_q_g_2': 8.0,
     'dil_k_g_2': 8.0,
     'swa_q_g_2': 8.0,
     'swa_k_g_2': 8.0,
     'group_out_g_2': 3.645,
     'mlp_norm_g_2': 3.672}
    for name, (base, spread) in spreads.items():
        noise = np.random.default_rng([zlib.crc32(name.encode()), seed]).standard_normal(out[name].shape)
        drawn = base * np.exp(spread * noise) if base else spread * noise
        out[name] = jnp.asarray(drawn.astype(out[name].dtype))
    for name, factor in factors.items():
        out[name] = (out[name] * factor).astype(out[name].dtype)
    return out
```

```python
from contextlib import ExitStack

import numpy as np
import concourse.bass as bass
from concourse import mybir

F32 = mybir.dt.float32
I32 = mybir.dt.int32
U32 = mybir.dt.uint32
ALU = mybir.AluOpType
ACT = mybir.ActivationFunctionType
AX = mybir.AxisListType
MUL, ADD, SUB, MAX, MIN = ALU.mult, ALU.add, ALU.subtract, ALU.max, ALU.min
EQ, GE, GT, LE = ALU.is_equal, ALU.is_ge, ALU.is_gt, ALU.is_le

S = 512
D = 1024
NT = 4
RING = 3
CAP = 128
NOV = 7
BIG = 1e30
TWO_PI = 6.283185307179586
MAGIC = 12582912.0

VECS = [
    ("norm_mix_w", 8), ("conv_b", 32), ("ssd_norm_w", 16), ("subln_w", 1), ("attn_norm_g_2", 8),
    ("group_out_g_2", 8), ("mlp_norm_g_2", 8), ("mla_qlat_g_2", 2), ("mla_kvlat_g_2", 1),
    ("moba_q_g_2", -1), ("moba_k_g_2", -1), ("dil_q_g_2", -1), ("dil_k_g_2", -1),
    ("swa_q_g_2", -1), ("swa_k_g_2", -1),
]


def vec_rows():
    at, n = {}, 0
    for name, rows in VECS:
        at[name] = n
        n += abs(rows)
    return at, n


CONSTS = [
    ("ident", 128), ("tri", 128), ("gt", 128), ("lt", 128), ("ones", 128), ("perm", 128),
    ("causal", 512), ("iota64", 64), ("iota128", 128), ("iota8m", 8), ("aid1", 8), ("ovid", 8),
    ("rcos", 64), ("rsin", 64), ("invf", 1), ("mhalf", 8),
]


def const_cols():
    at, n = {}, 0
    for name, cols in CONSTS:
        at[name] = (n, n + cols)
        n += cols
    return at, n


def constants():
    at, n = const_cols()
    c = np.zeros((128, n), np.float32)
    p = np.arange(128)

    def put(name, v):
        a, b = at[name]
        c[:, a:b] = np.broadcast_to(v, (128, b - a))

    put("ident", np.eye(128))
    put("tri", p[:, None] <= p[None, :])
    put("gt", p[:, None] > p[None, :])
    put("lt", p[:, None] < p[None, :])
    put("ones", 1.0)
    perm = np.zeros((128, 128))
    for m in range(128):
        if m % 64 < 32:
            perm[m + 32, m] = -1.0
        else:
            perm[m - 32, m] = 1.0
    put("perm", perm)
    dist = p[:, None] + 384 - np.arange(512)[None, :]
    put("causal", np.where(dist >= 0, 0.0, -BIG))
    put("iota64", np.arange(64))
    put("iota128", p)
    put("iota8m", np.arange(8) - 1000.0)
    aid = np.zeros((128, 8))
    for tt in range(4):
        for k in range(2):
            aid[:, tt * 2 + k] = k * 512 + tt * 128 + p + 1
    put("aid1", aid)
    put("ovid", np.arange(8))
    inv2 = (1.0 / (np.float32(10000.0) ** (np.arange(0, 32, 2, dtype=np.float32) / np.float32(32)))).astype(np.float32)
    ang = np.arange(512, dtype=np.float32)[:, None] * inv2[None, :]
    put("rcos", np.cos(ang).astype(np.float32).reshape(4, 128, 16).transpose(1, 0, 2).reshape(128, 64))
    put("rsin", np.sin(ang).astype(np.float32).reshape(4, 128, 16).transpose(1, 0, 2).reshape(128, 64))
    inv1 = (1.0 / (np.float32(10000.0) ** (np.arange(0, 64, 2, dtype=np.float32) / np.float32(64)))).astype(np.float32)
    put("invf", inv1[p % 32][:, None])
    put("mhalf", -0.5)
    bias = np.zeros((12, 128, 512), np.float32)
    slopes = np.exp2(-8.0 * np.arange(1, 13, dtype=np.float32).reshape(4, 3) / 12).astype(np.float32)
    mult = (dist <= 128) * 1 + (dist % 4 == 0) * 1 + (dist % 16 == 0) * 1
    lnm = np.where((dist >= 0) & (mult > 0), np.log(np.maximum(mult, 1)), -BIG)
    swa = np.where((dist >= 0) & (dist < 128), 0.0, -BIG)
    cau = np.where(dist >= 0, 0.0, -BIG)
    for h in range(4):
        for m, extra in enumerate((cau, lnm, swa)):
            bias[m * 4 + h] = (-slopes[h, m] * dist.astype(np.float32)).astype(np.float64) + extra
    return c, bias


class Engine:

    def __init__(self, eng, sem, serial=True):
        self.eng, self.sem, self.n, self.seen, self.serial = eng, sem, 0, {}, serial

    def w(self, *toks):
        for t in toks:
            if t is None:
                continue
            if isinstance(t, list):
                self.w(*t)
                continue
            sem, v = t
            if self.seen.get(sem.num, 0) < v:
                self.eng.wait_ge(sem, v)
                self.seen[sem.num] = v

    def __call__(self, ins):
        ins.then_inc(self.sem, 1)
        self.n += 1
        if self.serial:
            self.w((self.sem, self.n))
        return (self.sem, self.n)

    def last(self):
        return (self.sem, self.n)


class Lane:

    def __init__(self, sem):
        self.sem, self.n = sem, 0

    def __call__(self, ins):
        ins.then_inc(self.sem, 16)
        self.n += 16
        return (self.sem, self.n)


class Pool:

    def __init__(self, aps):
        self.free = [(a, None) for a in aps]

    def take(self):
        return self.free.pop(0)

    def give(self, ap, *toks):
        self.free.append((ap, list(toks)))


class Arena:

    def __init__(self, start, end):
        self.at, self.end = (start + 63) // 64 * 64, end

    def take(self, shape):
        at = self.at
        self.at = at + (int(np.prod(shape[1:])) * 4 + 63) // 64 * 64
        assert self.at <= self.end, (shape, self.at, self.end)
        return at


def run_both(a, b):
    live = [g for g in (a, b) if g is not None]
    while live:
        for g in list(live):
            try:
                next(g)
            except StopIteration:
                live.remove(g)


def build(nc, t, out):
    sems = []

    def sem(name):
        s = nc.alloc_semaphore(name)
        sems.append(s)
        return s

    V = Engine(nc.vector, sem("s_dve"))
    A = Engine(nc.scalar, sem("s_act"))
    T = Engine(nc.tensor, sem("s_pe"), serial=False)
    G = Engine(nc.gpsimd, sem("s_pool"))
    SP = Engine(nc.sync, sem("s_sp"))
    v, a, g, pe = nc.vector, nc.scalar, nc.gpsimd, nc.tensor

    persist = ExitStack()
    low, high = nc.sbuf_base, nc.sbuf_usable_end
    PM = Arena(low, high)

    def sb(name, shape, dt=F32, stack=None):
        return nc.alloc_sbuf_tensor_at(name, shape, dt, offset=(stack or PM).take(shape))

    banks = [persist.enter_context(nc.psum_tensor(f"ps{i}", [128, 512], F32)) for i in range(8)]
    PS = Pool(banks)

    def bank():
        b, tok = PS.take()
        T.w(tok)
        return b

    def fence():
        now = [e.last() for e in (V, A, T, G)]
        for e in (V, A, T, G):
            e.w(now)

    cat, ncc = const_cols()
    C = sb("consts", [128, ncc])
    lane0 = Lane(sem("s_in"))
    t_in = lane0(nc.gpsimd.dma_start(C[:, :], t["consts"]))

    def cc(name):
        x, y = cat[name]
        return C[:, x:y]

    ident = cc("ident")

    region_a = PM.at
    ssdT = sb("ssdT", [128, 16, S])
    both = ssdT[:, :, :].rearrange("p a b -> p (a b)")
    X = both[:, 0:4096].rearrange("p (a b) -> p a b", a=NT)
    XN = both[:, 4096:8192].rearrange("p (a b) -> p a b", a=NT)
    t_in = lane0(nc.gpsimd.dma_start(X, t["x"].rearrange("a (n p) d -> p (a n) d", p=128)))
    rows_at, nrow = vec_rows()
    hT = sb("hT", [128, 8, S])
    attT = sb("attT", [128, 8, S])
    ring = [sb(f"ring{i}", [128, 4096]) for i in range(RING)]
    vcol = sb("vcol", [128, nrow + 128])
    sc = sb("sc", [128, 512])
    st = sb("st", [128, 256])
    ovn = sb("ovn", [128, 8], I32)
    work0 = PM.at
    WK = Arena(work0, high)
    cosT = sb("cosT", [128, S], stack=WK)
    sinT = sb("sinT", [128, S], stack=WK)
    small = Arena(WK.at, high)
    vrow = sb("vrow", [nrow, 128], stack=small)
    crow = sb("crow", [128, 128], stack=small)
    for name, n in VECS:
        r = rows_at[name]
        if n < 0:
            for half in range(2):
                t_in = lane0(nc.gpsimd.dma_start(vrow[r:r + 1, half * 64:half * 64 + 64], t[name]))
        else:
            src = t[name]
            if name == "group_out_g_2":
                src = src.rearrange("a b (r c) -> (a b r) c", c=128)
            else:
                src = src.rearrange("a (r c) -> (a r) c", c=128)
            t_in = lane0(nc.gpsimd.dma_start(vrow[r:r + n, :], src))
    t_in = lane0(nc.gpsimd.dma_start(crow[:, :], t["conv_w"].rearrange("a k (r c) -> (a k r) c", c=128)))

    def col(name, i=0):
        return vcol[:, rows_at[name] + i:rows_at[name] + i + 1]

    def conv_col(k, i):
        return vcol[:, nrow + k * 32 + i:nrow + k * 32 + i + 1]

    sc_at = {}
    for name, n in (("dt_bias", 32), ("a_log", 32), ("d_skip", 32), ("lambda_q1", 64), ("lambda_k1", 64),
                    ("lambda_q2", 64), ("lambda_k2", 64), ("b_group_router", 8), ("b_expert_router", 64),
                    ("swa_sinks_2", 4)):
        o = sum(x[1] for x in sc_at.values())
        sc_at[name] = (o, n)
        t_in = lane0(nc.gpsimd.dma_start(sc[:, o:o + n], t[name].to_broadcast([128, n])))

    def scv(name):
        o, n = sc_at[name]
        return sc[:, o:o + n]

    posi = sb("posi", [128, S], I32, stack=small)
    t_in = lane0(nc.gpsimd.dma_start(posi[:, :], t["positions"].to_broadcast([128, S])))

    rlane = [Lane(sem(f"s_ring{i}")) for i in range(RING)]
    chunks = []

    def wview(name, c0, n):
        return t[name].rearrange("a (k p) n -> p (a k) n", p=128)[:, :, c0:c0 + n]

    for h in range(8):
        chunks.append([(0, 128, wview("w_in", h * 128, 128)), (128, 128, wview("w_in", 1024 + h * 128, 128)),
                       (256, 128, wview("w_in", 2048 + h * 128, 128)), (384, 0, None)])
    for gr in range(8):
        chunks.append([(0, 256, wview("w_in", 5120 + gr * 256, 256)),
                       (256, 128, wview("w_in", 7168 + gr * 128, 128)),
                       (384, 128, wview("w_in", 8192 + gr * 128, 128))])
        chunks.append([(0, 256, wview("w_in", 3072 + gr * 256, 256))])
    for half in range(2):
        o = half * 512
        chunks.append([(0, 512, wview("w_in", 9248 + o, 512))])
        chunks.append([(0, 512, wview("w_branch_attn", o, 512))])
        chunks.append([(0, 512, wview("w_in", 10272 + o, 512))])
        for kk in range(2):
            chunks.append([(0, 512, t["w_branch_ssd"].rearrange("a (k p) n -> p (a k) n", p=128)[:, kk * 8:kk * 8 + 8, o:o + 512])])
    for half in range(2):
        chunks.append([(0, 512, wview("w_out", half * 512, 512))])
    n_mix = len(chunks)

    def eview(name, e):
        return t[name][0, e].rearrange("(k p) n -> p k n", p=128)

    def moe_chunks(e):
        return ([(0, 512, eview("w_expert_gate", e))], [(0, 512, eview("w_expert_up", e))],
                [(0, 1024, eview("w_expert_down", e))])

    for e in range(65):
        if e < 64:
            chunks += moe_chunks(e)[0:2]
        if e > 0:
            chunks.append(moe_chunks(e - 1)[2])
    n_moe_end = len(chunks)
    for c0 in range(0, 2464, 512):
        n = min(512, 2464 - c0)
        chunks.append([(0, n, wview("w_in_2", c0, n))])
    for half in range(2):
        chunks.append([(0, 512, wview("w_o_2", half * 512, 512))])
    for c0 in range(8):
        chunks.append([(0, 512, wview("w_up_2", c0 * 512, 512))])
    for kk in range(8):
        chunks.append([(0, 1024, t["w_down_2"].rearrange("a (k p) n -> p (a k) n", p=128)[:, kk * 4:kk * 4 + 4, :])])

    state = {"issued": 0, "taken": 0}
    slot_tok = {}
    slot_of = {}
    slots = [(i, None) for i in range(RING)]

    def issue():
        i = state["issued"]
        if i >= len(chunks) or not slots:
            return
        r, free = slots.pop(0)
        slot_of[i] = r
        SP.w(free)
        width = sum(x[1] for x in chunks[i])
        width = 512 if len(chunks[i]) == 4 else width
        for c0, n, src in chunks[i]:
            if n:
                k = src.shape[1]
                dst = ring[r][:, 0:k * width].rearrange("p (k n) -> p k n", k=k)[:, :, c0:c0 + n]
                slot_tok[i] = rlane[r](nc.sync.dma_start(dst, src))
        state["issued"] = i + 1

    def take(k, n):
        i = state["taken"]
        state["taken"] = i + 1
        return ring[slot_of[i]][:, 0:k * n].rearrange("p (k n) -> p k n", k=k), slot_tok[i], i

    def release(i, *toks):
        if slot_of[i] < RING or state["issued"] < n_moe_end:
            slots.append((slot_of[i], list(toks)))
        issue()

    for _ in range(RING):
        issue()

    T.w(t_in)
    b = bank()
    pe.transpose(b[:, 0:nrow], vrow[:, :], ident[0:nrow, 0:nrow])
    tk = T(pe.transpose(b[:, nrow:nrow + 128], crow[:, :], ident))
    V.w(tk, t_in)
    t_col = V(v.tensor_copy(vcol[:, :], b[:, 0:nrow + 128]))
    PS.give(b, t_col)
    t_col = V(v.tensor_scalar(col("subln_w"), col("subln_w"), 0.8, None, MUL))
    for name in ("moba_q_g_2", "dil_q_g_2", "swa_q_g_2"):
        t_col = V(v.tensor_scalar(col(name), col(name), 0.125, None, MUL))
    A.w(t_in, t_col)
    G.w(t_in)

    mhalf = cc("mhalf")

    lamj = sb("lamj", [128, 64], stack=small)
    V(v.tensor_tensor_reduce(lamj[:, :], scv("lambda_q1"), scv("lambda_k1"), 1.0, 0.0, MUL, ADD, st[:, 0:1]))
    tk = V(v.tensor_tensor_reduce(lamj[:, :], scv("lambda_q2"), scv("lambda_k2"), 1.0, 0.0, MUL, ADD, st[:, 1:2]))
    A.w(tk)
    tk = A(a.activation(st[:, 2:4], st[:, 0:2], ACT.Exp))
    V.w(tk)
    V(v.tensor_tensor(st[:, 4:5], st[:, 3:4], st[:, 2:3], SUB))
    t_lam = V(v.tensor_scalar(st[:, 4:5], st[:, 4:5], 0.8 - 0.6, None, SUB))
    nlam = st[:, 4:5]

    ang = sb("ang", [128, S], stack=small)
    rn = sb("rn", [128, S], stack=small)
    V(v.tensor_copy(ang[:, :], posi[:, :]))
    V(v.tensor_scalar(ang[:, :], ang[:, :], cc("invf"), None, MUL))
    C1 = 6.28125
    C2 = float(np.float32(TWO_PI - C1))
    for dst, sh, off in ((sinT, 0.0, 0.0), (cosT, 0.25, TWO_PI / 4)):
        V(v.tensor_scalar(rn[:, :], ang[:, :], 1.0 / TWO_PI, sh, MUL, ADD))
        V(v.tensor_scalar(rn[:, :], rn[:, :], MAGIC, None, ADD))
        V(v.tensor_scalar(rn[:, :], rn[:, :], MAGIC, None, SUB))
        V(v.scalar_tensor_tensor(dst[:, :], rn[:, :], -C1, ang[:, :], MUL, ADD))
        V(v.scalar_tensor_tensor(dst[:, :], rn[:, :], -C2, dst[:, :], MUL, ADD))
        V(v.tensor_scalar(dst[:, :], dst[:, :], off, 3.1415925, ADD, MIN))
        tk = V(v.tensor_scalar(dst[:, :], dst[:, :], -3.1415925, None, MAX))
        A.w(tk)
        t_rot = A(a.activation(dst[:, :], dst[:, :], ACT.Sin))
    state_w = {"flip": 0}

    def evac(dst, src, scale=None, after=None):
        state_w["flip"] ^= 1
        if state_w["flip"]:
            V.w(after)
            if scale is None:
                return V(v.tensor_copy(dst, src))
            return V(v.tensor_scalar(dst, src, scale, None, MUL))
        A.w(after)
        if scale is None:
            return A(a.copy(dst, src))
        return A(a.activation(dst, src, ACT.Copy, scale=scale))

    def rstd(dst, ss, eps, tok):
        V.w(tok)
        tk = V(v.tensor_scalar(ss, ss, eps, None, ADD))
        G.w(tk)
        return G(g.tensor_tensor(dst, ss, mhalf[:, 0:ss.shape[1]], ALU.pow))

    def norm_to(dst, src, deps, eps=1e-6, free=None):
        toks = []
        A.w(free)
        for tt in range(NT):
            A.w(deps[tt])
            toks.append(A(a.activation(dst[:, tt, :], src[:, tt, :], ACT.Square, scale=1.0 / 32,
                                       accum_out=st[:, 8 + tt:9 + tt])))
        tk = rstd(st[:, 12:16], st[:, 8:12], eps, toks[-1])
        V.w(tk)
        return [V(v.tensor_scalar(dst[:, tt, :], src[:, tt, :], st[:, 12 + tt:13 + tt], None, MUL))
                for tt in range(NT)]

    def to_features(dst, src, toks, scol, free=None):
        outs = []
        for k in range(8):
            b = bank()
            for tt in range(NT):
                T.w(toks[tt])
                m = pe.transpose(b[:, tt * 128:tt * 128 + 128], src[:, tt, k * 128:k * 128 + 128], ident)
            tk = T(m)
            if free is not None:
                V.w(free)
                A.w(free)
            tk = evac(dst[:, k, :], b[:, :], None if scol is None else scol(k), after=tk)
            PS.give(b, tk)
            outs.append(tk)
        return outs

    def mm_group(o, lhs, rhs, n, start=True, stop=True):
        for k in range(n):
            m = pe.matmul(o, lhs(k), rhs(k), start=start and k == 0, stop=stop and k == n - 1)
        return m

    tn = norm_to(XN, X, [t_in] * NT)
    t_h = to_features(hT, XN, tn, lambda k: col("norm_mix_w", k))
    T.w(t_h, t_rot, t_lam)
    fence()
    V.w(t_rot)


    def bufs(name, n, shape, stack):
        return Pool([sb(f"{name}{i}", shape, stack=stack) for i in range(n)])

    B_raw = bufs("raw", 2, [128, S], WK)
    B_q = bufs("bq", 2, [128, S], WK)
    B_k = bufs("bk", 2, [128, S], WK)
    B_v = bufs("bv", 2, [128, NT, 128], WK)
    B_s = bufs("bs", 4, [128, 2, S], WK)
    B_w = bufs("bw", 3, [128, S], WK)
    B_wt = bufs("bwt", 3, [128, S], WK)
    B_st = bufs("bst", 4, [128, 16], WK)
    B_at = bufs("bat", 2, [128, NT, 128], WK)
    heads = {}

    def dense_head(h):
        w, wt, wi = take(8, 512)
        T.w(wt)
        outs = []
        raws = []
        for j in range(2):
            b = bank()
            tk = T(mm_group(b[:, :], lambda k: w[:, k, j * 128:j * 128 + 128], lambda k: hT[:, k, :], 8))
            raw, rt = B_raw.take()
            A.w(rt, tk)
            tk = A(a.copy(raw[:, :], b[:, :]))
            PS.give(b, tk)
            raws.append((raw, tk))
            yield
        for j, B in ((0, B_q), (1, B_k)):
            raw, tk = raws[j]
            b = bank()
            T.w(tk)
            tp = T(pe.matmul(b[:, :], cc("perm"), raw[:, :], start=True, stop=True))
            dst, dtk = B.take()
            V.w(dtk, tk)
            V(v.tensor_tensor(dst[:, :], raw[:, :], cosT[:, :], MUL))
            V.w(tp)
            t2 = V(v.tensor_tensor(raw[:, :], b[:, :], sinT[:, :], MUL))
            PS.give(b, t2)
            t3 = V(v.tensor_tensor(dst[:, :], dst[:, :], raw[:, :], ADD))
            B_raw.give(raw, t3)
            outs.append((dst, t3))
            yield
        b = bank()
        for tt in range(NT):
            tk = T(mm_group(b[:, tt * 128:tt * 128 + 128], lambda k: hT[:, k, tt * 128:tt * 128 + 128],
                            lambda k: w[:, k, 256:384], 8))
            if tt < 3:
                yield
        release(wi, tk)
        vv, vt = B_v.take()
        A.w(vt, tk)
        tk = A(a.copy(vv[:, :, :].rearrange("p a b -> p (a b)"), b[:, :]))
        PS.give(b, tk)
        outs.append((vv, tk))
        heads[h] = outs
        yield

    def attend(h):
        (q, tq), (k_, tk_), (vv, tv) = heads[h]
        at, att_ = B_at.take()
        items = [dict() for _ in range(4)]
        lastT = []

        def s1(i):
            it = items[i]
            kn = (i + 1) * 128
            s, stk = B_s.take()
            sm, smk = B_st.take()
            T.w(tq, tk_)
            for c in range(2):
                b = bank()
                r = slice(c * 64, c * 64 + 64)
                tk = T(pe.matmul(b[:, 0:kn], q[r, i * 128:i * 128 + 128], k_[r, 0:kn], start=True, stop=True))
                V.w(stk, smk, tk)
                tk = V(v.tensor_tensor_reduce(s[:, c, 0:kn], b[:, 0:kn], cc("causal")[:, 384 - 128 * i:512],
                                              1.0, -3e38, ADD, MAX, sm[:, c:c + 1]))
                PS.give(b, tk)
            tk = V(v.tensor_scalar(sm[:, 2:4], sm[:, 0:2], -0.125, None, MUL))
            A.w(tk)
            for c in range(2):
                tk = A(a.activation(s[:, c, 0:kn], s[:, c, 0:kn], ACT.Exp, scale=0.125, bias=sm[:, 2 + c:3 + c],
                                    accum_out=sm[:, 4 + c:5 + c]))
            it["s"], it["sm"] = s, sm
            W, Wt = B_w.take()
            V.w(tk, Wt)
            V(v.reciprocal(sm[:, 6:8], sm[:, 4:6]))
            V(v.tensor_scalar(sm[:, 8:9], sm[:, 7:8], nlam, None, MUL))
            V(v.tensor_scalar(W[:, 0:kn], s[:, 0, 0:kn], sm[:, 6:7], None, MUL))
            tk = V(v.scalar_tensor_tensor(W[:, 0:kn], s[:, 1, 0:kn], sm[:, 8:9], W[:, 0:kn], MUL, ADD))
            B_s.give(s, tk)
            it["W"], it["tW"] = W, tk

        def s2(i):
            it = items[i]
            b = bank()
            T.w(it["tW"])
            for j in range(i + 1):
                m = pe.transpose(b[:, j * 128:j * 128 + 128], it["W"][:, j * 128:j * 128 + 128], ident)
            tk = T(m)
            B_w.give(it["W"], tk)
            wt, wtt = B_wt.take()
            A.w(wtt, tk)
            tk = A(a.copy(wt[:, 0:(i + 1) * 128], b[:, 0:(i + 1) * 128]))
            PS.give(b, tk)
            it["wt"], it["twt"] = wt, tk

        def s3(i):
            it = items[i]
            sm = it["sm"]
            b = bank()
            T.w(it["twt"], tv)
            tk = T(mm_group(b[:, 0:128], lambda j: it["wt"][:, j * 128:j * 128 + 128], lambda j: vv[:, j, :], i + 1))
            B_wt.give(it["wt"], tk)
            lastT.append(tk)
            A.w(tk)
            if i == 0:
                A.w(att_)
                V.w(att_)
            tk = A(a.activation(at[:, i, :], b[:, 0:128], ACT.Square, scale=128.0 ** -0.5, accum_out=sm[:, 10:11]))
            tk = rstd(sm[:, 11:12], sm[:, 10:11], 1e-5, tk)
            V.w(tk)
            tk = V(v.tensor_scalar(at[:, i, :], b[:, 0:128], sm[:, 11:12], None, MUL))
            PS.give(b, tk)
            B_st.give(sm, tk)
            it["ta"] = tk

        plan = [[(s1, 0)], [(s1, 1)], [(s1, 2), (s2, 0)], [(s1, 3), (s2, 1), (s3, 0)], [(s2, 2), (s3, 1)],
                [(s2, 3), (s3, 2)], [(s3, 3)]]
        for step in plan:
            for f, i in step:
                f(i)
            yield
        B_q.give(q, lastT[-1])
        B_k.give(k_, lastT[-1])
        B_v.give(vv, lastT[-1])
        b = bank()
        for i in range(4):
            T.w(items[i]["ta"])
            m = pe.transpose(b[:, i * 128:i * 128 + 128], at[:, i, :], ident)
        tk = T(m)
        B_at.give(at, tk)
        tk = evac(attT[:, h, :], b[:, :], col("subln_w"), after=tk)
        PS.give(b, tk)
        heads[h] = tk
        yield

    run_both(dense_head(0), None)
    for h in range(7):
        run_both(dense_head(h + 1), attend(h))

    run_both(None, attend(7))
    fence()

    WS = Arena(work0, high)
    wdt = sb("wdt", [128, 8, 32], stack=WS)
    dt_ = sb("dt_", [128, NT, 32], stack=WS)
    da = sb("da", [128, NT, 32], stack=WS)
    sp1 = sb("sp1", [128, NT, 32], stack=WS)
    sp2 = sb("sp2", [128, NT, 32], stack=WS)
    sp3 = sb("sp3", [128, NT, 32], stack=WS)
    ecum = sb("ecum", [128, NT, 32], stack=WS)
    etail = sb("etail", [128, NT, 32], stack=WS)
    etot = sb("etot", [128, NT, 32], stack=WS)
    aexp = sb("aexp", [128, 32], stack=WS)
    U = [sb(f"u{i}", [128, 520], stack=WS) for i in range(2)]
    B_acc = bufs("acc", 2, [128, S], WS)
    B_x = bufs("xs", 2, [128, NT, 256], WS)
    B_BT = bufs("BT", 2, [128, S], WS)
    B_CT = bufs("CT", 2, [128, S], WS)
    B_Bk = bufs("Bk", 2, [128, NT, 128], WS)
    B_z = bufs("zs", 2, [128, NT, 256], WS)
    B_R = bufs("R", 2, [128, 4, 128], WS)
    B_E = bufs("E", 2, [128, 4, 128], WS)
    B_cb = bufs("cbm", 2, [128, 128], WS)
    B_xd = bufs("xd", 2, [128, 3, 256], WS)
    B_y = bufs("yy", 2, [128, 3, 256], WS)
    B_yn = bufs("yn", 2, [128, NT, 256], WS)
    B_sta = bufs("sta", 3, [128, 256], WS)
    B_st2 = bufs("st2", 4, [128, 4], WS)

    wl = Lane(sem("s_wdt"))
    t_wdt = wl(nc.gpsimd.dma_start(wdt[:, :, :], wview("w_in", 9216, 32)))
    for u in U:
        t_u0 = V(v.memset(u[:, 0:4], 0.0))
    B_u = Pool(U)

    def setup_ssd():
        b = bank()
        T.w(t_wdt)
        for tt in range(NT):
            tk = T(mm_group(b[:, tt * 32:tt * 32 + 32], lambda k: hT[:, k, tt * 128:tt * 128 + 128],
                            lambda k: wdt[:, k, :], 8))
        V.w(tk)
        bc = lambda x: x.unsqueeze(1).to_broadcast([128, NT, 32])
        tk = V(v.tensor_tensor(sp1[:, :, :], b[:, 0:128].rearrange("p (a b) -> p a b", a=NT), bc(scv("dt_bias")), ADD))
        PS.give(b, tk)
        V(v.tensor_scalar(sp2[:, :, :], sp1[:, :, :], -1.0, None, MUL))
        tk = V(v.tensor_tensor(sp2[:, :, :], sp1[:, :, :], sp2[:, :, :], MIN))
        A.w(tk)
        tk = A(a.activation(sp2[:, :, :], sp2[:, :, :], ACT.Exp))
        tk2 = A(a.activation(aexp[:, :], scv("a_log"), ACT.Exp))
        V.w(tk, tk2)
        V(v.tensor_scalar(sp3[:, :, :], sp2[:, :, :], 2.0, None, ADD))
        V(v.reciprocal(sp3[:, :, :], sp3[:, :, :]))
        V(v.tensor_tensor(sp2[:, :, :], sp2[:, :, :], sp3[:, :, :], MUL))
        V(v.tensor_tensor(sp3[:, :, :], sp2[:, :, :], sp2[:, :, :], MUL))
        V(v.tensor_scalar(dt_[:, :, :], sp3[:, :, :], 2.0 / 17, 2.0 / 15, MUL, ADD))
        for c in (13, 11, 9, 7, 5, 3, 1):
            V(v.tensor_tensor(dt_[:, :, :], dt_[:, :, :], sp3[:, :, :], MUL))
            V(v.tensor_scalar(dt_[:, :, :], dt_[:, :, :], 2.0 / c, None, ADD))
        V(v.tensor_tensor(dt_[:, :, :], dt_[:, :, :], sp2[:, :, :], MUL))
        V(v.scalar_tensor_tensor(dt_[:, :, :], sp1[:, :, :], 0.0, dt_[:, :, :], MAX, ADD))
        tk = V(v.scalar_tensor_tensor(da[:, :, :], dt_[:, :, :], -1.0, bc(aexp[:, :]), MUL, MUL))
        G.w(tk)
        T.w(tk)
        yield
        b = bank()
        daf = da[:, :, :].rearrange("p a b -> p (a b)")
        pe.matmul(b[:, 0:128], cc("tri"), daf, start=True, stop=True)
        pe.matmul(b[:, 128:256], cc("gt"), daf, start=True, stop=True)
        tk = T(pe.matmul(b[:, 256:384], cc("ones"), daf, start=True, stop=True))
        A.w(tk)
        for i, dst in enumerate((ecum, etail, etot)):
            tk = A(a.activation(dst[:, :, :].rearrange("p a b -> p (a b)"), b[:, i * 128:i * 128 + 128], ACT.Exp))
        PS.give(b, tk)
        V.w(tk)
        G.w(tk)
        yield

    groups = {}

    def dense_group(gr):
        w, wt, wi = take(8, 512)
        T.w(wt)
        xs, xt = B_x.take()
        BT, BTt = B_BT.take()
        CT, CTt = B_CT.take()
        Bk, Bkt = B_Bk.take()
        zs, zt = B_z.take()
        pend = None

        def turn(p):
            src, tk, j = p
            b = bank()
            T.w(tk)
            for tt in range(NT):
                m = pe.transpose(b[:, tt * 128:tt * 128 + 128], src[:, tt * 128:tt * 128 + 128], ident)
            tk = T(m)
            if j < 2:
                B_acc.give(src, tk)
                A.w(tk, xt)
                tk = A(a.copy(xs[:, :, j * 128:j * 128 + 128], b[:, :].rearrange("p (a b) -> p a b", a=NT)))
            else:
                A.w(tk, Bkt)
                tk = A(a.copy(Bk[:, :, :], b[:, :].rearrange("p (a b) -> p a b", a=NT)))
            PS.give(b, tk)
            return tk

        rec = {}
        for j in range(4):
            ch = (gr * 2, gr * 2 + 1, 16 + gr, 24 + gr)[j]
            b = bank()
            tk = T(mm_group(b[:, :], lambda k: w[:, k, j * 128:j * 128 + 128], lambda k: hT[:, k, :], 8))
            if j == 3:
                release(wi, tk)
            u, ut = B_u.take()
            A.w(ut, tk, t_u0)
            tk = A(a.copy(u[:, 4:516], b[:, :]))
            PS.give(b, tk)
            if j < 2:
                acc, at_ = B_acc.take()
            else:
                acc, at_ = (BT, BTt) if j == 2 else (CT, CTt)
            V.w(tk, at_)
            V(v.tensor_scalar(acc[:, :], u[:, 4:516], conv_col(3, ch), col("conv_b", ch), MUL, ADD))
            for kk in (2, 1, 0):
                tk = V(v.scalar_tensor_tensor(acc[:, :], u[:, 1 + kk:513 + kk], conv_col(kk, ch), acc[:, :], MUL, ADD))
            B_u.give(u, tk)
            A.w(tk)
            tk = A(a.activation(acc[:, :], acc[:, :], ACT.Silu))
            if j == 2:
                rec["BT"] = tk
            if j == 3:
                rec["CT"] = tk
            yield
            if pend is not None:
                rec[pend[2]] = turn(pend)
            pend = (acc, tk, j) if j < 3 else None
        w, wt, wi = take(8, 256)
        T.w(wt)
        for hb in range(2):
            b = bank()
            for q in range(2):
                tt = hb * 2 + q
                m = mm_group(b[:, q * 256:q * 256 + 256], lambda k: hT[:, k, tt * 128:tt * 128 + 128],
                             lambda k: w[:, k, :], 8)
                tk = T(m)
                yield
            A.w(tk, zt)
            tz = A(a.activation(zs[:, hb * 2:hb * 2 + 2, :].rearrange("p a b -> p (a b)"), b[:, :], ACT.Silu))
            PS.give(b, tz)
        release(wi, tk)
        rec["z"] = tz
        groups[gr] = (xs, BT, CT, Bk, zs, rec)

    def scan_group(gr):
        xs, BT, CT, Bk, zs, rec = groups[gr]
        yn, ynt = B_yn.take()
        its = [dict() for _ in range(4)]
        cur = {"s": None, "t": None}
        hs = slice(gr * 4, gr * 4 + 4)
        used = []

        def bc(x, n=64):
            return x.unsqueeze(2).to_broadcast([128, 4, n])

        def v4(x):
            return x.rearrange("p (r q) -> p r q", r=4)

        def t1(c):
            it = its[c]
            R, Rt = B_R.take()
            V.w(Rt)
            tr = V(v.tensor_tensor(R[:, :, :], cc("tri").unsqueeze(1).to_broadcast([128, 4, 128]),
                                   bc(da[:, c, hs], 128), MUL))
            xd, xdt = B_xd.take()
            G.w(xdt, rec[0], rec[1])
            G(g.tensor_tensor(v4(xd[:, 0, :]), v4(xs[:, c, :]), bc(dt_[:, c, hs]), MUL))
            G(g.tensor_tensor(v4(xd[:, 2, :]), v4(xs[:, c, :]), bc(scv("d_skip")[:, hs]), MUL))
            it["txd"] = G(g.tensor_tensor(v4(xd[:, 1, :]), v4(xd[:, 0, :]), bc(etail[:, c, hs]), MUL))
            it["xd"] = xd
            b = bank()
            T.w(rec["BT"], rec["CT"])
            ck = slice(c * 128, c * 128 + 128)
            tb = T(pe.matmul(b[:, 0:128], BT[:, ck], CT[:, ck], start=True, stop=True))
            b2 = bank()
            T.w(tr)
            ts = T(pe.matmul(b2[:, :], cc("gt"), R[:, :, :].rearrange("p a b -> p (a b)"), start=True, stop=True))
            B_R.give(R, ts)
            cb, cbt = B_cb.take()
            V.w(cbt, tb)
            tc = V(v.tensor_tensor(cb[:, :], b[:, 0:128], cc("tri"), MUL))
            PS.give(b, tc)
            E, Et = B_E.take()
            A.w(Et, ts)
            te = A(a.activation(E[:, :, :].rearrange("p a b -> p (a b)"), b2[:, :], ACT.Exp))
            PS.give(b2, te)
            V.w(te, tc)
            tm = V(v.tensor_tensor(E[:, :, :], E[:, :, :], cb[:, :].unsqueeze(1).to_broadcast([128, 4, 128]), MUL))
            B_cb.give(cb, tm)
            it["E"], it["tm"] = E, tm

        def t2(c):
            it = its[c]
            E, xd = it["E"], it["xd"]
            b = bank()
            ck = slice(c * 128, c * 128 + 128)
            if c > 0:
                T.w(cur["t"])
                pe.matmul(b[:, 256:512], CT[:, ck], cur["s"][:, :], start=True, stop=True)
            T.w(it["tm"], it["txd"])
            for r in range(4):
                m = pe.matmul(b[:, r * 64:r * 64 + 64], E[:, r, :], xd[:, 0, r * 64:r * 64 + 64], start=True, stop=True)
            ty = T(m)
            B_E.give(E, ty)
            if c < 3:
                b2 = bank()
                T.w(rec[2])
                ts = T(pe.matmul(b2[:, 0:256], Bk[:, c, :], xd[:, 1, :], start=True, stop=True))
                used.append(ts)
                new, nt = B_sta.take()
                V.w(nt, ts)
                if c == 0:
                    tk = V(v.tensor_copy(new[:, :], b2[:, 0:256]))
                else:
                    V.w(cur["t"])
                    V(v.tensor_tensor(v4(new[:, :]), v4(cur["s"][:, :]), bc(etot[:, c, hs]), MUL))
                    tk = V(v.tensor_tensor(new[:, :], new[:, :], b2[:, 0:256], ADD))
                PS.give(b2, tk)
                if c > 0:
                    B_sta.give(cur["s"], tk, ty)
                cur["s"], cur["t"] = new, tk
            else:
                B_sta.give(cur["s"], ty)
            used.append(ty)
            y, yt = B_y.take()
            V.w(yt, ty, it["txd"])
            V(v.tensor_tensor(y[:, 0, :], b[:, 0:256], xd[:, 2, :], ADD))
            if c > 0:
                V(v.tensor_tensor(v4(y[:, 1, :]), v4(b[:, 256:512]), bc(ecum[:, c, hs]), MUL))
                tk = V(v.tensor_tensor(y[:, 0, :], y[:, 0, :], y[:, 1, :], ADD))
            PS.give(b, V.last())
            B_xd.give(xd, V.last(), ty, it["txd"])
            V.w(rec["z"])
            tk = V(v.tensor_tensor(y[:, 0, :], y[:, 0, :], zs[:, c, :], MUL))
            sm, smt = B_st2.take()
            A.w(tk, smt)
            tk = A(a.activation(y[:, 1, :], y[:, 0, :], ACT.Square, scale=1.0 / 16, accum_out=sm[:, 0:1]))
            tk = rstd(sm[:, 1:2], sm[:, 0:1], 1e-5, tk)
            V.w(tk, ynt)
            tk = V(v.tensor_scalar(yn[:, c, :], y[:, 0, :], sm[:, 1:2], None, MUL))
            B_y.give(y, tk)
            B_st2.give(sm, tk)
            it["ty"] = tk

        for step in ([(t1, 0)], [(t1, 1)], [(t2, 0)], [(t1, 2)], [(t2, 1)], [(t1, 3)], [(t2, 2)], [(t2, 3)]):
            for f, i in step:
                f(i)
            yield
        B_x.give(xs, its[3]["txd"])
        B_BT.give(BT, used[-1])
        B_CT.give(CT, used[-1])
        B_Bk.give(Bk, used[-1])
        B_z.give(zs, its[3]["ty"])
        for j in range(2):
            b = bank()
            for c in range(4):
                T.w(its[c]["ty"])
                m = pe.transpose(b[:, c * 128:c * 128 + 128], yn[:, c, j * 128:j * 128 + 128], ident)
            tk = T(m)
            if j == 1:
                B_yn.give(yn, tk)
            tk = evac(ssdT[:, gr * 2 + j, :], b[:, :], col("ssd_norm_w", gr * 2 + j), after=tk)
            PS.give(b, tk)
            yield

    def first():
        yield from setup_ssd()
        yield from dense_group(0)

    run_both(first(), None)
    for gr in range(7):
        run_both(dense_group(gr + 1), scan_group(gr))
    run_both(None, scan_group(7))
    fence()

    WM = Arena(work0, high)
    X2 = sb("X2", [128, NT, D], stack=WM)
    sga = sb("sga", [128, 4, S], stack=WM)
    B_m2 = bufs("m2", 2, [128, S], WM)
    mT = sb("mT", [128, 8, S], stack=WM)
    lx = Lane(sem("s_x2"))
    t_x2 = lx(nc.gpsimd.dma_start(X2[:, :, :], t["x"].rearrange("a (n p) d -> p (a n) d", p=128)))
    tm_ = [None] * 8

    def gate_part(half, kind):
        w, wt, wi = take(8, 512)
        T.w(wt)
        rt = None
        for j in range(4):
            b = bank()
            tk = T(mm_group(b[:, :], lambda k: w[:, k, j * 128:j * 128 + 128], lambda k: hT[:, k, :], 8))
            A.w(tk, sg_free[j])
            sg_tok[j] = A(a.activation(sga[:, j, :], b[:, :], ACT.Sigmoid))
            PS.give(b, sg_tok[j])
            yield
        release(wi, tk)

    sg_free = [None] * 4
    sg_tok = [None] * 4

    def attn_part(half):
        w, wt, wi = take(8, 512)
        T.w(wt)
        for j in range(4):
            b = bank()
            tk = T(mm_group(b[:, :], lambda k: w[:, k, j * 128:j * 128 + 128], lambda k: attT[:, k, :], 8))
            f = half * 4 + j
            V.w(tk, sg_tok[j])
            tm_[f] = V(v.tensor_tensor(mT[:, f, :], b[:, :], sga[:, j, :], MUL))
            sg_free[j] = tm_[f]
            PS.give(b, tm_[f])
            yield
        release(wi, tk)

    def ssd_part(half):
        w0, wt0, wi0 = take(8, 512)
        w1, wt1, wi1 = take(8, 512)
        T.w(wt0, wt1)
        for j in range(4):
            b = bank()
            js = slice(j * 128, j * 128 + 128)
            mm_group(b[:, :], lambda k: w0[:, k, js], lambda k: ssdT[:, k, :], 8, stop=False)
            tk = T(mm_group(b[:, :], lambda k: w1[:, k, js], lambda k: ssdT[:, 8 + k, :], 8, start=False))
            f = half * 4 + j
            m2, mt = B_m2.take()
            V.w(tk, sg_tok[j], mt)
            t1 = V(v.tensor_tensor(m2[:, :], b[:, :], sga[:, j, :], MUL))
            sg_free[j] = t1
            PS.give(b, t1)
            tm_[f] = V(v.tensor_tensor(mT[:, f, :], mT[:, f, :], m2[:, :], ADD))
            B_m2.give(m2, tm_[f])
            yield
        release(wi0, tk)
        release(wi1, tk)

    for h in range(8):
        T.w(heads[h])

    for gen in (gate_part(0, 0), attn_part(0), gate_part(0, 1), ssd_part(0)):
        run_both(gen, None)
    for gen in (gate_part(1, 0), attn_part(1), gate_part(1, 1), ssd_part(1)):
        run_both(gen, None)
    T.w(tm_)
    tx = [None] * NT
    for half in range(2):
        w, wt, wi = take(8, 512)
        T.w(wt)
        for tt in range(NT):
            b = bank()
            tk = T(mm_group(b[:, :], lambda k: mT[:, k, tt * 128:tt * 128 + 128], lambda k: w[:, k, :], 8))
            V.w(tk, t_x2)
            xv = X2[:, tt, half * 512:half * 512 + 512]
            tx[tt] = V(v.tensor_tensor(xv, xv, b[:, :], ADD))
            PS.give(b, tx[tt])
        release(wi, tk)
    fence()

    RA = Arena(region_a, region_a + 65536)
    WR = Arena(work0 + 16384, high)
    for i in range(4):
        ring.append(sb(f"ringx{i}", [128, 4096], stack=RA))
        rlane.append(Lane(sem(f"s_ringx{i}")))
        slots.append((RING + i, None))
        SP.w(V.last(), A.last(), T.last(), G.last())
        issue()
    EB = 64 + NOV
    sidx = sb("sidx", [128, EB], I32, stack=WR)
    gidx = sb("gidx", [128, EB], I32, stack=WR)
    wts = sb("wts", [128, NT, 2], stack=WR)
    work1 = WR.at
    H2 = sb("H2", [128, NT, D], stack=WR)
    H2T = sb("H2T", [128, 8, S], stack=WR)
    wrt = sb("wrt", [128, 8, 72], stack=WR)
    frow = sb("frow", [128, D], stack=WR)
    L = sb("L", [128, NT, 72], stack=WR)
    ra = sb("ra", [128, NT, 64], stack=WR)
    rb = sb("rb", [128, NT, 64], stack=WR)
    O = [sb(f"O{k}", [128, NT, 64], stack=WR) for k in range(2)]
    AS = sb("AS", [128, NT, 64], stack=WR)
    s8 = sb("s8", [128, 12, NT, 8], stack=WR)
    s4 = sb("s4", [128, 16, NT], stack=WR)
    e64 = sb("e64", [128, 6, 64], stack=WR)
    oR = sb("oR", [128, 2, 128], stack=WR)
    oB = sb("oB", [128, 2, EB], stack=WR)
    lw = Lane(sem("s_rt"))
    t_rt = lw(nc.gpsimd.dma_start(wrt[:, :, 0:8], wview("w_group_router", 0, 8)))
    t_rt = lw(nc.gpsimd.dma_start(wrt[:, :, 8:72], wview("w_expert_router", 0, 64)))
    t_rt = lw(nc.gpsimd.dma_start(frow[:, :], t["norm_ffn_w"].to_broadcast([128, D])))
    h2d = nc.dram_tensor("h2d", (S, D), F32, kind="Internal").ap()
    ybuf = nc.dram_tensor("ybuf", (2 * S, D), F32, kind="Internal").ap()

    tn = norm_to(H2, X2, [None] * NT)
    V.w(t_rt)
    th = []
    for tt in range(NT):
        th.append(V(v.tensor_tensor(H2[:, tt, :], H2[:, tt, :], frow[:, :], MUL)))
    G.w(th)
    lh = Lane(sem("s_h2"))
    t_h2d = lh(nc.gpsimd.dma_start(h2d.rearrange("(n p) d -> p n d", p=128), H2[:, :, :]))
    t_h = to_features(H2T, H2, th, None)
    T.w(t_h, t_rt)
    b = bank()
    for tt in range(NT):
        tk = T(mm_group(b[:, tt * 72:tt * 72 + 72], lambda k: H2T[:, k, tt * 128:tt * 128 + 128],
                        lambda k: wrt[:, k, :], 8))
    V.w(tk)
    bv = b[:, 0:288].rearrange("p (a b) -> p a b", a=NT)
    V(v.tensor_tensor(L[:, :, 0:8], bv[:, :, 0:8], scv("b_group_router").unsqueeze(1).to_broadcast([128, NT, 8]), ADD))
    tk = V(v.tensor_tensor(L[:, :, 8:72], bv[:, :, 8:72],
                           scv("b_expert_router").unsqueeze(1).to_broadcast([128, NT, 64]), ADD))
    PS.give(b, tk)

    def up8(x):
        return x.unsqueeze(2).to_broadcast([128, NT, 8])

    iota8m = cc("iota8m").unsqueeze(1).to_broadcast([128, NT, 8])

    def first_max(src, mx, hot, tmp):
        V(v.tensor_reduce(mx, src, AX.X, MAX))
        V(v.tensor_tensor(hot, src, up8(mx), EQ))
        V(v.tensor_scalar(hot, hot, -1000.0, 1000.0, MUL, ADD))
        V(v.tensor_tensor(hot, hot, iota8m, ADD))
        V(v.tensor_reduce(tmp, hot, AX.X, MIN))
        return V(v.tensor_tensor(hot, iota8m, up8(tmp), EQ))

    gm, tmp, v1, v2, gate, w1c, w2c = (s4[:, i, :] for i in range(7))
    gh, es, h1, h2_, e2, ex = (s8[:, i, :, :] for i in range(6))
    first_max(L[:, :, 0:8], gm, gh, tmp)
    tk = V(v.tensor_tensor(ex, L[:, :, 0:8], up8(gm), SUB))
    A.w(tk)
    tk = A(a.activation(ex, ex, ACT.Exp))
    V.w(tk)
    V(v.tensor_reduce(gate, ex, AX.X, ADD))
    V(v.reciprocal(gate, gate))
    EL = L[:, :, 8:72].rearrange("p t (g j) -> p t g j", g=8)
    for tt in range(NT):
        V(v.tensor_tensor(ra[:, tt, :].rearrange("p (g j) -> p g j", g=8), EL[:, tt, :, :],
                          gh[:, tt, :].unsqueeze(2).to_broadcast([128, 8, 8]), MUL))
        V(v.tensor_reduce(es[:, tt, :], ra[:, tt, :].rearrange("p (g j) -> p j g", g=8), AX.X, ADD))
    first_max(es, v1, h1, tmp)
    V(v.scalar_tensor_tensor(e2, h1, -BIG, es, MUL, ADD))
    first_max(e2, v2, h2_, tmp)
    tk = V(v.tensor_tensor(w2c, v2, v1, SUB))
    A.w(tk)
    tk = A(a.activation(w2c, w2c, ACT.Exp))
    V.w(tk)
    V(v.tensor_scalar(w1c, w2c, 1.0, None, ADD))
    V(v.reciprocal(w1c, w1c))
    V(v.tensor_tensor(w1c, w1c, gate, MUL))
    V(v.tensor_tensor(w2c, w2c, w1c, MUL))
    V(v.tensor_copy(wts[:, :, 0], w1c))
    V(v.tensor_copy(wts[:, :, 1], w2c))
    for k, hot in ((0, h1), (1, h2_)):
        for tt in range(NT):
            V(v.tensor_tensor(O[k][:, tt, :].rearrange("p (g j) -> p g j", g=8),
                              gh[:, tt, :].unsqueeze(2).to_broadcast([128, 8, 8]),
                              hot[:, tt, :].unsqueeze(1).to_broadcast([128, 8, 8]), MUL))
    tk = V(v.tensor_tensor(AS[:, :, :], O[0][:, :, :], O[1][:, :, :], ADD))
    T.w(tk)
    b = bank()
    for tt in range(NT + 1):
        o = b[:, tt * 64:tt * 64 + 64]
        full = list(range(min(tt, NT)))
        for q in full:
            m = pe.matmul(o, cc("ones"), AS[:, q, :], start=q == 0, stop=(tt == NT and q == NT - 1))
        if tt < NT:
            m = pe.matmul(o, cc("lt"), AS[:, tt, :], start=tt == 0, stop=True)
    tk = T(m)
    V.w(tk)
    V(v.tensor_copy(rb[:, :, :].rearrange("p a b -> p (a b)"), b[:, 0:256]))
    cnt = e64[:, 0, :]
    tk = V(v.tensor_copy(cnt, b[:, 256:320]))
    PS.give(b, tk)
    nov = e64[:, 1, :]
    V(v.tensor_scalar(nov, cnt, float(CAP), None, GT))
    for m_ in range(CAP + 128, 512, 128):
        V(v.tensor_scalar(e64[:, 2, :], cnt, float(m_), None, GT))
        V(v.tensor_tensor(nov, nov, e64[:, 2, :], ADD))
    inc, alt = e64[:, 3, :], e64[:, 4, :]
    V(v.tensor_copy(inc, nov))
    d = 1
    while d < 64:
        V(v.tensor_copy(alt[:, 0:d], inc[:, 0:d]))
        V(v.tensor_tensor(alt[:, d:64], inc[:, d:64], inc[:, 0:64 - d], ADD))
        inc, alt = alt, inc
        d *= 2
    exc = e64[:, 5, :]
    V(v.tensor_tensor(exc, inc, nov, SUB))
    V(v.tensor_copy(ovn[:, 7:8], inc[:, 63:64]))
    for o in range(min(NOV, 7)):
        V(v.tensor_scalar(e64[:, 2, :], inc, float(o), None, LE))
        V(v.tensor_reduce(st[:, 20:21], e64[:, 2, :], AX.X, ADD))
        V(v.tensor_scalar(st[:, 20:21], st[:, 20:21], 63.0, None, MIN))
        t_ovn = V(v.tensor_copy(ovn[:, o:o + 1], st[:, 20:21]))
    b = bank()
    t_r = [None, None]
    for k in range(2):
        rank, eid, ovs, over, hi, pos, blk = (s4[:, 8 + i, :] for i in range(7))
        for dst, other in ((rank, rb[:, :, :]), (eid, cc("iota64").unsqueeze(1).to_broadcast([128, NT, 64])),
                           (ovs, exc.unsqueeze(1).to_broadcast([128, NT, 64]))):
            V(v.tensor_tensor(ra[:, :, :], O[k][:, :, :], other, MUL))
            V(v.tensor_reduce(dst, ra[:, :, :], AX.X, ADD))
        V(v.tensor_scalar(over, rank, float(CAP), None, GE))
        V(v.tensor_scalar(hi, rank, float(CAP + 128), None, GE))
        for m_ in range(CAP + 256, 512, 128):
            V(v.tensor_scalar(tmp, rank, float(m_), None, GE))
            V(v.tensor_tensor(hi, hi, tmp, ADD))
        V(v.scalar_tensor_tensor(pos, over, -float(CAP), rank, MUL, ADD))
        V(v.scalar_tensor_tensor(pos, hi, -128.0, pos, MUL, ADD))
        V(v.tensor_tensor(ovs, ovs, hi, ADD))
        V(v.tensor_scalar(ovs, ovs, 64.0, None, ADD))
        V(v.tensor_tensor(ovs, ovs, eid, SUB))
        V(v.tensor_tensor(ovs, ovs, over, MUL))
        V(v.tensor_tensor(blk, eid, ovs, ADD))
        for tt in range(NT):
            V.w(t_r[k])
            V(v.tensor_scalar(oR[:, k, :], cc("iota128"), pos[:, tt:tt + 1], None, EQ))
            V(v.tensor_scalar(oB[:, k, 0:64], cc("iota64"), blk[:, tt:tt + 1], cc("aid1")[:, tt * 2 + k:tt * 2 + k + 1], EQ, MUL))
            V(v.tensor_scalar(tmp[:, 0:1], blk[:, tt:tt + 1], -64.0, None, ADD))
            tk = V(v.tensor_scalar(oB[:, k, 64:EB], cc("ovid")[:, 0:NOV] if NOV <= 8 else cc("iota64")[:, 0:NOV], tmp[:, 0:1],
                                   cc("aid1")[:, tt * 2 + k:tt * 2 + k + 1], EQ, MUL))
            T.w(tk)
            t_r[k] = T(pe.matmul(b[:, 0:EB], oR[:, k, :], oB[:, k, :], start=(k == 0 and tt == 0),
                                 stop=(k == 1 and tt == NT - 1)))
    V.w(t_r)
    tabf = oB[:, 0, :]
    tab2 = oB[:, 1, :]
    V(v.tensor_copy(tabf, b[:, 0:EB]))
    PS.give(b, V.last())
    V(v.tensor_scalar(tab2, tabf, 0.5, 5001.0, LE, MUL))
    V(v.tensor_tensor(tabf, tabf, tab2, ADD))
    V(v.tensor_scalar(tabf, tabf, -1.0, None, ADD))
    V(v.tensor_copy(sidx[:, :], tabf))
    V(v.tensor_scalar(tab2, tabf, 512.0, -512.0, GE, MUL))
    V(v.tensor_tensor(tabf, tabf, tab2, ADD))
    t_idx = V(v.tensor_copy(gidx[:, :], tabf))
    G.w(t_h2d, t_idx)
    V.w(t_h2d)
    fence()

    WE = Arena(work1, high)
    gxs = [sb(f"gx{i}", [128, D], stack=WE) for i in range(3)]
    gxTs = [sb(f"gxT{i}", [128, 8, 128], stack=WE) for i in range(2)]
    sgs = [sb(f"sg{i}", [128, 512], stack=WE) for i in range(2)]
    hids = [sb(f"hid{i}", [128, 512], stack=WE) for i in range(2)]
    hidTs = [sb(f"hidT{i}", [128, 4, 128], stack=WE) for i in range(2)]
    ys = [sb(f"ys{i}", [128, D], stack=WE) for i in range(2)]
    glane = [Lane(sem(f"s_gx{i}")) for i in range(3)]
    ylane = [Lane(sem(f"s_y{i}")) for i in range(2)]
    for x in gxs:
        t_gz = V(v.memset(x[:, :], 0.0))
    G.w(t_gz)

    def expert_run(n, col0, takew, give, glane, ylane):
        P_gx = Pool([(x, l) for x, l in zip(gxs, glane)])
        P_gxT, P_sg, P_hid, P_hidT = Pool(gxTs), Pool(sgs), Pool(hids), Pool(hidTs)
        P_y = Pool([(x, l) for x, l in zip(ys, ylane)])
        gath, its = {}, {}

        def gather(e):
            if e >= n:
                return
            (x, lane), tk = P_gx.take()
            G.w(tk)
            gath[e] = (x, lane, lane(g.indirect_dma_start(
                out=x[:, :], out_offset=None, in_=h2d[:, :],
                in_offset=bass.IndirectOffsetOnAxis(ap=gidx[:, col0 + e:col0 + e + 1].bitcast(U32), axis=0),
                bounds_check=S - 1, oob_is_err=False)))

        def turn(e):
            if e >= n:
                return
            x, lane, tk = gath[e]
            T.w(tk)
            xT, xt = P_gxT.take()
            for half in range(2):
                b = bank()
                for j in range(4):
                    k = half * 4 + j
                    m = pe.transpose(b[:, j * 128:j * 128 + 128], x[:, k * 128:k * 128 + 128], ident)
                tk = T(m)
                dst = xT[:, half * 4:half * 4 + 4, :].rearrange("p a b -> p (a b)")
                if half == 0:
                    V.w(tk, xt)
                    t0 = V(v.tensor_copy(dst, b[:, :]))
                    PS.give(b, t0)
                else:
                    A.w(tk, xt)
                    t1 = A(a.copy(dst, b[:, :]))
                    PS.give(b, t1)
            P_gx.give((x, lane), tk)
            gather(e + 3)
            its[e] = (xT, [t0, t1])

        def up(e):
            if e >= n:
                return
            xT, tks = its[e]
            T.w(tks)
            ps = []
            for j in range(2):
                w, wt, wi = takew(8, 512)
                T.w(wt)
                b = bank()
                tk = T(mm_group(b[:, :], lambda k: xT[:, k, :], lambda k: w[:, k, :], 8))
                give(wi, tk)
                ps.append((b, tk))
            P_gxT.give(xT, tk)
            s, stk = P_sg.take()
            h, htk = P_hid.take()
            A.w(ps[0][1], stk)
            tk = A(a.activation(s[:, :], ps[0][0][:, :], ACT.Silu))
            PS.give(ps[0][0], tk)
            V.w(tk, ps[1][1], htk)
            tk = V(v.tensor_tensor(h[:, :], ps[1][0][:, :], s[:, :], MUL))
            PS.give(ps[1][0], tk)
            P_sg.give(s, tk)
            its[e] = (h, tk)

        def down(e):
            if e < 0:
                return
            h, tk = its[e]
            T.w(tk)
            b = bank()
            for j in range(4):
                m = pe.transpose(b[:, j * 128:j * 128 + 128], h[:, j * 128:j * 128 + 128], ident)
            tk = T(m)
            P_hid.give(h, tk)
            hT_, ht = P_hidT.take()
            V.w(tk, ht)
            tk = V(v.tensor_copy(hT_[:, :, :].rearrange("p a b -> p (a b)"), b[:, :]))
            PS.give(b, tk)
            T.w(tk)
            w, wt, wi = takew(4, 1024)
            T.w(wt)
            (y, lane), yt = P_y.take()
            tks = []
            for half in range(2):
                b = bank()
                tk = T(mm_group(b[:, :], lambda k: hT_[:, k, :], lambda k: w[:, k, half * 512:half * 512 + 512], 4))
                if half == 0:
                    V.w(tk, yt)
                    tks.append(V(v.tensor_copy(y[:, 0:512], b[:, :])))
                else:
                    A.w(tk, yt)
                    tks.append(A(a.copy(y[:, 512:1024], b[:, :])))
                PS.give(b, tks[-1])
            give(wi, tk)
            P_hidT.give(hT_, tk)
            G.w(tks)
            tk = lane(g.indirect_dma_start(
                out=ybuf[:, :],
                out_offset=bass.IndirectOffsetOnAxis(ap=sidx[:, col0 + e:col0 + e + 1].bitcast(U32), axis=0),
                in_=y[:, :], in_offset=None, bounds_check=2 * S - 1, oob_is_err=False))
            P_y.give((y, lane), tk)

        for e in range(3):
            gather(e)
        turn(0)
        for e in range(n + 1):
            up(e)
            turn(e + 1)
            down(e - 1)
        return [(lane.sem, lane.n) for lane in list(glane) + list(ylane)]

    t_y = expert_run(64, 0, take, release, glane, ylane)

    for e in (V, A, T, G, SP):
        e.w(t_y)
    fence()
    SP.w(V.last(), A.last(), T.last(), G.last())
    ovr = nc.values_load(ovn[0:1, 7:8], min_val=0, max_val=NOV)
    saved = (V, A, T, G, SP, PS)
    with nc.If(ovr > 0):
        V = Engine(nc.vector, sem("s_dve2"))
        A = Engine(nc.scalar, sem("s_act2"))
        T = Engine(nc.tensor, sem("s_pe2"), serial=False)
        G = Engine(nc.gpsimd, sem("s_pool2"))
        SP = Engine(nc.sync, sem("s_sp2"))
        PS = Pool(banks)
        ob = [sb(f"ob{i}", [128, 4096], stack=WE) for i in range(1)]
        olane = Lane(sem("s_ob"))
        ostate = {"n": 0, "free": None}

        def otake(k, n):
            i = ostate["n"]
            ostate["n"] = i + 1
            order = []
            for e in range(NOV + 1):
                if e < NOV:
                    order += [("w_expert_gate", e), ("w_expert_up", e)]
                if e > 0:
                    order.append(("w_expert_down", e - 1))
            name, e = order[i]
            SP.w(ostate["free"])
            er = nc.sync.value_load(ovn[0:1, min(e, 6):min(e, 6) + 1], min_val=0, max_val=63)
            src = t[name].rearrange("a e (k p) n -> p (a e) k n", p=128)[:, bass.ds(er, 1), :, :]
            dst = ob[0][:, 0:k * n].rearrange("p (e k n) -> p e k n", k=k, e=1)
            tk = olane(nc.sync.dma_start(dst, src))
            return ob[0][:, 0:k * n].rearrange("p (k n) -> p k n", k=k), tk, i

        def ogive(i, tk):
            ostate["free"] = [tk]

        gl2 = [Lane(sem(f"s_gz{i}")) for i in range(3)]
        yl2 = [Lane(sem(f"s_yz{i}")) for i in range(2)]
        ty2 = expert_run(NOV, 64, otake, ogive, gl2, yl2)
        for e in (V, A, T, G, SP):
            e.w(ty2)
        fence()
        SP.w(V.last(), A.last(), T.last(), G.last())
    V, A, T, G, SP, PS = saved
    PS = Pool(banks)
    A.w(V(v.memset(st[:, 20:21], 0.0)))
    A(a.copy(st[:, 21:22], st[:, 20:21]))
    T(pe.matmul(banks[0][:, 0:1], ident, ident[:, 0:1], start=True, stop=True))
    G(g.memset(st[:, 23:24], 0.0))
    fence()

    WC = Arena(work1, high)
    Y = [sb(f"Y{k}", [128, NT, D], stack=WC) for k in range(2)]
    nrow_ = sb("fnrow", [128, D], stack=WC)
    ly = [Lane(sem(f"s_cy{k}")) for k in range(2)]
    t_c = [ly[k](nc.gpsimd.dma_start(Y[k][:, :, :], ybuf[k * S:(k + 1) * S, :].rearrange("(n p) d -> p n d", p=128)))
           for k in range(2)]
    lf = Lane(sem("s_fn"))
    t_f = lf(nc.gpsimd.dma_start(nrow_[:, :], t["final_norm_w"].unsqueeze(0).to_broadcast([128, D])))
    tc = []
    V.w(t_c)
    for tt in range(NT):
        for k in range(2):
            tk = V(v.scalar_tensor_tensor(X2[:, tt, :], Y[k][:, tt, :], wts[:, tt, k:k + 1], X2[:, tt, :], MUL, ADD))
        tc.append(tk)
    tn = norm_to(Y[0], X2, tc)
    V.w(t_f)
    t_x3 = [V(v.tensor_tensor(X2[:, tt, :], Y[0][:, tt, :], nrow_[:, :], MUL)) for tt in range(NT)]
    fence()

    RB = Arena(region_a, region_a + 65536)
    WB = Arena(work0 + 16384, high)
    A1 = sb("A1", [128, NT, D], stack=RB)
    G1 = sb("G1", [128, 8, S], stack=RB)
    P2 = sb("P2", [128, NT, 2464], stack=WB)
    QT = sb("QT", [128, 11, S], stack=WB)
    wuq = sb("wuq", [128, 2, 384], stack=RB)
    wukv = sb("wukv", [128, 512], stack=RB)
    qlT = sb("qlT", [128, 2, S], stack=RB)
    kvT = sb("kvT", [128, S], stack=RB)
    vm = sb("vm", [128, NT, 256], stack=RB)
    mrow = sb("mrow", [128, 2, 96], stack=RB)
    B_QK = bufs("QK", 2, [128, 8, 96], RB)
    ss2 = sb("ss2", [128, NT, 24], stack=RB)
    rs2 = sb("rs2", [128, NT, 24], stack=RB)
    mh2 = sb("mh2", [128, NT, 24], stack=RB)
    sm3 = sb("sm3", [128, 4, 16], stack=RB)
    sq = QT[:, 0:2, :].rearrange("p a b -> p (a b)")
    lm = Lane(sem("s_mla"))
    t_ml = lm(nc.gpsimd.dma_start(wuq[:, :, :], wview("mla_w_uq_2", 0, 384)))
    t_ml = lm(nc.gpsimd.dma_start(wukv[:, :], t["mla_w_ukv_2"].rearrange("a p n -> (a p) n")))
    t_ml = lm(nc.gpsimd.dma_start(mrow[:, 0, :], t["mla_q_g_2"].to_broadcast([128, 96])))
    t_ml = lm(nc.gpsimd.dma_start(mrow[:, 1, :], t["mla_k_g_2"].to_broadcast([128, 96])))
    t_mh = V(v.memset(mh2[:, :, :], -0.5))
    tn = norm_to(A1, X2, [None] * NT)
    t_h = to_features(G1, A1, tn, lambda k: col("attn_norm_g_2", k))
    T.w(t_h)
    tp = [None] * NT
    for c0 in range(0, 2464, 512):
        n = min(512, 2464 - c0)
        w, wt, wi = take(8, n)
        T.w(wt)
        for tt in range(NT):
            b = bank()
            tk = T(mm_group(b[:, 0:n], lambda k: G1[:, k, tt * 128:tt * 128 + 128], lambda k: w[:, k, :], 8))
            tk2 = evac(P2[:, tt, c0:c0 + n], b[:, 0:n], after=tk)
            PS.give(b, tk2)
        release(wi, tk)
    fence()

    SEG = ((0, 8), (1184, 8), (1952, 6))

    def heads_view(tt, c0, n):
        return P2[:, tt, c0:c0 + n * 64].rearrange("p (h c) -> p h c", h=n)

    for tt in range(NT):
        o = 0
        for c0, n in SEG:
            V(v.tensor_tensor(sq[:, 0:n * 64], P2[:, tt, c0:c0 + n * 64], P2[:, tt, c0:c0 + n * 64], MUL))
            V(v.tensor_reduce(ss2[:, tt, o:o + n], sq[:, 0:n * 64].rearrange("p (h c) -> p h c", h=n), AX.X, ADD))
            o += n
        tk = A(a.activation(sq[:, 512:768], P2[:, tt, 768:1024], ACT.Square, scale=0.5, accum_out=ss2[:, tt, 22:23]))
        tk = A(a.activation(sq[:, 768:896], P2[:, tt, 1024:1152], ACT.Square, scale=0.5 ** 0.5,
                            accum_out=ss2[:, tt, 23:24]))
    V.w(tk)
    tk = V(v.tensor_scalar(ss2[:, :, :], ss2[:, :, :], 1.0 / 64, 1e-6, MUL, ADD))
    G.w(tk, t_mh)
    tk = G(g.tensor_tensor(rs2[:, :, :], ss2[:, :, :], mh2[:, :, :], ALU.pow))
    V.w(tk)
    t_n = []
    for tt in range(NT):
        V(v.tensor_scalar(P2[:, tt, 768:1024], P2[:, tt, 768:1024], rs2[:, tt, 22:23], None, MUL))
        V(v.tensor_scalar(P2[:, tt, 1024:1152], P2[:, tt, 1024:1152], rs2[:, tt, 23:24], None, MUL))
        o = 0
        for c0, n in SEG:
            hv = heads_view(tt, c0, n)
            if c0 == 1952:
                V(v.tensor_scalar(sq[:, 0:64], hv[:, 1, :], rs2[:, tt, o + 1:o + 2], None, MUL))
                V(v.tensor_scalar(hv[:, 1, :], hv[:, 2, :], rs2[:, tt, o + 2:o + 3], None, MUL))
                V(v.tensor_copy(hv[:, 2, :], sq[:, 0:64]))
                V(v.tensor_scalar(hv[:, 0, :], hv[:, 0, :], rs2[:, tt, o:o + 1], None, MUL))
                hv, o, n = hv[:, 3:6, :], o + 3, 3
            tk = V(v.tensor_tensor(hv, hv, rs2[:, tt, o:o + n].unsqueeze(2).to_broadcast([128, n, 64]), MUL))
            o += n
        t_n.append(tk)

    def turn4(dst, src, scol):
        b = bank()
        for tt in range(NT):
            T.w(t_n[tt])
            m = pe.transpose(b[:, tt * 128:tt * 128 + 128], src(tt), ident)
        tk = T(m)
        tk = evac(dst, b[:, :], scol, after=tk)
        PS.give(b, tk)
        return tk

    t_l = []
    for k in range(2):
        t_l.append(turn4(qlT[:, k, :], lambda tt: P2[:, tt, 768 + k * 128:896 + k * 128], col("mla_qlat_g_2", k)))
    t_l.append(turn4(kvT[:, :], lambda tt: P2[:, tt, 1024:1152], col("mla_kvlat_g_2")))
    A.w(t_n)
    t_qt = []
    for base, c0, names in ((0, 0, ("moba_q_g_2", "moba_q_g_2", "moba_k_g_2", "moba_k_g_2")),
                            (4, 1184, ("dil_q_g_2", "dil_q_g_2", "dil_k_g_2", "dil_k_g_2"))):
        for i, name in enumerate(names):
            t_qt.append(turn4(QT[:, base + i, :], lambda tt: P2[:, tt, c0 + i * 128:c0 + i * 128 + 128], col(name)))
    for r in range(2):
        t_qt.append(turn4(QT[:, 8 + r, :], lambda tt: P2[:, tt, 1952 + r * 128:2080 + r * 128], col("swa_q_g_2")))
    t_qt.append(turn4(QT[:, 10, :], lambda tt: P2[:, tt, 2208:2336], col("swa_k_g_2")))

    QM = G1
    T.w(t_l, t_ml)
    V.w(t_ml)
    t_qm = []
    for tt in range(NT):
        ts = slice(tt * 128, tt * 128 + 128)
        bq = bank()
        t1 = T(mm_group(bq[:, 0:384], lambda k: qlT[:, k, ts], lambda k: wuq[:, k, :], 2))
        bk = bank()
        t2 = T(pe.matmul(bk[:, :], kvT[:, ts], wukv[:, :], start=True, stop=True))
        QK, qt = B_QK.take()
        V.w(t1, qt)
        tk = V(v.tensor_copy(QK[:, 0:4, :], bq[:, 0:384].rearrange("p (h c) -> p h c", h=4)))
        PS.give(bq, tk)
        kv = bk[:, :].rearrange("p (h c) -> p h c", h=4)
        V.w(t2)
        V(v.tensor_copy(QK[:, 4:8, 0:64], kv[:, :, 0:64]))
        tk = V(v.tensor_copy(vm[:, tt, :].rearrange("p (h c) -> p h c", h=4), kv[:, :, 64:128]))
        PS.give(bk, tk)
        tk = V(v.tensor_copy(QK[:, 4:8, 64:96], P2[:, tt, 1152:1184].unsqueeze(1).to_broadcast([128, 4, 32])))
        T_ = P2[:, tt, 0:512]
        V.w(t_qt[3])
        V(v.tensor_tensor(T_[:, 0:480].rearrange("p (h c) -> p h c", h=5), QK[:, 0:5, :], QK[:, 0:5, :], MUL))
        V(v.tensor_reduce(sm3[:, tt, 0:5], T_[:, 0:480].rearrange("p (h c) -> p h c", h=5), AX.X, ADD))
        V(v.tensor_tensor(T_[:, 0:288].rearrange("p (h c) -> p h c", h=3), QK[:, 5:8, :], QK[:, 5:8, :], MUL))
        V(v.tensor_reduce(sm3[:, tt, 5:8], T_[:, 0:288].rearrange("p (h c) -> p h c", h=3), AX.X, ADD))
        tk = V(v.tensor_scalar(sm3[:, tt, 0:8], sm3[:, tt, 0:8], 1.0 / 96, 1e-6, MUL, ADD))
        G.w(tk)
        tk = G(g.tensor_tensor(sm3[:, tt, 8:16], sm3[:, tt, 0:8], mh2[:, 0, 0:8], ALU.pow))
        V.w(tk)
        V(v.tensor_tensor(QK[:, :, :], QK[:, :, :], sm3[:, tt, 8:16].unsqueeze(2).to_broadcast([128, 8, 96]), MUL))
        for i in range(2):
            V(v.tensor_tensor(QK[:, i * 4:i * 4 + 4, :], QK[:, i * 4:i * 4 + 4, :],
                              mrow[:, i, :].unsqueeze(1).to_broadcast([128, 4, 96]), MUL))
        cs = cc("rcos")[:, tt * 16:tt * 16 + 16].unsqueeze(1).to_broadcast([128, 8, 16])
        sn = cc("rsin")[:, tt * 16:tt * 16 + 16].unsqueeze(1).to_broadcast([128, 8, 16])
        x1, x2 = QK[:, :, 64:80], QK[:, :, 80:96]
        u1, u2, u3 = (T_[:, i * 128:i * 128 + 128].rearrange("p (h c) -> p h c", h=8) for i in range(3))
        V(v.tensor_tensor(u1, x1, cs, MUL))
        V(v.tensor_tensor(u2, x2, sn, MUL))
        V(v.tensor_tensor(u3, x1, sn, MUL))
        V(v.tensor_tensor(x1, u1, u2, SUB))
        V(v.tensor_tensor(u1, x2, cs, MUL))
        tk = V(v.tensor_tensor(x2, u1, u3, ADD))
        T.w(tk)
        for i in range(2):
            b = bank()
            for j in range(4):
                m = pe.transpose(b[0:96, j * 128:j * 128 + 128], QK[:, i * 4 + j, :], ident)
            tk = T(m)
            tk2 = evac(QM[0:96, i * 4:i * 4 + 4, ts], b[0:96, :].rearrange("p (h c) -> p h c", h=4), after=tk)
            PS.give(b, tk2)
            t_qm.append(tk2)
        B_QK.give(QK, tk)

    mixed = A1
    B_bi = [(sb(f"bi{i}", [128, S], stack=RB), Lane(sem(f"s_bi{i}"))) for i in range(2)]
    P_bi = Pool(B_bi)
    B_s2 = bufs("s2_", 3, [128, S], WB)
    B_t2 = bufs("t2_", 2, [128, S], RB)
    stm = sb("stm", [128, 16, 8], stack=RB)
    T.w(t_qt, t_qm)
    order = [(0, h) for h in range(4)] + [(2, h) for h in range(4)] + [(3, h) for h in range(4)] + [(1, h) for h in range(4)]
    biases = {}

    def load_bias(n):
        if n < 12:
            (x, lane), tk = P_bi.take()
            G.w(tk)
            biases[n] = (x, lane, lane(nc.gpsimd.dma_start(x[:, :], t["biases"][n])))

    load_bias(0)
    load_bias(1)
    items = []
    for hn, (mx, h) in enumerate(order):
        for i in range(4):
            items.append({"m": mx, "h": h, "i": i, "hn": hn, "n": len(items)})

    def q_k_v(mx, h):
        r = slice((h % 2) * 64, (h % 2) * 64 + 64)
        if mx == 0:
            return QT[r, h // 2, :], QT[r, 2 + h // 2, :], lambda j: P2[:, j, 512 + h * 64:576 + h * 64]
        if mx == 2:
            return QT[r, 4 + h // 2, :], QT[r, 6 + h // 2, :], lambda j: P2[:, j, 1696 + h * 64:1760 + h * 64]
        if mx == 3:
            r = slice((h // 2) * 64, (h // 2) * 64 + 64)
            return QT[r, 8 + h % 2, :], QT[r, 10, :], lambda j: P2[:, j, 2336 + (h // 2) * 64:2400 + (h // 2) * 64]
        return QM[0:96, h, :], QM[0:96, 4 + h, :], lambda j: vm[:, j, h * 64:h * 64 + 64]

    def a1(it):
        i, mx = it["i"], it["m"]
        q, k_, _ = q_k_v(mx, it["h"])
        j0 = max(0, i - 1) if mx == 3 else 0
        kn = (i + 1 - j0) * 128
        it["j0"], it["kn"] = j0, kn
        b = bank()
        tk = T(pe.matmul(b[:, 0:kn], q[:, i * 128:i * 128 + 128], k_[:, j0 * 128:(i + 1) * 128], start=True, stop=True))
        s, stk = B_s2.take()
        sm = stm[:, it["n"] % 16, :]
        if it["n"] >= 16:
            V.w(items[it["n"] - 16]["done"])
        V.w(tk, stk)
        if mx == 1:
            bias, scale = cc("causal"), 96.0 ** -0.5
        else:
            x, lane, bt = biases[it["hn"]]
            V.w(bt)
            bias, scale = x[:, :], 1.0
        tk = V(v.tensor_tensor_reduce(s[:, 0:kn], b[:, 0:kn], bias[:, 512 - kn:512], 1.0, -3e38, ADD, MAX, sm[:, 0:1]))
        PS.give(b, tk)
        if mx != 1 and i == 3:
            P_bi.give((x, lane), tk)
            load_bias(it["hn"] + 2)
        if mx == 3:
            V(v.tensor_tensor(sm[:, 0:1], sm[:, 0:1], scv("swa_sinks_2")[:, it["h"]:it["h"] + 1], MAX))
        tk = V(v.tensor_scalar(sm[:, 1:2], sm[:, 0:1], -scale, None, MUL))
        A.w(tk)
        tk = A(a.activation(s[:, 0:kn], s[:, 0:kn], ACT.Exp, scale=scale, bias=sm[:, 1:2], accum_out=sm[:, 2:3]))
        it["s"], it["ts"] = s, tk
        if mx == 3:
            tk = A(a.activation(sm[:, 3:4], scv("swa_sinks_2")[:, it["h"]:it["h"] + 1], ACT.Exp, bias=sm[:, 1:2]))
            it["te"] = tk

    def a2(it):
        nb = it["kn"] // 128
        s = it["s"]
        sm = stm[:, it["n"] % 16, :]
        b = bank()
        T.w(it["ts"])
        for j in range(nb):
            m = pe.transpose(b[:, j * 128:j * 128 + 128], s[:, j * 128:j * 128 + 128], ident)
        tk = T(m)
        B_s2.give(s, tk)
        wt, wtt = B_t2.take()
        V.w(it["ts"])
        if it["m"] == 3:
            V.w(it["te"])
            V(v.tensor_tensor(sm[:, 2:3], sm[:, 2:3], sm[:, 3:4], ADD))
        V(v.reciprocal(sm[:, 4:5], sm[:, 2:3]))
        V.w(tk, wtt)
        tk = V(v.tensor_copy(wt[:, 0:it["kn"]], b[:, 0:it["kn"]]))
        PS.give(b, tk)
        it["wt"], it["twt"] = wt, tk

    def a3(it):
        _, _, vv = q_k_v(it["m"], it["h"])
        b = bank()
        T.w(it["twt"])
        tk = T(mm_group(b[:, 0:64], lambda j: it["wt"][:, j * 128:j * 128 + 128], lambda j: vv(it["j0"] + j),
                        it["kn"] // 128))
        B_t2.give(it["wt"], tk)
        A.w(tk, it["twt"])
        c0 = it["m"] * 256 + it["h"] * 64
        tk = A(a.activation(mixed[:, it["i"], c0:c0 + 64], b[:, 0:64], ACT.Copy, scale=stm[:, it["n"] % 16, 4:5]))
        it["done"] = tk
        PS.give(b, tk)

    for n in range(len(items) + 2):
        if n < len(items):
            a1(items[n])
        if 0 <= n - 1 < len(items):
            a2(items[n - 1])
        if 0 <= n - 2 < len(items):
            a3(items[n - 2])
    tk = A.last()
    for tt in range(NT):
        for m_ in range(4):
            tk = A(a.activation(QT[:, m_, 0:256], mixed[:, tt, m_ * 256:m_ * 256 + 256], ACT.Square, scale=1.0 / 16,
                                accum_out=ss2[:, tt, m_:m_ + 1]))
    V.w(tk)
    tk = V(v.tensor_scalar(ss2[:, :, 0:4], ss2[:, :, 0:4], 1e-6, None, ADD))
    G.w(tk)
    tk = G(g.tensor_tensor(rs2[:, :, 0:4], ss2[:, :, 0:4], mh2[:, :, 0:4], ALU.pow))
    V.w(tk)
    t_n2 = []
    for tt in range(NT):
        mv = mixed[:, tt, :].rearrange("p (m c) -> p m c", m=4)
        t_n2.append(V(v.tensor_tensor(mv, mv, rs2[:, tt, 0:4].unsqueeze(2).to_broadcast([128, 4, 256]), MUL)))
    fence()
    MT = sb("MT", [128, 8, S], stack=Arena(work0 + 16384, high))
    t_h = to_features(MT, mixed, t_n2, lambda k: col("group_out_g_2", k))
    T.w(t_h)
    tx = [None] * NT
    for half in range(2):
        w, wt, wi = take(8, 512)
        T.w(wt)
        for tt in range(NT):
            b = bank()
            tk = T(mm_group(b[:, :], lambda k: MT[:, k, tt * 128:tt * 128 + 128], lambda k: w[:, k, :], 8))
            V.w(tk)
            xv = X2[:, tt, half * 512:half * 512 + 512]
            tx[tt] = V(v.tensor_tensor(xv, xv, b[:, :], ADD))
            PS.give(b, tx[tt])
        release(wi, tk)
    fence()

    WN = Arena(work0 + 16384, high)
    N3 = sb("N3", [128, NT, D], stack=WN)
    H3 = sb("H3", [128, 8, S], stack=WN)
    UU = sb("UU", [128, 32, S], stack=Arena(region_a, region_a + 65536))
    tn = norm_to(N3, X2, tx)
    t_h = to_features(H3, N3, tn, lambda k: col("mlp_norm_g_2", k))
    T.w(t_h)
    t_u = []
    for c in range(8):
        w, wt, wi = take(8, 512)
        T.w(wt)
        for j in range(4):
            b = bank()
            f = c * 4 + j
            tk = T(mm_group(b[:, :], lambda k: w[:, k, j * 128:j * 128 + 128], lambda k: H3[:, k, :], 8))
            A.w(tk)
            tr = A(a.activation(UU[:, f, :], b[:, :], ACT.Relu))
            PS.give(b, tr)
            V.w(tr)
            t_u.append(V(v.tensor_tensor(UU[:, f, :], UU[:, f, :], UU[:, f, :], MUL)))
        release(wi, tk)
    acc8 = [bank() for _ in range(8)]
    tk8 = [None] * 8
    for c in range(8):
        w, wt, wi = take(4, 1024)
        T.w(wt, t_u[c * 4:c * 4 + 4])
        for i in range(8):
            tt, half = i // 2, i % 2
            m = mm_group(acc8[i][:, :], lambda k: UU[:, c * 4 + k, tt * 128:tt * 128 + 128],
                         lambda k: w[:, k, half * 512:half * 512 + 512], 4, start=c == 0, stop=c == 7)
            tk8[i] = T(m)
        release(wi, tk8[7])
    lo = Lane(sem("s_out"))
    ov = out.rearrange("a (n p) d -> p (a n) d", p=128)
    for i in range(8):
        tt, half = i // 2, i % 2
        xv = X2[:, tt, half * 512:half * 512 + 512]
        V.w(tk8[i])
        tk = V(v.tensor_tensor(xv, xv, acc8[i][:, :], ADD))
        SP.w(tk)
        t_out = lo(nc.sync.dma_start(ov[:, tt, half * 512:half * 512 + 512], xv))
    SP.w(t_out)


NAMES = ["x", "positions", "norm_mix_w", "w_in", "conv_w", "conv_b", "dt_bias", "a_log", "d_skip", "ssd_norm_w",
         "lambda_q1", "lambda_k1", "lambda_q2", "lambda_k2", "subln_w", "w_branch_attn", "w_branch_ssd", "w_out",
         "norm_ffn_w", "w_group_router", "b_group_router", "w_expert_router", "b_expert_router", "w_expert_gate",
         "w_expert_up", "w_expert_down", "final_norm_w", "attn_norm_g_2", "w_in_2", "moba_q_g_2", "moba_k_g_2",
         "mla_qlat_g_2", "mla_kvlat_g_2", "mla_w_uq_2", "mla_w_ukv_2", "mla_q_g_2", "mla_k_g_2", "dil_q_g_2",
         "dil_k_g_2", "swa_q_g_2", "swa_k_g_2", "swa_sinks_2", "group_out_g_2", "w_o_2", "mlp_norm_g_2", "w_up_2",
         "w_down_2"]


def kernel(**inputs):
    import concourse.bacc as bacc
    from concourse.bass_utils import run_bass_kernel_spmd

    nc = bacc.Bacc("TRN2", target_bir_lowering=False, num_devices=1)
    consts, biases = constants()
    arrays, t = {}, {}
    for name, value in [("consts", consts), ("biases", biases)] + [(n, inputs[n]) for n in NAMES]:
        value = np.ascontiguousarray(value)
        arrays["in_" + name] = value
        t[name] = nc.dram_tensor("in_" + name, value.shape, mybir.dt.from_np(value.dtype), kind="ExternalInput").ap()
    out = nc.dram_tensor("out_0", (1, S, D), F32, kind="ExternalOutput").ap()
    build(nc, t, out)
    result = run_bass_kernel_spmd(nc, [arrays], core_ids=[0])
    return result.results[0]["out_0"]
```

```python
from contextlib import ExitStack

import numpy as np
import concourse.bass as bass
from concourse import mybir

F32 = mybir.dt.float32
I32 = mybir.dt.int32
U32 = mybir.dt.uint32
ALU = mybir.AluOpType
ACT = mybir.ActivationFunctionType
AX = mybir.AxisListType
MUL, ADD, SUB, MAX, MIN = ALU.mult, ALU.add, ALU.subtract, ALU.max, ALU.min
EQ, GE, GT, LE = ALU.is_equal, ALU.is_ge, ALU.is_gt, ALU.is_le

S = 512
D = 1024
NT = 4
RING = 3
CAP = 64
NOV = 15
BIG = 1e30
TWO_PI = 6.283185307179586
MAGIC = 12582912.0

VECS = [
    ("norm_mix_w", 8), ("conv_b", 32), ("ssd_norm_w", 16), ("subln_w", 1), ("attn_norm_g_2", 8),
    ("group_out_g_2", 8), ("mlp_norm_g_2", 8), ("mla_qlat_g_2", 2), ("mla_kvlat_g_2", 1),
    ("moba_q_g_2", -1), ("moba_k_g_2", -1), ("dil_q_g_2", -1), ("dil_k_g_2", -1),
    ("swa_q_g_2", -1), ("swa_k_g_2", -1),
]


def vec_rows():
    at, n = {}, 0
    for name, rows in VECS:
        at[name] = n
        n += abs(rows)
    return at, n


CONSTS = [
    ("ident", 128), ("tri", 128), ("gt", 128), ("lt", 128), ("ones", 128), ("perm", 128),
    ("causal", 512), ("iota64", 64), ("iota128", 128), ("iota8m", 8), ("aid1", 8), ("ovid", 16), ("jcol", 1), ("iota64x2", 128),
    ("rcos", 64), ("rsin", 64), ("invf", 1), ("mhalf", 8),
]


def const_cols():
    at, n = {}, 0
    for name, cols in CONSTS:
        at[name] = (n, n + cols)
        n += cols
    return at, n


def constants():
    at, n = const_cols()
    c = np.zeros((128, n), np.float32)
    p = np.arange(128)

    def put(name, v):
        a, b = at[name]
        c[:, a:b] = np.broadcast_to(v, (128, b - a))

    put("ident", np.eye(128))
    put("tri", p[:, None] <= p[None, :])
    put("gt", p[:, None] > p[None, :])
    put("lt", p[:, None] < p[None, :])
    put("ones", 1.0)
    perm = np.zeros((128, 128))
    for m in range(128):
        if m % 64 < 32:
            perm[m + 32, m] = -1.0
        else:
            perm[m - 32, m] = 1.0
    put("perm", perm)
    dist = p[:, None] + 384 - np.arange(512)[None, :]
    put("causal", np.where(dist >= 0, 0.0, -BIG))
    put("iota64", np.arange(64))
    put("iota128", p)
    put("iota8m", np.arange(8) - 1000.0)
    aid = np.zeros((128, 8))
    for tt in range(4):
        for k in range(2):
            aid[:, tt * 2 + k] = k * 512 + tt * 128 + p + 1
    put("aid1", aid)
    put("ovid", np.arange(16))
    put("jcol", (p >= 64)[:, None])
    put("iota64x2", p % 64)
    inv2 = (1.0 / (np.float32(10000.0) ** (np.arange(0, 32, 2, dtype=np.float32) / np.float32(32)))).astype(np.float32)
    ang = np.arange(512, dtype=np.float32)[:, None] * inv2[None, :]
    put("rcos", np.cos(ang).astype(np.float32).reshape(4, 128, 16).transpose(1, 0, 2).reshape(128, 64))
    put("rsin", np.sin(ang).astype(np.float32).reshape(4, 128, 16).transpose(1, 0, 2).reshape(128, 64))
    inv1 = (1.0 / (np.float32(10000.0) ** (np.arange(0, 64, 2, dtype=np.float32) / np.float32(64)))).astype(np.float32)
    put("invf", inv1[p % 32][:, None])
    put("mhalf", -0.5)
    bias = np.zeros((12, 128, 512), np.float32)
    slopes = np.exp2(-8.0 * np.arange(1, 13, dtype=np.float32).reshape(4, 3) / 12).astype(np.float32)
    mult = (dist <= 128) * 1 + (dist % 4 == 0) * 1 + (dist % 16 == 0) * 1
    lnm = np.where((dist >= 0) & (mult > 0), np.log(np.maximum(mult, 1)), -BIG)
    swa = np.where((dist >= 0) & (dist < 128), 0.0, -BIG)
    cau = np.where(dist >= 0, 0.0, -BIG)
    for h in range(4):
        for m, extra in enumerate((cau, lnm, swa)):
            bias[m * 4 + h] = (-slopes[h, m] * dist.astype(np.float32)).astype(np.float64) + extra
    return c, bias


class Engine:

    def __init__(self, eng, sem, serial=True):
        self.eng, self.sem, self.n, self.seen, self.serial = eng, sem, 0, {}, serial

    def w(self, *toks):
        for t in toks:
            if t is None:
                continue
            if isinstance(t, list):
                self.w(*t)
                continue
            sem, v = t
            if self.seen.get(sem.num, 0) < v:
                self.eng.wait_ge(sem, v)
                self.seen[sem.num] = v

    def __call__(self, ins):
        ins.then_inc(self.sem, 1)
        self.n += 1
        if self.serial:
            self.w((self.sem, self.n))
        return (self.sem, self.n)

    def last(self):
        return (self.sem, self.n)


class Lane:

    def __init__(self, sem):
        self.sem, self.n = sem, 0

    def __call__(self, ins):
        ins.then_inc(self.sem, 16)
        self.n += 16
        return (self.sem, self.n)


class Pool:

    def __init__(self, aps):
        self.free = [(a, None) for a in aps]

    def take(self):
        return self.free.pop(0)

    def give(self, ap, *toks):
        self.free.append((ap, list(toks)))


class Arena:

    def __init__(self, start, end):
        self.at, self.end = (start + 63) // 64 * 64, end

    def take(self, shape):
        at = self.at
        self.at = at + (int(np.prod(shape[1:])) * 4 + 63) // 64 * 64
        assert self.at <= self.end, (shape, self.at, self.end)
        return at


def run(gen):
    for _ in gen:
        pass


def interleave(a, na, b, nb):
    ia = ib = 0
    live_a = live_b = True
    while live_a or live_b:
        first = live_a and (not live_b or ia * nb <= ib * na)
        try:
            next(a if first else b)
        except StopIteration:
            if first:
                live_a = False
            else:
                live_b = False
            continue
        if first:
            ia += 1
        else:
            ib += 1


def build(nc, t, out):
    sems = []

    def sem(name):
        s = nc.alloc_semaphore(name)
        sems.append(s)
        return s

    V = Engine(nc.vector, sem("s_dve"))
    A = Engine(nc.scalar, sem("s_act"))
    T = Engine(nc.tensor, sem("s_pe"), serial=False)
    G = Engine(nc.gpsimd, sem("s_pool"))
    SP = Engine(nc.sync, sem("s_sp"))
    v, a, g, pe = nc.vector, nc.scalar, nc.gpsimd, nc.tensor

    persist = ExitStack()
    low, high = nc.sbuf_base, nc.sbuf_usable_end
    PM = Arena(low, high)

    def sb(name, shape, dt=F32, stack=None):
        return nc.alloc_sbuf_tensor_at(name, shape, dt, offset=(stack or PM).take(shape))

    banks = [persist.enter_context(nc.psum_tensor(f"ps{i}", [128, 512], F32)) for i in range(8)]
    PS = Pool(banks)

    def bank():
        b, tok = PS.take()
        T.w(tok)
        return b

    def fence():
        now = [e.last() for e in (V, A, T, G)]
        for e in (V, A, T, G):
            e.w(now)

    cat, ncc = const_cols()
    C = sb("consts", [128, ncc])
    lane0 = Lane(sem("s_in"))
    lanex = Lane(sem("s_x"))
    laneb = Lane(sem("s_bcast"))

    def cc(name):
        x, y = cat[name]
        return C[:, x:y]

    ident = cc("ident")

    region_a = PM.at
    ssdT = sb("ssdT", [128, 16, S])
    both = ssdT[:, :, :].rearrange("p a b -> p (a b)")
    X = both[:, 0:4096].rearrange("p (a b) -> p a b", a=NT)
    XN = both[:, 4096:8192].rearrange("p (a b) -> p a b", a=NT)
    xsrc = t["x"].rearrange("a (n p) d -> p (a n) d", p=128)
    t_x = lanex(nc.sync.dma_start(X, xsrc))
    t_in = lane0(nc.scalar.dma_start(C[:, :], t["consts"]))
    rows_at, nrow = vec_rows()
    hT = sb("hT", [128, 8, S])
    attT = sb("attT", [128, 8, S])
    ring = [sb(f"ring{i}", [128, 4096]) for i in range(RING)]
    vcol = sb("vcol", [128, nrow + 128])
    sc = sb("sc", [128, 512])
    st = sb("st", [128, 256])
    ovn = sb("ovn", [128, 16], I32)
    work0 = PM.at
    WK = Arena(work0, high)
    cosT = sb("cosT", [128, S], stack=WK)
    sinT = sb("sinT", [128, S], stack=WK)
    small = Arena(WK.at, high)
    vrow = sb("vrow", [nrow, 128], stack=small)
    crow = sb("crow", [128, 128], stack=small)
    for name, n in VECS:
        r = rows_at[name]
        if n < 0:
            for half in range(2):
                t_in = lane0(nc.scalar.dma_start(vrow[r:r + 1, half * 64:half * 64 + 64], t[name]))
        else:
            src = t[name]
            if name == "group_out_g_2":
                src = src.rearrange("a b (r c) -> (a b r) c", c=128)
            else:
                src = src.rearrange("a (r c) -> (a r) c", c=128)
            t_in = lane0(nc.scalar.dma_start(vrow[r:r + n, :], src))
    t_in = lane0(nc.sync.dma_start(crow[:, :], t["conv_w"].rearrange("a k (r c) -> (a k r) c", c=128)))

    def col(name, i=0):
        return vcol[:, rows_at[name] + i:rows_at[name] + i + 1]

    def conv_col(k, i):
        return vcol[:, nrow + k * 32 + i:nrow + k * 32 + i + 1]

    sc_at = {}
    for name, n in (("dt_bias", 32), ("a_log", 32), ("d_skip", 32), ("lambda_q1", 64), ("lambda_k1", 64),
                    ("lambda_q2", 64), ("lambda_k2", 64), ("b_group_router", 8), ("b_expert_router", 64),
                    ("swa_sinks_2", 4)):
        o = sum(x[1] for x in sc_at.values())
        sc_at[name] = (o, n)
        t_bc = laneb(nc.gpsimd.dma_start(sc[:, o:o + n], t[name].to_broadcast([128, n])))

    def scv(name):
        o, n = sc_at[name]
        return sc[:, o:o + n]

    posi = sb("posi", [128, S], I32, stack=small)
    t_in = lane0(nc.sync.dma_start(posi[:, :], t["positions"].to_broadcast([128, S])))

    rlane = [Lane(sem(f"s_ring{i}")) for i in range(RING)]
    chunks = []

    def wview(name, c0, n):
        return t[name].rearrange("a (k p) n -> p (a k) n", p=128)[:, :, c0:c0 + n]

    for h in range(8):
        chunks.append([(0, 128, wview("w_in", h * 128, 128)), (128, 128, wview("w_in", 1024 + h * 128, 128)),
                       (256, 128, wview("w_in", 2048 + h * 128, 128)), (384, 0, None)])
    for gr in range(8):
        chunks.append([(0, 256, wview("w_in", 5120 + gr * 256, 256)),
                       (256, 128, wview("w_in", 7168 + gr * 128, 128)),
                       (384, 128, wview("w_in", 8192 + gr * 128, 128))])
        chunks.append([(0, 256, wview("w_in", 3072 + gr * 256, 256))])
    for half in range(2):
        o = half * 512
        chunks.append([(0, 512, wview("w_in", 9248 + o, 512))])
        chunks.append([(0, 512, wview("w_branch_attn", o, 512))])
        chunks.append([(0, 512, wview("w_in", 10272 + o, 512))])
        for kk in range(2):
            chunks.append([(0, 512, t["w_branch_ssd"].rearrange("a (k p) n -> p (a k) n", p=128)[:, kk * 8:kk * 8 + 8, o:o + 512])])
    for half in range(2):
        chunks.append([(0, 512, wview("w_out", half * 512, 512))])
    n_mix = len(chunks)

    def eview(name, e):
        return t[name][0, e].rearrange("(k p) n -> p k n", p=128)

    def moe_chunks(e):
        return ([(0, 512, eview("w_expert_gate", e))], [(0, 512, eview("w_expert_up", e))],
                [(0, 1024, eview("w_expert_down", e))])

    for e in range(65):
        if e < 64:
            chunks += moe_chunks(e)[0:2]
        if e > 0:
            chunks.append(moe_chunks(e - 1)[2])
    n_moe_end = len(chunks)
    for c0 in range(0, 2464, 512):
        n = min(512, 2464 - c0)
        chunks.append([(0, n, wview("w_in_2", c0, n))])
    for half in range(2):
        chunks.append([(0, 512, wview("w_o_2", half * 512, 512))])
    for c0 in range(8):
        chunks.append([(0, 512, wview("w_up_2", c0 * 512, 512))])
    for kk in range(8):
        chunks.append([(0, 1024, t["w_down_2"].rearrange("a (k p) n -> p (a k) n", p=128)[:, kk * 4:kk * 4 + 4, :])])

    state = {"issued": 0, "taken": 0}
    slot_tok = {}
    slot_of = {}
    slots = [(i, None) for i in range(RING)]

    def issue():
        i = state["issued"]
        if i >= len(chunks) or not slots:
            return
        r, free = slots.pop(0)
        slot_of[i] = r
        SP.w(free)
        width = sum(x[1] for x in chunks[i])
        width = 512 if len(chunks[i]) == 4 else width
        for c0, n, src in chunks[i]:
            if n:
                k = src.shape[1]
                dst = ring[r][:, 0:k * width].rearrange("p (k n) -> p k n", k=k)[:, :, c0:c0 + n]
                slot_tok[i] = rlane[r](nc.sync.dma_start(dst, src))
        state["issued"] = i + 1

    def take(k, n):
        i = state["taken"]
        state["taken"] = i + 1
        return ring[slot_of[i]][:, 0:k * n].rearrange("p (k n) -> p k n", k=k), slot_tok[i], i

    def release(i, *toks):
        if slot_of[i] < RING or state["issued"] < n_moe_end:
            slots.append((slot_of[i], list(toks)))
        issue()

    for _ in range(RING):
        issue()

    t_in = [t_in, t_bc]
    T.w(t_in)
    b = bank()
    pe.transpose(b[:, 0:nrow], vrow[:, :], ident[0:nrow, 0:nrow])
    tk = T(pe.transpose(b[:, nrow:nrow + 128], crow[:, :], ident))
    V.w(tk, t_in)
    t_col = V(v.tensor_copy(vcol[:, :], b[:, 0:nrow + 128]))
    PS.give(b, t_col)
    t_col = V(v.tensor_scalar(col("subln_w"), col("subln_w"), 0.8, None, MUL))
    for name in ("moba_q_g_2", "dil_q_g_2", "swa_q_g_2"):
        t_col = V(v.tensor_scalar(col(name), col(name), 0.125, None, MUL))
    A.w(t_in, t_col)
    G.w(t_in)

    mhalf = cc("mhalf")

    lamj = sb("lamj", [128, 64], stack=small)
    V(v.tensor_tensor_reduce(lamj[:, :], scv("lambda_q1"), scv("lambda_k1"), 1.0, 0.0, MUL, ADD, st[:, 0:1]))
    tk = V(v.tensor_tensor_reduce(lamj[:, :], scv("lambda_q2"), scv("lambda_k2"), 1.0, 0.0, MUL, ADD, st[:, 1:2]))
    A.w(tk)
    tk = A(a.activation(st[:, 2:4], st[:, 0:2], ACT.Exp))
    V.w(tk)
    V(v.tensor_tensor(st[:, 4:5], st[:, 3:4], st[:, 2:3], SUB))
    t_lam = V(v.tensor_scalar(st[:, 4:5], st[:, 4:5], 0.8 - 0.6, None, SUB))
    nlam = st[:, 4:5]

    ang = sb("ang", [128, S], stack=small)
    rn = sb("rn", [128, S], stack=small)
    V(v.tensor_copy(ang[:, :], posi[:, :]))
    V(v.tensor_scalar(ang[:, :], ang[:, :], cc("invf"), None, MUL))
    C1 = 6.28125
    C2 = float(np.float32(TWO_PI - C1))
    for dst, sh, off in ((sinT, 0.0, 0.0), (cosT, 0.25, TWO_PI / 4)):
        V(v.tensor_scalar(rn[:, :], ang[:, :], 1.0 / TWO_PI, sh, MUL, ADD))
        V(v.tensor_scalar(rn[:, :], rn[:, :], MAGIC, None, ADD))
        V(v.tensor_scalar(rn[:, :], rn[:, :], MAGIC, None, SUB))
        V(v.scalar_tensor_tensor(dst[:, :], rn[:, :], -C1, ang[:, :], MUL, ADD))
        V(v.scalar_tensor_tensor(dst[:, :], rn[:, :], -C2, dst[:, :], MUL, ADD))
        V(v.tensor_scalar(dst[:, :], dst[:, :], off, 3.1415925, ADD, MIN))
        tk = V(v.tensor_scalar(dst[:, :], dst[:, :], -3.1415925, None, MAX))
        A.w(tk)
        t_rot = A(a.activation(dst[:, :], dst[:, :], ACT.Sin))
    state_w = {"flip": 0}

    def evac(dst, src, scale=None, after=None):
        state_w["flip"] ^= 1
        if state_w["flip"]:
            V.w(after)
            if scale is None:
                return V(v.tensor_copy(dst, src))
            return V(v.tensor_scalar(dst, src, scale, None, MUL))
        A.w(after)
        if scale is None:
            return A(a.copy(dst, src))
        return A(a.activation(dst, src, ACT.Copy, scale=scale))

    def rstd(dst, ss, eps, tok):
        G.w(tok)
        G(g.tensor_scalar(ss, ss, eps, None, ADD))
        return G(g.tensor_tensor(dst, ss, mhalf[:, 0:ss.shape[1]], ALU.pow))

    def norm_to(dst, src, deps, eps=1e-6, free=None):
        toks = []
        A.w(free)
        for tt in range(NT):
            A.w(deps[tt])
            toks.append(A(a.activation(dst[:, tt, :], src[:, tt, :], ACT.Square, scale=1.0 / 32,
                                       accum_out=st[:, 8 + tt:9 + tt])))
        tk = rstd(st[:, 12:16], st[:, 8:12], eps, toks[-1])
        V.w(tk)
        return [V(v.tensor_scalar(dst[:, tt, :], src[:, tt, :], st[:, 12 + tt:13 + tt], None, MUL))
                for tt in range(NT)]

    def to_features(dst, src, toks, scol, free=None):
        outs = []
        for k in range(8):
            b = bank()
            for tt in range(NT):
                T.w(toks[tt])
                m = pe.transpose(b[:, tt * 128:tt * 128 + 128], src[:, tt, k * 128:k * 128 + 128], ident)
            tk = T(m)
            if free is not None:
                V.w(free)
                A.w(free)
            tk = evac(dst[:, k, :], b[:, :], None if scol is None else scol(k), after=tk)
            PS.give(b, tk)
            outs.append(tk)
        return outs

    def mm_group(o, lhs, rhs, n, start=True, stop=True):
        for k in range(n):
            m = pe.matmul(o, lhs(k), rhs(k), start=start and k == 0, stop=stop and k == n - 1)
        return m

    tn = norm_to(XN, X, [t_x] * NT)
    t_h = to_features(hT, XN, tn, lambda k: col("norm_mix_w", k))
    T.w(t_h, t_rot, t_lam)
    fence()
    V.w(t_rot)


    def bufs(name, n, shape, stack):
        return Pool([sb(f"{name}{i}", shape, stack=stack) for i in range(n)])

    B_raw = bufs("raw", 2, [128, S], WK)
    B_q = bufs("bq", 2, [128, S], WK)
    B_k = bufs("bk", 2, [128, S], WK)
    B_v = bufs("bv", 3, [128, NT, 128], WK)
    B_s = bufs("bs", 3, [128, 2, S], WK)
    B_w = bufs("bw", 2, [128, S], WK)
    B_wt = bufs("bwt", 2, [128, S], WK)
    B_st = bufs("bst", 6, [128, 16], WK)
    B_at = bufs("bat", 3, [128, NT, 128], WK)
    heads = {}

    def dense_head(h):
        w, wt, wi = take(8, 512)
        T.w(wt)
        raws = []
        for j in range(2):
            b = bank()
            for k in range(8):
                m = pe.matmul(b[:, :], w[:, k, j * 128:j * 128 + 128], hT[:, k, :], start=k == 0, stop=k == 7)
                if k == 3:
                    yield
            tk = T(m)
            raw, rt = B_raw.take()
            A.w(rt, tk)
            tk = A(a.copy(raw[:, :], b[:, :]))
            PS.give(b, tk)
            raws.append((raw, tk))
            yield
        outs = []
        bv = bank()
        for j, B in ((0, B_q), (1, B_k)):
            raw, tk = raws[j]
            b = bank()
            T.w(tk)
            tp = T(pe.matmul(b[:, :], cc("perm"), raw[:, :], start=True, stop=True))
            dst, dtk = B.take()
            V.w(dtk, tk)
            V(v.tensor_tensor(dst[:, :], raw[:, :], cosT[:, :], MUL))
            V.w(tp)
            t2 = V(v.tensor_tensor(raw[:, :], b[:, :], sinT[:, :], MUL))
            PS.give(b, t2)
            t3 = V(v.tensor_tensor(dst[:, :], dst[:, :], raw[:, :], ADD))
            B_raw.give(raw, t3)
            outs.append((dst, t3))
            for tt in (2 * j, 2 * j + 1):
                tv = T(mm_group(bv[:, tt * 128:tt * 128 + 128], lambda k: hT[:, k, tt * 128:tt * 128 + 128],
                                lambda k: w[:, k, 256:384], 8))
            if j == 0:
                yield
        release(wi, tv)
        vv, vt = B_v.take()
        A.w(vt, tv)
        tk = A(a.copy(vv[:, :, :].rearrange("p a b -> p (a b)"), bv[:, :]))
        PS.give(bv, tk)
        outs.append((vv, tk))
        heads[h] = outs
        yield

    items = [{"h": n // 4, "i": n % 4} for n in range(32)]
    t_att = [None] * 8

    def scores(it):
        h, i = it["h"], it["i"]
        (q, tq), (k_, tk_), _ = heads[h]
        kn = (i + 1) * 128
        s, stk = B_s.take()
        sm, smk = B_st.take()
        T.w(tq, tk_)
        for c in range(2):
            b = bank()
            r = slice(c * 64, c * 64 + 64)
            tk = T(pe.matmul(b[:, 0:kn], q[r, i * 128:i * 128 + 128], k_[r, 0:kn], start=True, stop=True))
            V.w(stk, smk, tk)
            tv = V(v.tensor_tensor_reduce(s[:, c, 0:kn], b[:, 0:kn], cc("causal")[:, 384 - 128 * i:512],
                                          1.0, -3e38, ADD, MAX, sm[:, c:c + 1]))
            PS.give(b, tv)
        if i == 3:
            B_q.give(q, tk)
            B_k.give(k_, tk)
        tv = V(v.tensor_scalar(sm[:, 2:4], sm[:, 0:2], -0.125, None, MUL))
        A.w(tv)
        for c in range(2):
            tk = A(a.activation(s[:, c, 0:kn], s[:, c, 0:kn], ACT.Exp, scale=0.125, bias=sm[:, 2 + c:3 + c],
                                accum_out=sm[:, 4 + c:5 + c]))
        it["s"], it["sm"], it["ts"], it["kn"] = s, sm, tk, kn

    def weights(it):
        s, sm, kn = it["s"], it["sm"], it["kn"]
        W, Wt = B_w.take()
        V.w(it["ts"], Wt)
        V(v.reciprocal(sm[:, 6:8], sm[:, 4:6]))
        V(v.tensor_scalar(sm[:, 8:9], sm[:, 7:8], nlam, None, MUL))
        V(v.tensor_scalar(W[:, 0:kn], s[:, 0, 0:kn], sm[:, 6:7], None, MUL))
        tk = V(v.scalar_tensor_tensor(W[:, 0:kn], s[:, 1, 0:kn], sm[:, 8:9], W[:, 0:kn], MUL, ADD))
        B_s.give(s, tk)
        it["W"], it["tW"] = W, tk

    def weights_turned(it):
        b = bank()
        T.w(it["tW"])
        for j in range(it["i"] + 1):
            m = pe.transpose(b[:, j * 128:j * 128 + 128], it["W"][:, j * 128:j * 128 + 128], ident)
        tk = T(m)
        B_w.give(it["W"], tk)
        wt, wtt = B_wt.take()
        A.w(wtt, tk)
        tk = A(a.copy(wt[:, 0:it["kn"]], b[:, 0:it["kn"]]))
        PS.give(b, tk)
        it["wt"], it["twt"] = wt, tk

    at_of = {}

    def values(it):
        sm, h, i = it["sm"], it["h"], it["i"]
        vv, tv = heads[h][2]
        if i == 0:
            at_of[h] = B_at.take()
        at, att_ = at_of[h]
        b = bank()
        T.w(it["twt"], tv)
        tk = T(mm_group(b[:, 0:128], lambda j: it["wt"][:, j * 128:j * 128 + 128], lambda j: vv[:, j, :], i + 1))
        B_wt.give(it["wt"], tk)
        if i == 3:
            B_v.give(vv, tk)
        A.w(tk, att_)
        tk = A(a.activation(at[:, i, :], b[:, 0:128], ACT.Square, scale=128.0 ** -0.5, accum_out=sm[:, 10:11]))
        it["tr"] = rstd(sm[:, 11:12], sm[:, 10:11], 1e-5, tk)
        it["b"] = b

    def scaled(it):
        at, att_ = at_of[it["h"]]
        V.w(it["tr"])
        tk = V(v.tensor_scalar(at[:, it["i"], :], it["b"][:, 0:128], it["sm"][:, 11:12], None, MUL))
        PS.give(it["b"], tk)
        B_st.give(it["sm"], tk)
        it["ta"] = tk

    def head_turned(h):
        at, att_ = at_of[h]
        b = bank()
        for i in range(4):
            T.w(items[h * 4 + i]["ta"])
            m = pe.transpose(b[:, i * 128:i * 128 + 128], at[:, i, :], ident)
        tk = T(m)
        B_at.give(at, tk)
        t_att[h] = evac(attT[:, h, :], b[:, :], col("subln_w"), after=tk)
        PS.give(b, t_att[h])

    def attention(n0, n1):
        for n in range(n0, n1):
            for lag, f in ((2, weights_turned), (3, values), (0, scores), (1, weights), (4, scaled)):
                if 0 <= n - lag < 32:
                    f(items[n - lag])
            if n - 5 >= 0 and (n - 5) % 4 == 3:
                head_turned((n - 5) // 4)
            yield

    run(dense_head(0))

    def dense_heads():
        for h in range(1, 8):
            yield from dense_head(h)

    interleave(dense_heads(), 42, attention(0, 28), 28)

    WT = Arena(WK.at, high)
    WS = Arena(work0, WK.at)
    wdt = sb("wdt", [128, 8, 32], stack=WT)
    dt_, da, sp1, sp2, sp3 = (sb(f"dt{i}", [128, NT, 32], stack=WT) for i in range(5))
    aexp = sb("aexp", [128, 32], stack=WT)
    ecum, etail, etot = (sb(f"ec{i}", [128, NT, 32], stack=WT) for i in range(3))
    U = [sb(f"u{i}", [128, 520], stack=WT) for i in range(2)]
    B_acc = bufs("acc", 2, [128, S], WT)

    def pair(name, shape):
        return Pool([sb(name + "0", shape, stack=WT), sb(name + "1", shape, stack=WS)])

    B_x = pair("xs", [128, NT, 256])
    B_BT = pair("BT", [128, S])
    B_CT = pair("CT", [128, S])
    B_Bk = pair("Bk", [128, NT, 128])
    B_z = pair("zs", [128, NT, 256])
    B_R = bufs("R", 2, [128, 4, 128], WS)
    B_E = bufs("E", 2, [128, 4, 128], WS)
    B_cb = bufs("cbm", 2, [128, 128], WS)
    B_xd = bufs("xd", 2, [128, 3, 256], WS)
    B_y = bufs("yy", 2, [128, 2, 256], WS)
    B_yn = bufs("yn", 2, [128, NT, 256], WS)
    B_sta = bufs("sta", 3, [128, 256], WS)
    B_st2 = bufs("st2", 4, [128, 4], WS)

    wl = Lane(sem("s_wdt"))
    t_wdt = wl(nc.gpsimd.dma_start(wdt[:, :, :], wview("w_in", 9216, 32)))
    for u in U:
        t_u0 = V(v.memset(u[:, 0:4], 0.0))
    B_u = Pool(U)

    def setup_ssd():
        b = bank()
        T.w(t_wdt)
        for tt in range(NT):
            tk = T(mm_group(b[:, tt * 32:tt * 32 + 32], lambda k: hT[:, k, tt * 128:tt * 128 + 128],
                            lambda k: wdt[:, k, :], 8))
        V.w(tk)
        bc = lambda x: x.unsqueeze(1).to_broadcast([128, NT, 32])
        tk = V(v.tensor_tensor(sp1[:, :, :], b[:, 0:128].rearrange("p (a b) -> p a b", a=NT), bc(scv("dt_bias")), ADD))
        PS.give(b, tk)
        V(v.tensor_scalar(sp2[:, :, :], sp1[:, :, :], -1.0, None, MUL))
        tk = V(v.tensor_tensor(sp2[:, :, :], sp1[:, :, :], sp2[:, :, :], MIN))
        A.w(tk)
        tk = A(a.activation(sp2[:, :, :], sp2[:, :, :], ACT.Exp))
        tk2 = A(a.activation(aexp[:, :], scv("a_log"), ACT.Exp))
        V.w(tk, tk2)
        V(v.tensor_scalar(sp3[:, :, :], sp2[:, :, :], 2.0, None, ADD))
        V(v.reciprocal(sp3[:, :, :], sp3[:, :, :]))
        V(v.tensor_tensor(sp2[:, :, :], sp2[:, :, :], sp3[:, :, :], MUL))
        V(v.tensor_tensor(sp3[:, :, :], sp2[:, :, :], sp2[:, :, :], MUL))
        V(v.tensor_scalar(dt_[:, :, :], sp3[:, :, :], 2.0 / 17, 2.0 / 15, MUL, ADD))
        for c in (13, 11, 9, 7, 5, 3, 1):
            V(v.tensor_tensor(dt_[:, :, :], dt_[:, :, :], sp3[:, :, :], MUL))
            V(v.tensor_scalar(dt_[:, :, :], dt_[:, :, :], 2.0 / c, None, ADD))
        V(v.tensor_tensor(dt_[:, :, :], dt_[:, :, :], sp2[:, :, :], MUL))
        V(v.scalar_tensor_tensor(dt_[:, :, :], sp1[:, :, :], 0.0, dt_[:, :, :], MAX, ADD))
        tk = V(v.scalar_tensor_tensor(da[:, :, :], dt_[:, :, :], -1.0, bc(aexp[:, :]), MUL, MUL))
        G.w(tk)
        T.w(tk)
        yield
        b = bank()
        daf = da[:, :, :].rearrange("p a b -> p (a b)")
        pe.matmul(b[:, 0:128], cc("tri"), daf, start=True, stop=True)
        pe.matmul(b[:, 128:256], cc("gt"), daf, start=True, stop=True)
        tk = T(pe.matmul(b[:, 256:384], cc("ones"), daf, start=True, stop=True))
        A.w(tk)
        for i, dst in enumerate((ecum, etail, etot)):
            tk = A(a.activation(dst[:, :, :].rearrange("p a b -> p (a b)"), b[:, i * 128:i * 128 + 128], ACT.Exp))
        PS.give(b, tk)
        V.w(tk)
        G.w(tk)
        yield

    groups = {}

    def dense_group(gr):
        w, wt, wi = take(8, 512)
        T.w(wt)
        xs, xt = B_x.take()
        BT, BTt = B_BT.take()
        CT, CTt = B_CT.take()
        Bk, Bkt = B_Bk.take()
        zs, zt = B_z.take()
        pend = None

        def turn(p):
            src, tk, j = p
            b = bank()
            T.w(tk)
            for tt in range(NT):
                m = pe.transpose(b[:, tt * 128:tt * 128 + 128], src[:, tt * 128:tt * 128 + 128], ident)
            tk = T(m)
            if j < 2:
                B_acc.give(src, tk)
                A.w(tk, xt)
                tk = A(a.copy(xs[:, :, j * 128:j * 128 + 128], b[:, :].rearrange("p (a b) -> p a b", a=NT)))
            else:
                A.w(tk, Bkt)
                tk = A(a.copy(Bk[:, :, :], b[:, :].rearrange("p (a b) -> p a b", a=NT)))
            PS.give(b, tk)
            return tk

        rec = {}
        for j in range(4):
            ch = (gr * 2, gr * 2 + 1, 16 + gr, 24 + gr)[j]
            b = bank()
            for k in range(8):
                m = pe.matmul(b[:, :], w[:, k, j * 128:j * 128 + 128], hT[:, k, :], start=k == 0, stop=k == 7)
                if k == 3:
                    yield
            tk = T(m)
            if j == 3:
                release(wi, tk)
            u, ut = B_u.take()
            A.w(ut, tk, t_u0)
            tk = A(a.copy(u[:, 4:516], b[:, :]))
            PS.give(b, tk)
            if j < 2:
                acc, at_ = B_acc.take()
            else:
                acc, at_ = (BT, BTt) if j == 2 else (CT, CTt)
            V.w(tk, at_)
            V(v.tensor_scalar(acc[:, :], u[:, 4:516], conv_col(3, ch), col("conv_b", ch), MUL, ADD))
            for kk in (2, 1, 0):
                tk = V(v.scalar_tensor_tensor(acc[:, :], u[:, 1 + kk:513 + kk], conv_col(kk, ch), acc[:, :], MUL, ADD))
            B_u.give(u, tk)
            A.w(tk)
            tk = A(a.activation(acc[:, :], acc[:, :], ACT.Silu))
            if j == 2:
                rec["BT"] = tk
            if j == 3:
                rec["CT"] = tk
            if pend is not None:
                rec[pend[2]] = turn(pend)
            pend = (acc, tk, j) if j < 3 else None
            yield
        w, wt, wi = take(8, 256)
        T.w(wt)
        for hb in range(2):
            b = bank()
            for q in range(2):
                tt = hb * 2 + q
                m = mm_group(b[:, q * 256:q * 256 + 256], lambda k: hT[:, k, tt * 128:tt * 128 + 128],
                             lambda k: w[:, k, :], 8)
                tk = T(m)
                yield
            A.w(tk, zt)
            tz = A(a.activation(zs[:, hb * 2:hb * 2 + 2, :].rearrange("p a b -> p (a b)"), b[:, :], ACT.Silu))
            PS.give(b, tz)
        release(wi, tk)
        rec["z"] = tz
        groups[gr] = (xs, BT, CT, Bk, zs, rec)

    def scan_group(gr):
        xs, BT, CT, Bk, zs, rec = groups[gr]
        yn, ynt = B_yn.take()
        its = [dict() for _ in range(4)]
        cur = {"s": None, "t": None}
        hs = slice(gr * 4, gr * 4 + 4)
        used = []

        def bc(x, n=64):
            return x.unsqueeze(2).to_broadcast([128, 4, n])

        def v4(x):
            return x.rearrange("p (r q) -> p r q", r=4)

        def ready(c):
            it = its[c]
            R, Rt = B_R.take()
            V.w(Rt)
            it["tR"] = V(v.tensor_tensor(R[:, :, :], cc("tri").unsqueeze(1).to_broadcast([128, 4, 128]),
                                         bc(da[:, c, hs], 128), MUL))
            it["R"] = R

        def inputs(c):
            it = its[c]
            xd, xdt = B_xd.take()
            G.w(xdt, rec[0], rec[1])
            G(g.tensor_tensor(v4(xd[:, 0, :]), v4(xs[:, c, :]), bc(dt_[:, c, hs]), MUL))
            G(g.tensor_tensor(v4(xd[:, 2, :]), v4(xs[:, c, :]), bc(scv("d_skip")[:, hs]), MUL))
            it["txd"] = G(g.tensor_tensor(v4(xd[:, 1, :]), v4(xd[:, 0, :]), bc(etail[:, c, hs]), MUL))
            it["xd"] = xd

        def decays(c):
            it = its[c]
            b = bank()
            T.w(rec["BT"], rec["CT"])
            ck = slice(c * 128, c * 128 + 128)
            tb = T(pe.matmul(b[:, 0:128], BT[:, ck], CT[:, ck], start=True, stop=True))
            b2 = bank()
            T.w(it["tR"])
            ts = T(pe.matmul(b2[:, :], cc("gt"), it["R"][:, :, :].rearrange("p a b -> p (a b)"), start=True, stop=True))
            B_R.give(it["R"], ts)
            cb, cbt = B_cb.take()
            V.w(cbt, tb)
            tc = V(v.tensor_tensor(cb[:, :], b[:, 0:128], cc("tri"), MUL))
            PS.give(b, tc)
            E, Et = B_E.take()
            A.w(Et, ts)
            it["te"] = A(a.activation(E[:, :, :].rearrange("p a b -> p (a b)"), b2[:, :], ACT.Exp))
            PS.give(b2, it["te"])
            it["E"], it["cb"], it["tc"] = E, cb, tc

        def mixing(c):
            it = its[c]
            E, cb = it["E"], it["cb"]
            V.w(it["te"], it["tc"])
            it["tm"] = V(v.tensor_tensor(E[:, :, :], E[:, :, :], cb[:, :].unsqueeze(1).to_broadcast([128, 4, 128]), MUL))
            B_cb.give(cb, it["tm"])

        def outputs(c):
            it = its[c]
            E, xd = it["E"], it["xd"]
            b = bank()
            ck = slice(c * 128, c * 128 + 128)
            if c > 0:
                T.w(cur["t"])
                pe.matmul(b[:, 256:512], CT[:, ck], cur["s"][:, :], start=True, stop=True)
            T.w(it["tm"], it["txd"])
            for r in range(4):
                m = pe.matmul(b[:, r * 64:r * 64 + 64], E[:, r, :], xd[:, 0, r * 64:r * 64 + 64], start=True, stop=True)
            ty = T(m)
            B_E.give(E, ty)
            if c < 3:
                b2 = bank()
                T.w(rec[2])
                ts = T(pe.matmul(b2[:, 0:256], Bk[:, c, :], xd[:, 1, :], start=True, stop=True))
                used.append(ts)
                new, nt = B_sta.take()
                V.w(nt, ts)
                if c == 0:
                    tk = V(v.tensor_copy(new[:, :], b2[:, 0:256]))
                else:
                    V.w(cur["t"])
                    V(v.tensor_tensor(v4(new[:, :]), v4(cur["s"][:, :]), bc(etot[:, c, hs]), MUL))
                    tk = V(v.tensor_tensor(new[:, :], new[:, :], b2[:, 0:256], ADD))
                PS.give(b2, tk)
                if c > 0:
                    B_sta.give(cur["s"], tk, ty)
                cur["s"], cur["t"] = new, tk
            else:
                B_sta.give(cur["s"], ty)
            used.append(ty)
            y, yt = B_y.take()
            V.w(yt, ty, it["txd"])
            V(v.tensor_tensor(y[:, 0, :], b[:, 0:256], xd[:, 2, :], ADD))
            if c > 0:
                V(v.tensor_tensor(v4(y[:, 1, :]), v4(b[:, 256:512]), bc(ecum[:, c, hs]), MUL))
                V(v.tensor_tensor(y[:, 0, :], y[:, 0, :], y[:, 1, :], ADD))
            PS.give(b, V.last())
            B_xd.give(xd, V.last(), ty, it["txd"])
            V.w(rec["z"])
            tk = V(v.tensor_tensor(y[:, 0, :], y[:, 0, :], zs[:, c, :], MUL))
            sm, smt = B_st2.take()
            A.w(tk, smt)
            tk = A(a.activation(y[:, 1, :], y[:, 0, :], ACT.Square, scale=1.0 / 16, accum_out=sm[:, 0:1]))
            it["tr"] = rstd(sm[:, 1:2], sm[:, 0:1], 1e-5, tk)
            it["y"], it["sm"] = y, sm

        def normed(c):
            it = its[c]
            V.w(it["tr"], ynt)
            tk = V(v.tensor_scalar(yn[:, c, :], it["y"][:, 0, :], it["sm"][:, 1:2], None, MUL))
            B_y.give(it["y"], tk)
            B_st2.give(it["sm"], tk)
            it["ty"] = tk

        for n in range(8):
            for lag, f in ((3, outputs), (1, decays), (1, inputs), (0, ready), (2, mixing), (4, normed)):
                if 0 <= n - lag < 4:
                    f(n - lag)
            yield
        B_x.give(xs, its[3]["txd"])
        B_BT.give(BT, used[-1])
        B_CT.give(CT, used[-1])
        B_Bk.give(Bk, used[-1])
        B_z.give(zs, its[3]["ty"])
        for j in range(2):
            b = bank()
            for c in range(4):
                T.w(its[c]["ty"])
                m = pe.transpose(b[:, c * 128:c * 128 + 128], yn[:, c, j * 128:j * 128 + 128], ident)
            tk = T(m)
            if j == 1:
                B_yn.give(yn, tk)
            tk = evac(ssdT[:, gr * 2 + j, :], b[:, :], col("ssd_norm_w", gr * 2 + j), after=tk)
            PS.give(b, tk)
        yield

    def first():
        yield from setup_ssd()
        yield from dense_group(0)

    interleave(first(), 14, attention(28, 37), 9)
    fence()
    for gr in range(7):
        interleave(dense_group(gr + 1), 12, scan_group(gr), 9)
    run(scan_group(7))
    fence()

    WM = Arena(work0, high)
    X2 = sb("X2", [128, NT, D], stack=WM)
    sga = sb("sga", [128, 4, S], stack=WM)
    B_m2 = bufs("m2", 2, [128, S], WM)
    mT = sb("mT", [128, 8, S], stack=WM)
    lx = Lane(sem("s_x2"))
    t_x2 = lx(nc.gpsimd.dma_start(X2[:, :, :], t["x"].rearrange("a (n p) d -> p (a n) d", p=128)))
    tm_ = [None] * 8

    def gate_part(half, kind):
        w, wt, wi = take(8, 512)
        T.w(wt)
        rt = None
        for j in range(4):
            b = bank()
            tk = T(mm_group(b[:, :], lambda k: w[:, k, j * 128:j * 128 + 128], lambda k: hT[:, k, :], 8))
            A.w(tk, sg_free[j])
            sg_tok[j] = A(a.activation(sga[:, j, :], b[:, :], ACT.Sigmoid))
            PS.give(b, sg_tok[j])
            yield
        release(wi, tk)

    sg_free = [None] * 4
    sg_tok = [None] * 4

    def attn_part(half):
        w, wt, wi = take(8, 512)
        T.w(wt)
        for j in range(4):
            b = bank()
            tk = T(mm_group(b[:, :], lambda k: w[:, k, j * 128:j * 128 + 128], lambda k: attT[:, k, :], 8))
            f = half * 4 + j
            V.w(tk, sg_tok[j])
            tm_[f] = V(v.tensor_tensor(mT[:, f, :], b[:, :], sga[:, j, :], MUL))
            sg_free[j] = tm_[f]
            PS.give(b, tm_[f])
            yield
        release(wi, tk)

    def ssd_part(half):
        w0, wt0, wi0 = take(8, 512)
        w1, wt1, wi1 = take(8, 512)
        T.w(wt0, wt1)
        for j in range(4):
            b = bank()
            js = slice(j * 128, j * 128 + 128)
            mm_group(b[:, :], lambda k: w0[:, k, js], lambda k: ssdT[:, k, :], 8, stop=False)
            tk = T(mm_group(b[:, :], lambda k: w1[:, k, js], lambda k: ssdT[:, 8 + k, :], 8, start=False))
            f = half * 4 + j
            m2, mt = B_m2.take()
            V.w(tk, sg_tok[j], mt)
            t1 = V(v.tensor_tensor(m2[:, :], b[:, :], sga[:, j, :], MUL))
            sg_free[j] = t1
            PS.give(b, t1)
            tm_[f] = V(v.tensor_tensor(mT[:, f, :], mT[:, f, :], m2[:, :], ADD))
            B_m2.give(m2, tm_[f])
            yield
        release(wi0, tk)
        release(wi1, tk)

    T.w(t_att)

    for gen in (gate_part(0, 0), attn_part(0), gate_part(0, 1), ssd_part(0)):
        run(gen)
    for gen in (gate_part(1, 0), attn_part(1), gate_part(1, 1), ssd_part(1)):
        run(gen)
    T.w(tm_)
    tx = [None] * NT
    for half in range(2):
        w, wt, wi = take(8, 512)
        T.w(wt)
        for tt in range(NT):
            b = bank()
            tk = T(mm_group(b[:, :], lambda k: mT[:, k, tt * 128:tt * 128 + 128], lambda k: w[:, k, :], 8))
            V.w(tk, t_x2)
            xv = X2[:, tt, half * 512:half * 512 + 512]
            tx[tt] = V(v.tensor_tensor(xv, xv, b[:, :], ADD))
            PS.give(b, tx[tt])
        release(wi, tk)
    fence()

    RA = Arena(region_a, region_a + 65536)
    WR = Arena(work0 + 16384, high)
    for i in range(4):
        ring.append(sb(f"ringx{i}", [128, 4096], stack=RA))
        rlane.append(Lane(sem(f"s_ringx{i}")))
        slots.append((RING + i, None))
        SP.w(V.last(), A.last(), T.last(), G.last())
        issue()
    EB = 64 + NOV
    sidx = sb("sidx", [128, EB], I32, stack=WR)
    gidx = sb("gidx", [128, EB], I32, stack=WR)
    wts = sb("wts", [128, NT, 2], stack=WR)
    work1 = WR.at
    H2 = sb("H2", [128, NT, D], stack=WR)
    H2T = sb("H2T", [128, 8, S], stack=WR)
    wrt = sb("wrt", [128, 8, 72], stack=WR)
    frow = sb("frow", [128, D], stack=WR)
    L = sb("L", [128, NT, 72], stack=WR)
    ra = sb("ra", [128, NT, 64], stack=WR)
    rb = sb("rb", [128, NT, 64], stack=WR)
    O = [sb(f"O{k}", [128, NT, 64], stack=WR) for k in range(2)]
    AS = sb("AS", [128, NT, 64], stack=WR)
    s8 = sb("s8", [128, 12, NT, 8], stack=WR)
    s4 = sb("s4", [128, 16, NT], stack=WR)
    e64 = sb("e64", [128, 6, 64], stack=WR)
    oR = sb("oR", [128, 2, 128], stack=WR)
    oB = sb("oB", [128, 2, EB], stack=WR)
    lw = Lane(sem("s_rt"))
    t_rt = lw(nc.gpsimd.dma_start(wrt[:, :, 0:8], wview("w_group_router", 0, 8)))
    t_rt = lw(nc.gpsimd.dma_start(wrt[:, :, 8:72], wview("w_expert_router", 0, 64)))
    t_rt = lw(nc.gpsimd.dma_start(frow[:, :], t["norm_ffn_w"].to_broadcast([128, D])))
    h2d = nc.dram_tensor("h2d", (S, D), F32, kind="Internal").ap()
    ybuf = nc.dram_tensor("ybuf", (2 * S, D), F32, kind="Internal").ap()

    tn = norm_to(H2, X2, [None] * NT)
    V.w(t_rt)
    th = []
    for tt in range(NT):
        th.append(V(v.tensor_tensor(H2[:, tt, :], H2[:, tt, :], frow[:, :], MUL)))
    G.w(th)
    lh = Lane(sem("s_h2"))
    t_h2d = lh(nc.gpsimd.dma_start(h2d.rearrange("(n p) d -> p n d", p=128), H2[:, :, :]))
    t_h = to_features(H2T, H2, th, None)
    T.w(t_h, t_rt)
    b = bank()
    for tt in range(NT):
        tk = T(mm_group(b[:, tt * 72:tt * 72 + 72], lambda k: H2T[:, k, tt * 128:tt * 128 + 128],
                        lambda k: wrt[:, k, :], 8))
    V.w(tk)
    bv = b[:, 0:288].rearrange("p (a b) -> p a b", a=NT)
    V(v.tensor_tensor(L[:, :, 0:8], bv[:, :, 0:8], scv("b_group_router").unsqueeze(1).to_broadcast([128, NT, 8]), ADD))
    tk = V(v.tensor_tensor(L[:, :, 8:72], bv[:, :, 8:72],
                           scv("b_expert_router").unsqueeze(1).to_broadcast([128, NT, 64]), ADD))
    PS.give(b, tk)

    def up8(x):
        return x.unsqueeze(2).to_broadcast([128, NT, 8])

    iota8m = cc("iota8m").unsqueeze(1).to_broadcast([128, NT, 8])

    def first_max(src, mx, hot, tmp):
        V(v.tensor_reduce(mx, src, AX.X, MAX))
        V(v.tensor_tensor(hot, src, up8(mx), EQ))
        V(v.tensor_scalar(hot, hot, -1000.0, 1000.0, MUL, ADD))
        V(v.tensor_tensor(hot, hot, iota8m, ADD))
        V(v.tensor_reduce(tmp, hot, AX.X, MIN))
        return V(v.tensor_tensor(hot, iota8m, up8(tmp), EQ))

    gm, tmp, v1, v2, gate, w1c, w2c = (s4[:, i, :] for i in range(7))
    gh, es, h1, h2_, e2, ex = (s8[:, i, :, :] for i in range(6))
    first_max(L[:, :, 0:8], gm, gh, tmp)
    tk = V(v.tensor_tensor(ex, L[:, :, 0:8], up8(gm), SUB))
    A.w(tk)
    tk = A(a.activation(ex, ex, ACT.Exp))
    V.w(tk)
    V(v.tensor_reduce(gate, ex, AX.X, ADD))
    V(v.reciprocal(gate, gate))
    EL = L[:, :, 8:72].rearrange("p t (g j) -> p t g j", g=8)
    for tt in range(NT):
        V(v.tensor_tensor(ra[:, tt, :].rearrange("p (g j) -> p g j", g=8), EL[:, tt, :, :],
                          gh[:, tt, :].unsqueeze(2).to_broadcast([128, 8, 8]), MUL))
        V(v.tensor_reduce(es[:, tt, :], ra[:, tt, :].rearrange("p (g j) -> p j g", g=8), AX.X, ADD))
    first_max(es, v1, h1, tmp)
    V(v.scalar_tensor_tensor(e2, h1, -BIG, es, MUL, ADD))
    first_max(e2, v2, h2_, tmp)
    tk = V(v.tensor_tensor(w2c, v2, v1, SUB))
    A.w(tk)
    tk = A(a.activation(w2c, w2c, ACT.Exp))
    V.w(tk)
    V(v.tensor_scalar(w1c, w2c, 1.0, None, ADD))
    V(v.reciprocal(w1c, w1c))
    V(v.tensor_tensor(w1c, w1c, gate, MUL))
    V(v.tensor_tensor(w2c, w2c, w1c, MUL))
    V(v.tensor_copy(wts[:, :, 0], w1c))
    V(v.tensor_copy(wts[:, :, 1], w2c))
    for k, hot in ((0, h1), (1, h2_)):
        for tt in range(NT):
            V(v.tensor_tensor(O[k][:, tt, :].rearrange("p (g j) -> p g j", g=8),
                              gh[:, tt, :].unsqueeze(2).to_broadcast([128, 8, 8]),
                              hot[:, tt, :].unsqueeze(1).to_broadcast([128, 8, 8]), MUL))
    tk = V(v.tensor_tensor(AS[:, :, :], O[0][:, :, :], O[1][:, :, :], ADD))
    T.w(tk)
    b = bank()
    for tt in range(NT + 1):
        o = b[:, tt * 64:tt * 64 + 64]
        full = list(range(min(tt, NT)))
        for q in full:
            m = pe.matmul(o, cc("ones"), AS[:, q, :], start=q == 0, stop=(tt == NT and q == NT - 1))
        if tt < NT:
            m = pe.matmul(o, cc("lt"), AS[:, tt, :], start=tt == 0, stop=True)
    tk = T(m)
    V.w(tk)
    V(v.tensor_copy(rb[:, :, :].rearrange("p a b -> p (a b)"), b[:, 0:256]))
    cnt = e64[:, 0, :]
    tk = V(v.tensor_copy(cnt, b[:, 256:320]))
    PS.give(b, tk)
    nov = e64[:, 1, :]
    V(v.tensor_scalar(nov, cnt, float(CAP), None, GT))
    for m_ in range(CAP + 64, 512, 64):
        V(v.tensor_scalar(e64[:, 2, :], cnt, float(m_), None, GT))
        V(v.tensor_tensor(nov, nov, e64[:, 2, :], ADD))
    inc, alt = e64[:, 3, :], e64[:, 4, :]
    V(v.tensor_copy(inc, nov))
    d = 1
    while d < 64:
        V(v.tensor_copy(alt[:, 0:d], inc[:, 0:d]))
        V(v.tensor_tensor(alt[:, d:64], inc[:, d:64], inc[:, 0:64 - d], ADD))
        inc, alt = alt, inc
        d *= 2
    exc = e64[:, 5, :]
    V(v.tensor_tensor(exc, inc, nov, SUB))
    V(v.tensor_copy(ovn[:, 15:16], inc[:, 63:64]))
    for o in range(NOV):
        V(v.tensor_scalar(e64[:, 2, :], inc, float(o), None, LE))
        V(v.tensor_reduce(st[:, 20:21], e64[:, 2, :], AX.X, ADD))
        V(v.tensor_scalar(st[:, 20:21], st[:, 20:21], 63.0, None, MIN))
        t_ovn = V(v.tensor_copy(ovn[:, o:o + 1], st[:, 20:21]))
    b = bank()
    t_r = [None, None]
    for k in range(2):
        rank, eid, ovs, over, hi, pos, blk = (s4[:, 8 + i, :] for i in range(7))
        for dst, other in ((rank, rb[:, :, :]), (eid, cc("iota64").unsqueeze(1).to_broadcast([128, NT, 64])),
                           (ovs, exc.unsqueeze(1).to_broadcast([128, NT, 64]))):
            V(v.tensor_tensor(ra[:, :, :], O[k][:, :, :], other, MUL))
            V(v.tensor_reduce(dst, ra[:, :, :], AX.X, ADD))
        V(v.tensor_scalar(over, rank, float(CAP), None, GE))
        V(v.tensor_scalar(hi, rank, float(CAP + 64), None, GE))
        for m_ in range(CAP + 128, 512, 64):
            V(v.tensor_scalar(tmp, rank, float(m_), None, GE))
            V(v.tensor_tensor(hi, hi, tmp, ADD))
        V(v.scalar_tensor_tensor(pos, over, -float(CAP), rank, MUL, ADD))
        V(v.scalar_tensor_tensor(pos, hi, -64.0, pos, MUL, ADD))
        V(v.tensor_tensor(ovs, ovs, hi, ADD))
        V(v.tensor_scalar(ovs, ovs, 64.0, None, ADD))
        V(v.tensor_tensor(ovs, ovs, eid, SUB))
        V(v.tensor_tensor(ovs, ovs, over, MUL))
        V(v.tensor_tensor(blk, eid, ovs, ADD))
        for tt in range(NT):
            V.w(t_r[k])
            V(v.tensor_scalar(oR[:, k, :], cc("iota64x2"), pos[:, tt:tt + 1], None, EQ))
            V(v.tensor_scalar(oB[:, k, 0:64], cc("iota64"), blk[:, tt:tt + 1], cc("aid1")[:, tt * 2 + k:tt * 2 + k + 1], EQ, MUL))
            V(v.tensor_scalar(tmp[:, 0:1], blk[:, tt:tt + 1], -64.0, None, ADD))
            tk = V(v.tensor_scalar(oB[:, k, 64:EB], cc("ovid")[:, 0:NOV], tmp[:, 0:1],
                                   cc("aid1")[:, tt * 2 + k:tt * 2 + k + 1], EQ, MUL))
            T.w(tk)
            t_r[k] = T(pe.matmul(b[:, 0:EB], oR[:, k, :], oB[:, k, :], start=(k == 0 and tt == 0),
                                 stop=(k == 1 and tt == NT - 1)))
    V.w(t_r)
    tabf = oB[:, 0, :]
    tab2 = oB[:, 1, :]
    V(v.tensor_copy(tabf, b[:, 0:EB]))
    PS.give(b, V.last())
    V(v.tensor_scalar(tab2, tabf, 0.5, 5001.0, LE, MUL))
    V(v.tensor_tensor(tabf, tabf, tab2, ADD))
    V(v.tensor_scalar(tabf, tabf, -1.0, None, ADD))
    V(v.tensor_scalar(tab2, tabf, 2.0, cc("jcol"), MUL, ADD))
    V(v.tensor_copy(sidx[:, :], tab2))
    V(v.tensor_scalar(tab2, tabf, 512.0, -512.0, GE, MUL))
    V(v.tensor_tensor(tabf, tabf, tab2, ADD))
    V(v.tensor_scalar(tab2, tabf, 2.0, cc("jcol"), MUL, ADD))
    t_idx = V(v.tensor_copy(gidx[:, :], tab2))
    G.w(t_h2d, t_idx)
    V.w(t_h2d)
    fence()

    WE = Arena(work1, high)
    h2r = h2d.rearrange("t (j c) -> (t j) c", j=2)
    ybr = ybuf.rearrange("t (j c) -> (t j) c", j=2)
    gxs = [sb(f"gx{i}", [128, 512], stack=WE) for i in range(3)]
    gxTs = [sb(f"gxT{i}", [128, 4, 128], stack=WE) for i in range(2)]
    sgs = [sb(f"sg{i}", [128, 256], stack=WE) for i in range(2)]
    hids = [sb(f"hid{i}", [128, 256], stack=WE) for i in range(2)]
    hidTs = [sb(f"hidT{i}", [128, 2, 128], stack=WE) for i in range(2)]
    ys = [sb(f"ys{i}", [128, 512], stack=WE) for i in range(2)]
    glane = [Lane(sem(f"s_gx{i}")) for i in range(3)]
    ylane = [Lane(sem(f"s_y{i}")) for i in range(2)]
    for x in gxs:
        t_gz = V(v.memset(x[:, :], 0.0))
    G.w(t_gz)

    def expert_run(n, col0, takew, give, glane, ylane):
        P_gx = Pool([(x, l) for x, l in zip(gxs, glane)])
        P_gxT, P_sg, P_hid, P_hidT = Pool(gxTs), Pool(sgs), Pool(hids), Pool(hidTs)
        P_y = Pool([(x, l) for x, l in zip(ys, ylane)])
        gath, its = {}, {}

        def gather(e):
            if e >= n:
                return
            (x, lane), tk = P_gx.take()
            G.w(tk)
            gath[e] = (x, lane, lane(g.indirect_dma_start(
                out=x[:, :], out_offset=None, in_=h2r[:, :],
                in_offset=bass.IndirectOffsetOnAxis(ap=gidx[:, col0 + e:col0 + e + 1].bitcast(U32), axis=0),
                bounds_check=2 * S - 1, oob_is_err=False)))

        def turn(e):
            if e >= n:
                return
            x, lane, tk = gath[e]
            T.w(tk)
            xT, xt = P_gxT.take()
            b = bank()
            for q in range(4):
                m = pe.transpose(b[:, q * 128:q * 128 + 128], x[:, q * 128:q * 128 + 128], ident)
            tk = T(m)
            V.w(tk, xt)
            t0 = V(v.tensor_copy(xT[:, :, :].rearrange("p a b -> p (a b)"), b[:, :]))
            PS.give(b, t0)
            P_gx.give((x, lane), tk)
            gather(e + 3)
            its[e] = (xT, [t0])

        def up(e):
            if e >= n:
                return
            xT, tks = its[e]
            T.w(tks)
            ps = []
            for j in range(2):
                w, wt, wi = takew(8, 512)
                T.w(wt)
                b = bank()
                for k in range(8):
                    for c in range(2):
                        m = pe.matmul(b[c * 64:c * 64 + 64, 0:256], xT[:, k % 4, k // 4 * 64:k // 4 * 64 + 64],
                                      w[:, k, c * 256:c * 256 + 256], start=k == 0, stop=k == 7)
                tk = T(m)
                give(wi, tk)
                ps.append((b, tk))
            P_gxT.give(xT, tk)
            s, stk = P_sg.take()
            h, htk = P_hid.take()
            A.w(ps[0][1], stk)
            tk = A(a.activation(s[:, :], ps[0][0][:, 0:256], ACT.Silu))
            PS.give(ps[0][0], tk)
            V.w(tk, ps[1][1], htk)
            tk = V(v.tensor_tensor(h[:, :], ps[1][0][:, 0:256], s[:, :], MUL))
            PS.give(ps[1][0], tk)
            P_sg.give(s, tk)
            its[e] = (h, tk)

        def down(e):
            if e < 0:
                return
            h, tk = its[e]
            T.w(tk)
            b = bank()
            for j in range(2):
                m = pe.transpose(b[:, j * 128:j * 128 + 128], h[:, j * 128:j * 128 + 128], ident)
            tk = T(m)
            P_hid.give(h, tk)
            hT_, ht = P_hidT.take()
            V.w(tk, ht)
            tk = V(v.tensor_copy(hT_[:, :, :].rearrange("p a b -> p (a b)"), b[:, 0:256]))
            PS.give(b, tk)
            T.w(tk)
            w, wt, wi = takew(4, 1024)
            T.w(wt)
            (y, lane), yt = P_y.take()
            b = bank()
            for k in range(4):
                for c in range(2):
                    m = pe.matmul(b[c * 64:c * 64 + 64, :], hT_[:, k % 2, k // 2 * 64:k // 2 * 64 + 64],
                                  w[:, k, c * 512:c * 512 + 512], start=k == 0, stop=k == 3)
            tk = T(m)
            A.w(tk, yt)
            tks = A(a.copy(y[:, :], b[:, :]))
            PS.give(b, tks)
            give(wi, tk)
            P_hidT.give(hT_, tk)
            G.w(tks)
            tk = lane(g.indirect_dma_start(
                out=ybr[:, :],
                out_offset=bass.IndirectOffsetOnAxis(ap=sidx[:, col0 + e:col0 + e + 1].bitcast(U32), axis=0),
                in_=y[:, :], in_offset=None, bounds_check=4 * S - 1, oob_is_err=False))
            P_y.give((y, lane), tk)

        for e in range(3):
            gather(e)
        turn(0)
        for e in range(n + 1):
            up(e)
            turn(e + 1)
            down(e - 1)
        return [(lane.sem, lane.n) for lane in list(glane) + list(ylane)]

    t_y = expert_run(64, 0, take, release, glane, ylane)

    for e in (V, A, T, G, SP):
        e.w(t_y)
    fence()
    SP.w(V.last(), A.last(), T.last(), G.last())
    ovr = nc.values_load(ovn[0:1, 15:16], min_val=0, max_val=NOV)
    saved = (V, A, T, G, SP, PS)
    with nc.If(ovr > 0):
        V = Engine(nc.vector, sem("s_dve2"))
        A = Engine(nc.scalar, sem("s_act2"))
        T = Engine(nc.tensor, sem("s_pe2"), serial=False)
        G = Engine(nc.gpsimd, sem("s_pool2"))
        SP = Engine(nc.sync, sem("s_sp2"))
        PS = Pool(banks)
        ob = [sb(f"ob{i}", [128, 4096], stack=WE) for i in range(1)]
        olane = Lane(sem("s_ob"))
        ostate = {"n": 0, "free": None}

        def otake(k, n):
            i = ostate["n"]
            ostate["n"] = i + 1
            order = []
            for e in range(NOV + 1):
                if e < NOV:
                    order += [("w_expert_gate", e), ("w_expert_up", e)]
                if e > 0:
                    order.append(("w_expert_down", e - 1))
            name, e = order[i]
            SP.w(ostate["free"])
            er = nc.sync.value_load(ovn[0:1, e:e + 1], min_val=0, max_val=63)
            src = t[name].rearrange("a e (k p) n -> p (a e) k n", p=128)[:, bass.ds(er, 1), :, :]
            dst = ob[0][:, 0:k * n].rearrange("p (e k n) -> p e k n", k=k, e=1)
            tk = olane(nc.sync.dma_start(dst, src))
            return ob[0][:, 0:k * n].rearrange("p (k n) -> p k n", k=k), tk, i

        def ogive(i, tk):
            ostate["free"] = [tk]

        gl2 = [Lane(sem(f"s_gz{i}")) for i in range(3)]
        yl2 = [Lane(sem(f"s_yz{i}")) for i in range(2)]
        ty2 = expert_run(NOV, 64, otake, ogive, gl2, yl2)
        for e in (V, A, T, G, SP):
            e.w(ty2)
        fence()
        SP.w(V.last(), A.last(), T.last(), G.last())
    V, A, T, G, SP, PS = saved
    PS = Pool(banks)
    A.w(V(v.memset(st[:, 20:21], 0.0)))
    A(a.copy(st[:, 21:22], st[:, 20:21]))
    T(pe.matmul(banks[0][:, 0:1], ident, ident[:, 0:1], start=True, stop=True))
    G(g.memset(st[:, 23:24], 0.0))
    fence()

    WC = Arena(work1, high)
    Y = [sb(f"Y{k}", [128, NT, D], stack=WC) for k in range(2)]
    nrow_ = sb("fnrow", [128, D], stack=WC)
    ly = [Lane(sem(f"s_cy{k}")) for k in range(2)]
    t_c = [ly[k](nc.gpsimd.dma_start(Y[k][:, :, :], ybuf[k * S:(k + 1) * S, :].rearrange("(n p) d -> p n d", p=128)))
           for k in range(2)]
    lf = Lane(sem("s_fn"))
    t_f = lf(nc.gpsimd.dma_start(nrow_[:, :], t["final_norm_w"].unsqueeze(0).to_broadcast([128, D])))
    tc = []
    V.w(t_c)
    for tt in range(NT):
        for k in range(2):
            tk = V(v.scalar_tensor_tensor(X2[:, tt, :], Y[k][:, tt, :], wts[:, tt, k:k + 1], X2[:, tt, :], MUL, ADD))
        tc.append(tk)
    tn = norm_to(Y[0], X2, tc)
    V.w(t_f)
    t_x3 = [V(v.tensor_tensor(X2[:, tt, :], Y[0][:, tt, :], nrow_[:, :], MUL)) for tt in range(NT)]
    fence()

    RB = Arena(region_a, region_a + 65536)
    WB = Arena(work0 + 16384, high)
    A1 = sb("A1", [128, NT, D], stack=RB)
    G1 = sb("G1", [128, 8, S], stack=RB)
    P2 = sb("P2", [128, NT, 2464], stack=WB)
    QT = sb("QT", [128, 11, S], stack=WB)
    wuq = sb("wuq", [128, 2, 384], stack=RB)
    wukv = sb("wukv", [128, 512], stack=RB)
    qlT = sb("qlT", [128, 2, S], stack=RB)
    kvT = sb("kvT", [128, S], stack=RB)
    vm = sb("vm", [128, NT, 256], stack=RB)
    mrow = sb("mrow", [128, 2, 96], stack=RB)
    B_QK = bufs("QK", 2, [128, 8, 96], RB)
    ss2 = sb("ss2", [128, NT, 24], stack=RB)
    rs2 = sb("rs2", [128, NT, 24], stack=RB)
    mh2 = sb("mh2", [128, NT, 24], stack=RB)
    sm3 = sb("sm3", [128, 4, 16], stack=RB)
    sq = QT[:, 0:2, :].rearrange("p a b -> p (a b)")
    lm = Lane(sem("s_mla"))
    t_ml = lm(nc.gpsimd.dma_start(wuq[:, :, :], wview("mla_w_uq_2", 0, 384)))
    t_ml = lm(nc.gpsimd.dma_start(wukv[:, :], t["mla_w_ukv_2"].rearrange("a p n -> (a p) n")))
    t_ml = lm(nc.gpsimd.dma_start(mrow[:, 0, :], t["mla_q_g_2"].to_broadcast([128, 96])))
    t_ml = lm(nc.gpsimd.dma_start(mrow[:, 1, :], t["mla_k_g_2"].to_broadcast([128, 96])))
    t_mh = V(v.memset(mh2[:, :, :], -0.5))
    tn = norm_to(A1, X2, [None] * NT)
    t_h = to_features(G1, A1, tn, lambda k: col("attn_norm_g_2", k))
    T.w(t_h)
    tp = [None] * NT
    for c0 in range(0, 2464, 512):
        n = min(512, 2464 - c0)
        w, wt, wi = take(8, n)
        T.w(wt)
        for tt in range(NT):
            b = bank()
            tk = T(mm_group(b[:, 0:n], lambda k: G1[:, k, tt * 128:tt * 128 + 128], lambda k: w[:, k, :], 8))
            tk2 = evac(P2[:, tt, c0:c0 + n], b[:, 0:n], after=tk)
            PS.give(b, tk2)
        release(wi, tk)
    fence()

    SEG = ((0, 8), (1184, 8), (1952, 6))

    def heads_view(tt, c0, n):
        return P2[:, tt, c0:c0 + n * 64].rearrange("p (h c) -> p h c", h=n)

    for tt in range(NT):
        o = 0
        for c0, n in SEG:
            V(v.tensor_tensor(sq[:, 0:n * 64], P2[:, tt, c0:c0 + n * 64], P2[:, tt, c0:c0 + n * 64], MUL))
            V(v.tensor_reduce(ss2[:, tt, o:o + n], sq[:, 0:n * 64].rearrange("p (h c) -> p h c", h=n), AX.X, ADD))
            o += n
        tk = A(a.activation(sq[:, 512:768], P2[:, tt, 768:1024], ACT.Square, scale=0.5, accum_out=ss2[:, tt, 22:23]))
        tk = A(a.activation(sq[:, 768:896], P2[:, tt, 1024:1152], ACT.Square, scale=0.5 ** 0.5,
                            accum_out=ss2[:, tt, 23:24]))
    V.w(tk)
    tk = V(v.tensor_scalar(ss2[:, :, :], ss2[:, :, :], 1.0 / 64, 1e-6, MUL, ADD))
    G.w(tk, t_mh)
    tk = G(g.tensor_tensor(rs2[:, :, :], ss2[:, :, :], mh2[:, :, :], ALU.pow))
    V.w(tk)
    t_n = []
    for tt in range(NT):
        V(v.tensor_scalar(P2[:, tt, 768:1024], P2[:, tt, 768:1024], rs2[:, tt, 22:23], None, MUL))
        V(v.tensor_scalar(P2[:, tt, 1024:1152], P2[:, tt, 1024:1152], rs2[:, tt, 23:24], None, MUL))
        o = 0
        for c0, n in SEG:
            hv = heads_view(tt, c0, n)
            if c0 == 1952:
                V(v.tensor_scalar(sq[:, 0:64], hv[:, 1, :], rs2[:, tt, o + 1:o + 2], None, MUL))
                V(v.tensor_scalar(hv[:, 1, :], hv[:, 2, :], rs2[:, tt, o + 2:o + 3], None, MUL))
                V(v.tensor_copy(hv[:, 2, :], sq[:, 0:64]))
                V(v.tensor_scalar(hv[:, 0, :], hv[:, 0, :], rs2[:, tt, o:o + 1], None, MUL))
                hv, o, n = hv[:, 3:6, :], o + 3, 3
            tk = V(v.tensor_tensor(hv, hv, rs2[:, tt, o:o + n].unsqueeze(2).to_broadcast([128, n, 64]), MUL))
            o += n
        t_n.append(tk)

    def turn4(dst, src, scol):
        b = bank()
        for tt in range(NT):
            T.w(t_n[tt])
            m = pe.transpose(b[:, tt * 128:tt * 128 + 128], src(tt), ident)
        tk = T(m)
        tk = evac(dst, b[:, :], scol, after=tk)
        PS.give(b, tk)
        return tk

    t_l = []
    for k in range(2):
        t_l.append(turn4(qlT[:, k, :], lambda tt: P2[:, tt, 768 + k * 128:896 + k * 128], col("mla_qlat_g_2", k)))
    t_l.append(turn4(kvT[:, :], lambda tt: P2[:, tt, 1024:1152], col("mla_kvlat_g_2")))
    A.w(t_n)
    t_qt = []
    for base, c0, names in ((0, 0, ("moba_q_g_2", "moba_q_g_2", "moba_k_g_2", "moba_k_g_2")),
                            (4, 1184, ("dil_q_g_2", "dil_q_g_2", "dil_k_g_2", "dil_k_g_2"))):
        for i, name in enumerate(names):
            t_qt.append(turn4(QT[:, base + i, :], lambda tt: P2[:, tt, c0 + i * 128:c0 + i * 128 + 128], col(name)))
    for r in range(2):
        t_qt.append(turn4(QT[:, 8 + r, :], lambda tt: P2[:, tt, 1952 + r * 128:2080 + r * 128], col("swa_q_g_2")))
    t_qt.append(turn4(QT[:, 10, :], lambda tt: P2[:, tt, 2208:2336], col("swa_k_g_2")))

    QM = G1
    T.w(t_l, t_ml)
    V.w(t_ml)
    t_qm = []
    for tt in range(NT):
        ts = slice(tt * 128, tt * 128 + 128)
        bq = bank()
        t1 = T(mm_group(bq[:, 0:384], lambda k: qlT[:, k, ts], lambda k: wuq[:, k, :], 2))
        bk = bank()
        t2 = T(pe.matmul(bk[:, :], kvT[:, ts], wukv[:, :], start=True, stop=True))
        QK, qt = B_QK.take()
        V.w(t1, qt)
        tk = V(v.tensor_copy(QK[:, 0:4, :], bq[:, 0:384].rearrange("p (h c) -> p h c", h=4)))
        PS.give(bq, tk)
        kv = bk[:, :].rearrange("p (h c) -> p h c", h=4)
        V.w(t2)
        V(v.tensor_copy(QK[:, 4:8, 0:64], kv[:, :, 0:64]))
        tk = V(v.tensor_copy(vm[:, tt, :].rearrange("p (h c) -> p h c", h=4), kv[:, :, 64:128]))
        PS.give(bk, tk)
        tk = V(v.tensor_copy(QK[:, 4:8, 64:96], P2[:, tt, 1152:1184].unsqueeze(1).to_broadcast([128, 4, 32])))
        T_ = P2[:, tt, 0:512]
        V.w(t_qt[3])
        V(v.tensor_tensor(T_[:, 0:480].rearrange("p (h c) -> p h c", h=5), QK[:, 0:5, :], QK[:, 0:5, :], MUL))
        V(v.tensor_reduce(sm3[:, tt, 0:5], T_[:, 0:480].rearrange("p (h c) -> p h c", h=5), AX.X, ADD))
        V(v.tensor_tensor(T_[:, 0:288].rearrange("p (h c) -> p h c", h=3), QK[:, 5:8, :], QK[:, 5:8, :], MUL))
        V(v.tensor_reduce(sm3[:, tt, 5:8], T_[:, 0:288].rearrange("p (h c) -> p h c", h=3), AX.X, ADD))
        tk = V(v.tensor_scalar(sm3[:, tt, 0:8], sm3[:, tt, 0:8], 1.0 / 96, 1e-6, MUL, ADD))
        G.w(tk)
        tk = G(g.tensor_tensor(sm3[:, tt, 8:16], sm3[:, tt, 0:8], mh2[:, 0, 0:8], ALU.pow))
        V.w(tk)
        V(v.tensor_tensor(QK[:, :, :], QK[:, :, :], sm3[:, tt, 8:16].unsqueeze(2).to_broadcast([128, 8, 96]), MUL))
        for i in range(2):
            V(v.tensor_tensor(QK[:, i * 4:i * 4 + 4, :], QK[:, i * 4:i * 4 + 4, :],
                              mrow[:, i, :].unsqueeze(1).to_broadcast([128, 4, 96]), MUL))
        cs = cc("rcos")[:, tt * 16:tt * 16 + 16].unsqueeze(1).to_broadcast([128, 8, 16])
        sn = cc("rsin")[:, tt * 16:tt * 16 + 16].unsqueeze(1).to_broadcast([128, 8, 16])
        x1, x2 = QK[:, :, 64:80], QK[:, :, 80:96]
        u1, u2, u3 = (T_[:, i * 128:i * 128 + 128].rearrange("p (h c) -> p h c", h=8) for i in range(3))
        V(v.tensor_tensor(u1, x1, cs, MUL))
        V(v.tensor_tensor(u2, x2, sn, MUL))
        V(v.tensor_tensor(u3, x1, sn, MUL))
        V(v.tensor_tensor(x1, u1, u2, SUB))
        V(v.tensor_tensor(u1, x2, cs, MUL))
        tk = V(v.tensor_tensor(x2, u1, u3, ADD))
        T.w(tk)
        for i in range(2):
            b = bank()
            for j in range(4):
                m = pe.transpose(b[0:96, j * 128:j * 128 + 128], QK[:, i * 4 + j, :], ident)
            tk = T(m)
            tk2 = evac(QM[0:96, i * 4:i * 4 + 4, ts], b[0:96, :].rearrange("p (h c) -> p h c", h=4), after=tk)
            PS.give(b, tk2)
            t_qm.append(tk2)
        B_QK.give(QK, tk)

    mixed = A1
    B_bi = [(sb(f"bi{i}", [128, S], stack=RB), Lane(sem(f"s_bi{i}"))) for i in range(2)]
    P_bi = Pool(B_bi)
    B_s2 = bufs("s2_", 3, [128, S], WB)
    B_t2 = bufs("t2_", 2, [128, S], RB)
    stm = sb("stm", [128, 16, 8], stack=RB)
    T.w(t_qt, t_qm)
    order = [(0, h) for h in range(4)] + [(2, h) for h in range(4)] + [(3, h) for h in range(4)] + [(1, h) for h in range(4)]
    biases = {}

    def load_bias(n):
        if n < 12:
            (x, lane), tk = P_bi.take()
            G.w(tk)
            biases[n] = (x, lane, lane(nc.gpsimd.dma_start(x[:, :], t["biases"][n])))

    load_bias(0)
    load_bias(1)
    items = []
    for hn, (mx, h) in enumerate(order):
        for i in range(4):
            items.append({"m": mx, "h": h, "i": i, "hn": hn, "n": len(items)})

    def q_k_v(mx, h):
        r = slice((h % 2) * 64, (h % 2) * 64 + 64)
        if mx == 0:
            return QT[r, h // 2, :], QT[r, 2 + h // 2, :], lambda j: P2[:, j, 512 + h * 64:576 + h * 64]
        if mx == 2:
            return QT[r, 4 + h // 2, :], QT[r, 6 + h // 2, :], lambda j: P2[:, j, 1696 + h * 64:1760 + h * 64]
        if mx == 3:
            r = slice((h // 2) * 64, (h // 2) * 64 + 64)
            return QT[r, 8 + h % 2, :], QT[r, 10, :], lambda j: P2[:, j, 2336 + (h // 2) * 64:2400 + (h // 2) * 64]
        return QM[0:96, h, :], QM[0:96, 4 + h, :], lambda j: vm[:, j, h * 64:h * 64 + 64]

    def a1(it):
        i, mx = it["i"], it["m"]
        q, k_, _ = q_k_v(mx, it["h"])
        j0 = max(0, i - 1) if mx == 3 else 0
        kn = (i + 1 - j0) * 128
        it["j0"], it["kn"] = j0, kn
        b = bank()
        tk = T(pe.matmul(b[:, 0:kn], q[:, i * 128:i * 128 + 128], k_[:, j0 * 128:(i + 1) * 128], start=True, stop=True))
        s, stk = B_s2.take()
        sm = stm[:, it["n"] % 16, :]
        if it["n"] >= 16:
            V.w(items[it["n"] - 16]["done"])
        V.w(tk, stk)
        if mx == 1:
            bias, scale = cc("causal"), 96.0 ** -0.5
        else:
            x, lane, bt = biases[it["hn"]]
            V.w(bt)
            bias, scale = x[:, :], 1.0
        tk = V(v.tensor_tensor_reduce(s[:, 0:kn], b[:, 0:kn], bias[:, 512 - kn:512], 1.0, -3e38, ADD, MAX, sm[:, 0:1]))
        PS.give(b, tk)
        if mx != 1 and i == 3:
            P_bi.give((x, lane), tk)
            load_bias(it["hn"] + 2)
        if mx == 3:
            V(v.tensor_tensor(sm[:, 0:1], sm[:, 0:1], scv("swa_sinks_2")[:, it["h"]:it["h"] + 1], MAX))
        tk = V(v.tensor_scalar(sm[:, 1:2], sm[:, 0:1], -scale, None, MUL))
        A.w(tk)
        tk = A(a.activation(s[:, 0:kn], s[:, 0:kn], ACT.Exp, scale=scale, bias=sm[:, 1:2], accum_out=sm[:, 2:3]))
        it["s"], it["ts"] = s, tk
        if mx == 3:
            tk = A(a.activation(sm[:, 3:4], scv("swa_sinks_2")[:, it["h"]:it["h"] + 1], ACT.Exp, bias=sm[:, 1:2]))
            it["te"] = tk

    def a2(it):
        nb = it["kn"] // 128
        s = it["s"]
        sm = stm[:, it["n"] % 16, :]
        b = bank()
        T.w(it["ts"])
        for j in range(nb):
            m = pe.transpose(b[:, j * 128:j * 128 + 128], s[:, j * 128:j * 128 + 128], ident)
        tk = T(m)
        B_s2.give(s, tk)
        wt, wtt = B_t2.take()
        V.w(it["ts"])
        if it["m"] == 3:
            V.w(it["te"])
            V(v.tensor_tensor(sm[:, 2:3], sm[:, 2:3], sm[:, 3:4], ADD))
        V(v.reciprocal(sm[:, 4:5], sm[:, 2:3]))
        V.w(tk, wtt)
        tk = V(v.tensor_copy(wt[:, 0:it["kn"]], b[:, 0:it["kn"]]))
        PS.give(b, tk)
        it["wt"], it["twt"] = wt, tk

    def a3(it):
        _, _, vv = q_k_v(it["m"], it["h"])
        b = bank()
        T.w(it["twt"])
        tk = T(mm_group(b[:, 0:64], lambda j: it["wt"][:, j * 128:j * 128 + 128], lambda j: vv(it["j0"] + j),
                        it["kn"] // 128))
        B_t2.give(it["wt"], tk)
        A.w(tk, it["twt"])
        c0 = it["m"] * 256 + it["h"] * 64
        tk = A(a.activation(mixed[:, it["i"], c0:c0 + 64], b[:, 0:64], ACT.Copy, scale=stm[:, it["n"] % 16, 4:5]))
        it["done"] = tk
        PS.give(b, tk)

    for n in range(len(items) + 2):
        if n < len(items):
            a1(items[n])
        if 0 <= n - 1 < len(items):
            a2(items[n - 1])
        if 0 <= n - 2 < len(items):
            a3(items[n - 2])
    tk = A.last()
    for tt in range(NT):
        for m_ in range(4):
            tk = A(a.activation(QT[:, m_, 0:256], mixed[:, tt, m_ * 256:m_ * 256 + 256], ACT.Square, scale=1.0 / 16,
                                accum_out=ss2[:, tt, m_:m_ + 1]))
    V.w(tk)
    tk = V(v.tensor_scalar(ss2[:, :, 0:4], ss2[:, :, 0:4], 1e-6, None, ADD))
    G.w(tk)
    tk = G(g.tensor_tensor(rs2[:, :, 0:4], ss2[:, :, 0:4], mh2[:, :, 0:4], ALU.pow))
    V.w(tk)
    t_n2 = []
    for tt in range(NT):
        mv = mixed[:, tt, :].rearrange("p (m c) -> p m c", m=4)
        t_n2.append(V(v.tensor_tensor(mv, mv, rs2[:, tt, 0:4].unsqueeze(2).to_broadcast([128, 4, 256]), MUL)))
    fence()
    MT = sb("MT", [128, 8, S], stack=Arena(work0 + 16384, high))
    t_h = to_features(MT, mixed, t_n2, lambda k: col("group_out_g_2", k))
    T.w(t_h)
    tx = [None] * NT
    for half in range(2):
        w, wt, wi = take(8, 512)
        T.w(wt)
        for tt in range(NT):
            b = bank()
            tk = T(mm_group(b[:, :], lambda k: MT[:, k, tt * 128:tt * 128 + 128], lambda k: w[:, k, :], 8))
            V.w(tk)
            xv = X2[:, tt, half * 512:half * 512 + 512]
            tx[tt] = V(v.tensor_tensor(xv, xv, b[:, :], ADD))
            PS.give(b, tx[tt])
        release(wi, tk)
    fence()

    WN = Arena(work0 + 16384, high)
    N3 = sb("N3", [128, NT, D], stack=WN)
    H3 = sb("H3", [128, 8, S], stack=WN)
    UU = sb("UU", [128, 32, S], stack=Arena(region_a, region_a + 65536))
    tn = norm_to(N3, X2, tx)
    t_h = to_features(H3, N3, tn, lambda k: col("mlp_norm_g_2", k))
    T.w(t_h)
    t_u = []
    for c in range(8):
        w, wt, wi = take(8, 512)
        T.w(wt)
        for j in range(4):
            b = bank()
            f = c * 4 + j
            tk = T(mm_group(b[:, :], lambda k: w[:, k, j * 128:j * 128 + 128], lambda k: H3[:, k, :], 8))
            A.w(tk)
            tr = A(a.activation(UU[:, f, :], b[:, :], ACT.Relu))
            PS.give(b, tr)
            V.w(tr)
            t_u.append(V(v.tensor_tensor(UU[:, f, :], UU[:, f, :], UU[:, f, :], MUL)))
        release(wi, tk)
    acc8 = [bank() for _ in range(8)]
    tk8 = [None] * 8
    for c in range(8):
        w, wt, wi = take(4, 1024)
        T.w(wt, t_u[c * 4:c * 4 + 4])
        for i in range(8):
            tt, half = i // 2, i % 2
            m = mm_group(acc8[i][:, :], lambda k: UU[:, c * 4 + k, tt * 128:tt * 128 + 128],
                         lambda k: w[:, k, half * 512:half * 512 + 512], 4, start=c == 0, stop=c == 7)
            tk8[i] = T(m)
        release(wi, tk8[7])
    lo = Lane(sem("s_out"))
    ov = out.rearrange("a (n p) d -> p (a n) d", p=128)
    for i in range(8):
        tt, half = i // 2, i % 2
        xv = X2[:, tt, half * 512:half * 512 + 512]
        V.w(tk8[i])
        tk = V(v.tensor_tensor(xv, xv, acc8[i][:, :], ADD))
        SP.w(tk)
        t_out = lo(nc.sync.dma_start(ov[:, tt, half * 512:half * 512 + 512], xv))
    SP.w(t_out)


NAMES = ["x", "positions", "norm_mix_w", "w_in", "conv_w", "conv_b", "dt_bias", "a_log", "d_skip", "ssd_norm_w",
         "lambda_q1", "lambda_k1", "lambda_q2", "lambda_k2", "subln_w", "w_branch_attn", "w_branch_ssd", "w_out",
         "norm_ffn_w", "w_group_router", "b_group_router", "w_expert_router", "b_expert_router", "w_expert_gate",
         "w_expert_up", "w_expert_down", "final_norm_w", "attn_norm_g_2", "w_in_2", "moba_q_g_2", "moba_k_g_2",
         "mla_qlat_g_2", "mla_kvlat_g_2", "mla_w_uq_2", "mla_w_ukv_2", "mla_q_g_2", "mla_k_g_2", "dil_q_g_2",
         "dil_k_g_2", "swa_q_g_2", "swa_k_g_2", "swa_sinks_2", "group_out_g_2", "w_o_2", "mlp_norm_g_2", "w_up_2",
         "w_down_2"]


def kernel(**inputs):
    import concourse.bacc as bacc
    from concourse.bass_utils import run_bass_kernel_spmd

    nc = bacc.Bacc("TRN2", target_bir_lowering=False, num_devices=1)
    consts, biases = constants()
    arrays, t = {}, {}
    for name, value in [("consts", consts), ("biases", biases)] + [(n, inputs[n]) for n in NAMES]:
        value = np.ascontiguousarray(value)
        arrays["in_" + name] = value
        t[name] = nc.dram_tensor("in_" + name, value.shape, mybir.dt.from_np(value.dtype), kind="ExternalInput").ap()
    out = nc.dram_tensor("out_0", (1, S, D), F32, kind="ExternalOutput").ap()
    build(nc, t, out)
    result = run_bass_kernel_spmd(nc, [arrays], core_ids=[0])
    return result.results[0]["out_0"]
```

```python
from contextlib import ExitStack

import numpy as np
import concourse.bass as bass
from concourse import mybir

F32 = mybir.dt.float32
F32R = mybir.dt.float32r
I32 = mybir.dt.int32
U32 = mybir.dt.uint32
ALU = mybir.AluOpType
ACT = mybir.ActivationFunctionType
AX = mybir.AxisListType
MUL, ADD, SUB, MAX, MIN = ALU.mult, ALU.add, ALU.subtract, ALU.max, ALU.min
EQ, GE, GT, LE = ALU.is_equal, ALU.is_ge, ALU.is_gt, ALU.is_le

S = 512
D = 1024
NT = 4
RING = 3
CAP = 64
NOV = 15
BIG = 1e30
TWO_PI = 6.283185307179586
MAGIC = 12582912.0

VECS = [
    ("norm_mix_w", 8), ("conv_b", 32), ("ssd_norm_w", 16), ("subln_w", 1), ("attn_norm_g_2", 8),
    ("group_out_g_2", 8), ("mlp_norm_g_2", 8), ("mla_qlat_g_2", 2), ("mla_kvlat_g_2", 1),
    ("moba_q_g_2", -1), ("moba_k_g_2", -1), ("dil_q_g_2", -1), ("dil_k_g_2", -1),
    ("swa_q_g_2", -1), ("swa_k_g_2", -1),
]


def vec_rows():
    at, n = {}, 0
    for name, rows in VECS:
        at[name] = n
        n += abs(rows)
    return at, n


CONSTS = [
    ("ident", 128), ("tri", 128), ("gt", 128), ("lt", 128), ("ones", 128), ("perm", 128),
    ("causal", 512), ("iota64", 64), ("iota128", 128), ("iota8m", 8), ("aid1", 8), ("ovid", 16), ("jcol", 1), ("iota64x2", 128),
    ("rcos", 64), ("rsin", 64), ("invf", 1), ("mhalf", 8),
]


def const_cols():
    at, n = {}, 0
    for name, cols in CONSTS:
        at[name] = (n, n + cols)
        n += cols
    return at, n


def constants():
    at, n = const_cols()
    c = np.zeros((128, n), np.float32)
    p = np.arange(128)

    def put(name, v):
        a, b = at[name]
        c[:, a:b] = np.broadcast_to(v, (128, b - a))

    put("ident", np.eye(128))
    put("tri", p[:, None] <= p[None, :])
    put("gt", p[:, None] > p[None, :])
    put("lt", p[:, None] < p[None, :])
    put("ones", 1.0)
    perm = np.zeros((128, 128))
    for m in range(128):
        if m % 64 < 32:
            perm[m + 32, m] = -1.0
        else:
            perm[m - 32, m] = 1.0
    put("perm", perm)
    dist = p[:, None] + 384 - np.arange(512)[None, :]
    put("causal", np.where(dist >= 0, 0.0, -BIG))
    put("iota64", np.arange(64))
    put("iota128", p)
    put("iota8m", np.arange(8) - 1000.0)
    aid = np.zeros((128, 8))
    for tt in range(4):
        for k in range(2):
            aid[:, tt * 2 + k] = k * 512 + tt * 128 + p + 1
    put("aid1", aid)
    put("ovid", np.arange(16))
    put("jcol", (p >= 64)[:, None])
    put("iota64x2", p % 64)
    inv2 = (1.0 / (np.float32(10000.0) ** (np.arange(0, 32, 2, dtype=np.float32) / np.float32(32)))).astype(np.float32)
    ang = np.arange(512, dtype=np.float32)[:, None] * inv2[None, :]
    put("rcos", np.cos(ang).astype(np.float32).reshape(4, 128, 16).transpose(1, 0, 2).reshape(128, 64))
    put("rsin", np.sin(ang).astype(np.float32).reshape(4, 128, 16).transpose(1, 0, 2).reshape(128, 64))
    inv1 = (1.0 / (np.float32(10000.0) ** (np.arange(0, 64, 2, dtype=np.float32) / np.float32(64)))).astype(np.float32)
    put("invf", inv1[p % 32][:, None])
    put("mhalf", -0.5)
    bias = np.zeros((12, 128, 512), np.float32)
    slopes = np.exp2(-8.0 * np.arange(1, 13, dtype=np.float32).reshape(4, 3) / 12).astype(np.float32)
    mult = (dist <= 128) * 1 + (dist % 4 == 0) * 1 + (dist % 16 == 0) * 1
    lnm = np.where((dist >= 0) & (mult > 0), np.log(np.maximum(mult, 1)), -BIG)
    swa = np.where((dist >= 0) & (dist < 128), 0.0, -BIG)
    cau = np.where(dist >= 0, 0.0, -BIG)
    for h in range(4):
        for m, extra in enumerate((cau, lnm, swa)):
            bias[m * 4 + h] = (-slopes[h, m] * dist.astype(np.float32)).astype(np.float64) + extra
    return c, bias


class Engine:

    def __init__(self, eng, sem, serial=True):
        self.eng, self.sem, self.n, self.seen, self.serial = eng, sem, 0, {}, serial

    def w(self, *toks):
        for t in toks:
            if t is None:
                continue
            if isinstance(t, list):
                self.w(*t)
                continue
            sem, v = t
            if self.seen.get(sem.num, 0) < v:
                self.eng.wait_ge(sem, v)
                self.seen[sem.num] = v

    def __call__(self, ins):
        ins.then_inc(self.sem, 1)
        self.n += 1
        if self.serial:
            self.w((self.sem, self.n))
        return (self.sem, self.n)

    def last(self):
        return (self.sem, self.n)


class Lane:

    def __init__(self, sem):
        self.sem, self.n = sem, 0

    def __call__(self, ins):
        ins.then_inc(self.sem, 16)
        self.n += 16
        return (self.sem, self.n)


class Pool:

    def __init__(self, aps):
        self.free = [(a, None) for a in aps]

    def take(self):
        return self.free.pop(0)

    def give(self, ap, *toks):
        self.free.append((ap, list(toks)))


class Arena:

    def __init__(self, start, end):
        self.at, self.end = (start + 63) // 64 * 64, end

    def take(self, shape):
        at = self.at
        self.at = at + (int(np.prod(shape[1:])) * 4 + 63) // 64 * 64
        assert self.at <= self.end, (shape, self.at, self.end)
        return at


def run(gen):
    for _ in gen:
        pass


def interleave(a, na, b, nb):
    ia = ib = 0
    live_a = live_b = True
    while live_a or live_b:
        first = live_a and (not live_b or ia * nb <= ib * na)
        try:
            next(a if first else b)
        except StopIteration:
            if first:
                live_a = False
            else:
                live_b = False
            continue
        if first:
            ia += 1
        else:
            ib += 1


def build(nc, t, out):
    sems = []

    def sem(name):
        s = nc.alloc_semaphore(name)
        sems.append(s)
        return s

    V = Engine(nc.vector, sem("s_dve"))
    A = Engine(nc.scalar, sem("s_act"))
    T = Engine(nc.tensor, sem("s_pe"), serial=False)
    G = Engine(nc.gpsimd, sem("s_pool"))
    SP = Engine(nc.sync, sem("s_sp"))
    v, a, g, pe = nc.vector, nc.scalar, nc.gpsimd, nc.tensor

    persist = ExitStack()
    low, high = nc.sbuf_base, nc.sbuf_usable_end
    PM = Arena(low, high)

    def sb(name, shape, dt=F32, stack=None):
        return nc.alloc_sbuf_tensor_at(name, shape, dt, offset=(stack or PM).take(shape))

    banks = [persist.enter_context(nc.psum_tensor(f"ps{i}", [128, 512], F32)) for i in range(8)]
    PS = Pool(banks)

    def bank():
        b, tok = PS.take()
        T.w(tok)
        return b

    def fence():
        now = [e.last() for e in (V, A, T, G)]
        for e in (V, A, T, G):
            e.w(now)

    cat, ncc = const_cols()
    C = sb("consts", [128, ncc])
    lane0 = Lane(sem("s_in"))
    lanex = Lane(sem("s_x"))
    laneb = Lane(sem("s_bcast"))

    def cc(name):
        x, y = cat[name]
        return C[:, x:y]

    ident = cc("ident")

    region_a = PM.at
    X = sb("X", [128, NT, D])
    XN = sb("XN", [128, NT, D])
    hTh = sb("hTh", [128, 8, S], F32R)
    attT = sb("attT", [128, 8, S])
    hTl = nc.alloc_sbuf_tensor_at("hTl", [128, 8, S], F32R, offset=region_a)
    B_hb = Pool([nc.alloc_sbuf_tensor_at(f"hb{i}", [128, 8, 128], F32R, offset=region_a + 16384 + i * 4096)
                 for i in range(4)])
    ssdd = nc.dram_tensor("ssdd", (2048, S), F32, kind="Internal").ap()
    xsrc = t["x"].rearrange("a (n p) d -> p (a n) d", p=128)
    t_x = lanex(nc.sync.dma_start(X[:, :, :], xsrc))
    lanec = Lane(sem("s_consts"))
    t_cst = lanec(nc.scalar.dma_start(C[:, :], t["consts"]))
    rows_at, nrow = vec_rows()
    ring_at = PM.at
    ring = [sb(f"ring{i}", [128, 4096]) for i in range(RING)]
    vcol = sb("vcol", [128, nrow + 128])
    sc = sb("sc", [128, 512])
    st = sb("st", [128, 256])
    ovn = sb("ovn", [128, 16], I32)
    work0 = PM.at
    WK = Arena(work0, high)
    cosT = sb("cosT", [128, S], stack=WK)
    sinT = sb("sinT", [128, S], stack=WK)
    small = Arena(high - 8192, high)
    vrow = sb("vrow", [nrow, 128], stack=small)
    crow = sb("crow", [128, 128], stack=small)
    for name, n in VECS:
        r = rows_at[name]
        if n < 0:
            for half in range(2):
                t_in = lane0(nc.sync.dma_start(vrow[r:r + 1, half * 64:half * 64 + 64], t[name]))
        else:
            src = t[name]
            if name == "group_out_g_2":
                src = src.rearrange("a b (r c) -> (a b r) c", c=128)
            else:
                src = src.rearrange("a (r c) -> (a r) c", c=128)
            t_in = lane0(nc.sync.dma_start(vrow[r:r + n, :], src))
    t_in = lane0(nc.sync.dma_start(crow[:, :], t["conv_w"].rearrange("a k (r c) -> (a k r) c", c=128)))

    def col(name, i=0):
        return vcol[:, rows_at[name] + i:rows_at[name] + i + 1]

    def conv_col(k, i):
        return vcol[:, nrow + k * 32 + i:nrow + k * 32 + i + 1]

    sc_at = {}
    for name, n in (("dt_bias", 32), ("a_log", 32), ("d_skip", 32), ("lambda_q1", 64), ("lambda_k1", 64),
                    ("lambda_q2", 64), ("lambda_k2", 64), ("b_group_router", 8), ("b_expert_router", 64),
                    ("swa_sinks_2", 4)):
        o = sum(x[1] for x in sc_at.values())
        sc_at[name] = (o, n)
        t_bc = laneb(nc.gpsimd.dma_start(sc[:, o:o + n], t[name].to_broadcast([128, n])))

    def scv(name):
        o, n = sc_at[name]
        return sc[:, o:o + n]

    posi = sb("posi", [128, S], I32, stack=small)
    t_bc = laneb(nc.gpsimd.dma_start(posi[:, :], t["positions"].to_broadcast([128, S])))

    rlane = [Lane(sem(f"s_ring{i}")) for i in range(RING)]
    chunks = []

    def wview(name, c0, n):
        return t[name].rearrange("a (k p) n -> p (a k) n", p=128)[:, :, c0:c0 + n]

    for h in range(8):
        chunks.append([(0, 128, wview("w_in", h * 128, 128)), (128, 128, wview("w_in", 1024 + h * 128, 128)),
                       (256, 128, wview("w_in", 2048 + h * 128, 128)), (384, 0, None)])
    for gr in range(8):
        chunks.append([(0, 256, wview("w_in", 5120 + gr * 256, 256)),
                       (256, 128, wview("w_in", 7168 + gr * 128, 128)),
                       (384, 128, wview("w_in", 8192 + gr * 128, 128))])
        chunks.append([(0, 256, wview("w_in", 3072 + gr * 256, 256))])
    for half in range(2):
        o = half * 512
        chunks.append([(0, 512, wview("w_in", 9248 + o, 512))])
        chunks.append([(0, 512, wview("w_branch_attn", o, 512))])
        chunks.append([(0, 512, wview("w_in", 10272 + o, 512))])
        for kk in range(2):
            chunks.append([(0, 512, t["w_branch_ssd"].rearrange("a (k p) n -> p (a k) n", p=128)[:, kk * 8:kk * 8 + 8, o:o + 512])])
    for half in range(2):
        chunks.append([(0, 512, wview("w_out", half * 512, 512))])
    n_mix = len(chunks)

    def eview(name, e):
        return t[name][0, e].rearrange("(k p) n -> p k n", p=128)

    def moe_chunks(e):
        return ([(0, 512, eview("w_expert_gate", e))], [(0, 512, eview("w_expert_up", e))],
                [(0, 1024, eview("w_expert_down", e))])

    for e in range(65):
        if e < 64:
            chunks += moe_chunks(e)[0:2]
        if e > 0:
            chunks.append(moe_chunks(e - 1)[2])
    n_moe_end = len(chunks)
    for c0 in range(0, 2464, 512):
        n = min(512, 2464 - c0)
        chunks.append([(0, n, wview("w_in_2", c0, n))])
    for half in range(2):
        chunks.append([(0, 512, wview("w_o_2", half * 512, 512))])
    for part in range(2):
        for c0 in range(part * 4, part * 4 + 4):
            chunks.append([(0, 512, wview("w_up_2", c0 * 512, 512))])
        for kk in range(part * 4, part * 4 + 4):
            chunks.append([(0, 1024, t["w_down_2"].rearrange("a (k p) n -> p (a k) n", p=128)[:, kk * 4:kk * 4 + 4, :])])

    state = {"issued": 0, "taken": 0, "limit": n_moe_end + 1}
    slot_tok = {}
    slot_of = {}
    slots = [(i, None) for i in range(RING)]

    def issue():
        i = state["issued"]
        if i >= len(chunks) or not slots or i >= state["limit"]:
            return
        r, free = slots.pop(0)
        slot_of[i] = r
        SP.w(free)
        width = sum(x[1] for x in chunks[i])
        width = 512 if len(chunks[i]) == 4 else width
        for c0, n, src in chunks[i]:
            if n:
                k = src.shape[1]
                dst = ring[r][:, 0:k * width].rearrange("p (k n) -> p k n", k=k)[:, :, c0:c0 + n]
                slot_tok[i] = rlane[r](nc.sync.dma_start(dst, src))
        state["issued"] = i + 1

    def take(k, n):
        i = state["taken"]
        state["taken"] = i + 1
        return ring[slot_of[i]][:, 0:k * n].rearrange("p (k n) -> p k n", k=k), slot_tok[i], i

    def release(i, *toks):
        if slot_of[i] < RING or state["issued"] < n_moe_end:
            slots.append((slot_of[i], list(toks)))
        issue()

    for _ in range(RING):
        issue()

    rview = [nc.alloc_sbuf_tensor_at(f"ringr{i}", [128, 4096], F32R, offset=ring_at + i * 16384) for i in range(RING)]

    seq = [(h, 512, j * 128) for h in range(8) for j in range(3)]
    for gr in range(8):
        seq += [(8 + 2 * gr, 512, j * 128) for j in range(4)] + [(9 + 2 * gr, 256, j * 128) for j in range(2)]
    for half in range(2):
        seq += [(24 + 5 * half + i, 512, j * 128) for i in (0, 2) for j in range(4)]
    ready_b, half_b = [], []

    def split_next():
        if half_b:
            blk = half_b.pop(0)
            V.w(blk["th"], slot_tok[blk["i"]])
            blk["tok"] = V(v.tensor_tensor(blk["lo"], blk["raw"], blk["hi"], SUB))
            ready_b.append(blk)
        if seq and seq[0][0] in slot_of and len(B_hb.free) > 0:
            i, width, c0 = seq.pop(0)
            r = slot_of[i]
            c = slice(c0, c0 + 128)
            raw = ring[r][:, 0:8 * width].rearrange("p (k n) -> p k n", k=8)[:, :, c]
            lo = rview[r][:, 0:8 * width].rearrange("p (k n) -> p k n", k=8)[:, :, c]
            hb, ht = B_hb.take()
            A.w(slot_tok[i], ht)
            half_b.append({"i": i, "hb": hb, "hi": hb[:, :, :], "raw": raw, "lo": lo,
                           "th": A(a.copy(hb[:, :, :], raw))})
            return True
        return False

    def times_h():
        while not ready_b:
            split_next()
        blk = ready_b.pop(0)
        while len(ready_b) + len(half_b) < 3 and split_next():
            pass
        b = bank()
        T.w(blk["tok"])
        for k in range(8):
            pe.matmul(b[:, :], blk["hi"][:, k, :], hTh[:, k, :], start=k == 0, stop=False)
            pe.matmul(b[:, :], blk["hi"][:, k, :], hTl[:, k, :], start=False, stop=False)
            m = pe.matmul(b[:, :], blk["lo"][:, k, :], hTh[:, k, :], start=False, stop=k == 7)
            if k == 3:
                yield
        tk = T(m)
        B_hb.give(blk["hb"], tk)
        return b, tk, blk["i"]

    def prepare(k, n, B_hi):
        w, wt, wi = take(k, n)
        hi, ht = B_hi.take()
        lo = rview[slot_of[wi]]
        return {"k": k, "n": n, "raw": ring[slot_of[wi]], "hi": hi, "lo": lo, "wt": wt, "ht": ht, "wi": wi, "tok": [],
                "B": B_hi, "vh": hi[:, 0:k * n].rearrange("p (k n) -> p k n", k=k),
                "vl": lo[:, 0:k * n].rearrange("p (k n) -> p k n", k=k)}

    def split_part(rec, q, parts=4):
        if rec is None:
            return
        n = rec["k"] * rec["n"] // parts
        c = slice(q * n, q * n + n)
        A.w(rec["wt"], rec["ht"])
        V.w(rec["wt"], A(a.copy(rec["hi"][:, c], rec["raw"][:, c])))
        rec["tok"].append(V(v.tensor_tensor(rec["lo"][:, c], rec["raw"][:, c], rec["hi"][:, c], SUB)))

    def retire(rec, tok):
        rec["B"].give(rec["hi"], tok)
        release(rec["wi"], tok)

    def mm3(o, lhs, rhs, n, start=True, stop=True):
        for k in range(n):
            (lh, ll), (rh, rl) = lhs(k), rhs(k)
            pe.matmul(o, lh, rh, start=start and k == 0, stop=False)
            pe.matmul(o, lh, rl, start=False, stop=False)
            m = pe.matmul(o, ll, rh, start=False, stop=stop and k == n - 1)
        return m

    mhalf = cc("mhalf")

    state_w = {"flip": 0}

    def evac(dst, src, scale=None, after=None):
        state_w["flip"] ^= 1
        if state_w["flip"]:
            V.w(after)
            if scale is None:
                return V(v.tensor_copy(dst, src))
            return V(v.tensor_scalar(dst, src, scale, None, MUL))
        A.w(after)
        if scale is None:
            return A(a.copy(dst, src))
        return A(a.activation(dst, src, ACT.Copy, scale=scale))

    def rstd(dst, ss, eps, tok):
        G.w(tok)
        G(g.tensor_scalar(ss, ss, eps, None, ADD))
        return G(g.tensor_tensor(dst, ss, mhalf[:, 0:ss.shape[1]], ALU.pow))

    def norm_to(dst, src, deps, eps=1e-6, free=None):
        toks = []
        A.w(free)
        for tt in range(NT):
            A.w(deps[tt])
            toks.append(A(a.activation(dst[:, tt, :], src[:, tt, :], ACT.Square, scale=1.0 / 32,
                                       accum_out=st[:, 8 + tt:9 + tt])))
        tk = rstd(st[:, 12:16], st[:, 8:12], eps, toks[-1])
        V.w(tk)
        return [V(v.tensor_scalar(dst[:, tt, :], src[:, tt, :], st[:, 12 + tt:13 + tt], None, MUL))
                for tt in range(NT)]

    def norm_start(junk, src, tt, tok, o):
        A.w(tok)
        tk = A(a.activation(junk, src[:, tt, :], ACT.Square, scale=1.0 / 32, accum_out=st[:, o + tt:o + tt + 1]))
        return rstd(st[:, o + 4 + tt:o + 5 + tt], st[:, o + tt:o + tt + 1], 1e-6, tk)

    def norm_end(dst, src, tt, tok, o, row=None):
        V.w(tok)
        if row is None:
            return V(v.tensor_scalar(dst[:, tt, :], src[:, tt, :], st[:, o + 4 + tt:o + 5 + tt], None, MUL))
        return V(v.scalar_tensor_tensor(dst[:, tt, :], src[:, tt, :], st[:, o + 4 + tt:o + 5 + tt], row, MUL, MUL))

    def turn_tile(dst, src, tt, tok, name=None):
        outs = []
        T.w(tok)
        for i in range(2):
            b = bank()
            for k in range(4):
                m = pe.transpose(b[:, k * 128:k * 128 + 128], src[:, tt, (i * 4 + k) * 128:(i * 4 + k) * 128 + 128], ident)
            tk = T(m)
            d = dst[:, i * 4:i * 4 + 4, tt * 128:tt * 128 + 128]
            bv = b[:, :].rearrange("p (k c) -> p k c", k=4)
            if name is None:
                tk = evac(d, bv, after=tk)
            else:
                r = rows_at[name] + i * 4
                V.w(tk)
                tk = V(v.tensor_tensor(d, bv, vcol[:, r:r + 4].unsqueeze(2).to_broadcast([128, 4, 128]), MUL))
            PS.give(b, tk)
            outs.append(tk)
        return outs

    def mm_group(o, lhs, rhs, n, start=True, stop=True):
        for k in range(n):
            m = pe.matmul(o, lhs(k), rhs(k), start=start and k == 0, stop=stop and k == n - 1)
        return m

    G.w(t_cst)
    tn = norm_to(XN, X, [t_x] * NT)

    T.w(t_cst, t_in)
    b = bank()
    pe.transpose(b[:, 0:nrow], vrow[:, :], ident[0:nrow, 0:nrow])
    tk = T(pe.transpose(b[:, nrow:nrow + 128], crow[:, :], ident))
    V.w(tk, t_cst)
    t_col = V(v.tensor_copy(vcol[:, :], b[:, 0:nrow + 128]))
    PS.give(b, t_col)
    t_col = V(v.tensor_scalar(col("subln_w"), col("subln_w"), 0.8, None, MUL))
    for name in ("moba_q_g_2", "dil_q_g_2", "swa_q_g_2"):
        t_col = V(v.tensor_scalar(col(name), col(name), 0.125, None, MUL))
    A.w(t_col, t_cst)
    t_h = []
    A.w(tn)
    for k in range(8):
        b = bank()
        for tt in range(NT):
            T.w(tn[tt])
            m = pe.transpose(b[:, tt * 128:tt * 128 + 128], XN[:, tt, k * 128:k * 128 + 128], ident)
        tk = T(m)
        A.w(tk)
        tk = A(a.activation(hTh[:, k, :], b[:, :], ACT.Copy, scale=col("norm_mix_w", k)))
        V.w(tk)
        tk = V(v.scalar_tensor_tensor(hTl[:, k, :], b[:, :], col("norm_mix_w", k), hTh[:, k, :], MUL, SUB))
        PS.give(b, tk)
        t_h.append(tk)
    T.w(t_h)
    A.w(t_h)
    for _ in range(3):
        split_next()

    for e in (V, A, G):
        e.w(t_in, t_bc)
    lamj = sb("lamj", [128, 64], stack=small)
    V(v.tensor_tensor_reduce(lamj[:, :], scv("lambda_q1"), scv("lambda_k1"), 1.0, 0.0, MUL, ADD, st[:, 0:1]))
    tk = V(v.tensor_tensor_reduce(lamj[:, :], scv("lambda_q2"), scv("lambda_k2"), 1.0, 0.0, MUL, ADD, st[:, 1:2]))
    A.w(tk)
    tk = A(a.activation(st[:, 2:4], st[:, 0:2], ACT.Exp))
    V.w(tk)
    V(v.tensor_tensor(st[:, 4:5], st[:, 3:4], st[:, 2:3], SUB))
    t_lam = V(v.tensor_scalar(st[:, 4:5], st[:, 4:5], 0.8 - 0.6, None, SUB))
    nlam = st[:, 4:5]

    ang = sb("ang", [128, S], stack=small)
    rn = sb("rn", [128, S], stack=small)
    V(v.tensor_copy(ang[:, :], posi[:, :]))
    V(v.tensor_scalar(ang[:, :], ang[:, :], cc("invf"), None, MUL))
    C1 = 6.28125
    C2 = float(np.float32(TWO_PI - C1))
    for dst, sh, off in ((sinT, 0.0, 0.0), (cosT, 0.25, TWO_PI / 4)):
        V(v.tensor_scalar(rn[:, :], ang[:, :], 1.0 / TWO_PI, sh, MUL, ADD))
        V(v.tensor_scalar(rn[:, :], rn[:, :], MAGIC, None, ADD))
        V(v.tensor_scalar(rn[:, :], rn[:, :], MAGIC, None, SUB))
        V(v.scalar_tensor_tensor(dst[:, :], rn[:, :], -C1, ang[:, :], MUL, ADD))
        V(v.scalar_tensor_tensor(dst[:, :], rn[:, :], -C2, dst[:, :], MUL, ADD))
        V(v.tensor_scalar(dst[:, :], dst[:, :], off, 3.1415925, ADD, MIN))
        tk = V(v.tensor_scalar(dst[:, :], dst[:, :], -3.1415925, None, MAX))
        A.w(tk)
        t_rot = A(a.activation(dst[:, :], dst[:, :], ACT.Sin))
    V.w(t_rot)


    def bufs(name, n, shape, stack):
        return Pool([sb(f"{name}{i}", shape, stack=stack) for i in range(n)])

    B_raw = bufs("raw", 3, [128, S], WK)
    B_q = bufs("bq", 2, [128, S], WK)
    B_k = bufs("bk", 2, [128, S], WK)
    B_v = bufs("bv", 3, [128, NT, 128], WK)
    B_s = bufs("bs", 3, [128, 2, S], WK)
    B_w = bufs("bw", 2, [128, S], WK)
    B_wt = bufs("bwt", 2, [128, S], WK)
    B_st = bufs("bst", 6, [128, 16], WK)
    B_at = bufs("bat", 3, [128, NT, 128], WK)
    heads = {}

    def dense_head(h):
        raws = []
        outs = []
        for j in range(3):
            b, tk, wi = yield from times_h()
            if j == 2:
                release(wi, tk)
            raw, rt = B_raw.take()
            A.w(rt, tk)
            tk = A(a.copy(raw[:, :], b[:, :]))
            PS.give(b, tk)
            raws.append((raw, tk))
            yield
            if j == 0:
                continue
            raw, tk = raws[j - 1]
            dst, dtk = (B_q, B_k)[j - 1].take()
            b = bank()
            T.w(tk)
            tp = T(pe.matmul(b[:, :], cc("perm"), raw[:, :], start=True, stop=True))
            V.w(dtk, tk)
            V(v.tensor_tensor(dst[:, :], raw[:, :], cosT[:, :], MUL))
            V.w(tp)
            t2 = V(v.tensor_tensor(raw[:, :], b[:, :], sinT[:, :], MUL))
            PS.give(b, t2)
            t3 = V(v.tensor_tensor(dst[:, :], dst[:, :], raw[:, :], ADD))
            B_raw.give(raw, t3)
            outs.append((dst, t3))
        raw, tk = raws[2]
        vv, vt = B_v.take()
        b = bank()
        T.w(tk)
        for tt in range(NT):
            m = pe.transpose(b[:, tt * 128:tt * 128 + 128], raw[:, tt * 128:tt * 128 + 128], ident)
        tv = T(m)
        B_raw.give(raw, tv)
        A.w(vt, tv)
        tk = A(a.copy(vv[:, :, :].rearrange("p a b -> p (a b)"), b[:, :]))
        PS.give(b, tk)
        outs.append((vv, tk))
        heads[h] = outs
        yield

    items = [{"h": n // 4, "i": n % 4} for n in range(32)]
    t_att = [None] * 8

    def scores(it):
        h, i = it["h"], it["i"]
        (q, tq), (k_, tk_), _ = heads[h]
        kn = (i + 1) * 128
        s, stk = B_s.take()
        sm, smk = B_st.take()
        T.w(tq, tk_)
        for c in range(2):
            b = bank()
            r = slice(c * 64, c * 64 + 64)
            tk = T(pe.matmul(b[:, 0:kn], q[r, i * 128:i * 128 + 128], k_[r, 0:kn], start=True, stop=True))
            V.w(stk, smk, tk)
            tv = V(v.tensor_tensor_reduce(s[:, c, 0:kn], b[:, 0:kn], cc("causal")[:, 384 - 128 * i:512],
                                          1.0, -3e38, ADD, MAX, sm[:, c:c + 1]))
            PS.give(b, tv)
        if i == 3:
            B_q.give(q, tk)
            B_k.give(k_, tk)
        tv = V(v.tensor_scalar(sm[:, 2:4], sm[:, 0:2], -0.125, None, MUL))
        A.w(tv)
        for c in range(2):
            tk = A(a.activation(s[:, c, 0:kn], s[:, c, 0:kn], ACT.Exp, scale=0.125, bias=sm[:, 2 + c:3 + c],
                                accum_out=sm[:, 4 + c:5 + c]))
        it["s"], it["sm"], it["ts"], it["kn"] = s, sm, tk, kn

    def weights(it):
        s, sm, kn = it["s"], it["sm"], it["kn"]
        W, Wt = B_w.take()
        V.w(it["ts"], Wt)
        V(v.reciprocal(sm[:, 6:8], sm[:, 4:6]))
        V(v.tensor_scalar(sm[:, 8:9], sm[:, 7:8], nlam, None, MUL))
        V(v.tensor_scalar(W[:, 0:kn], s[:, 0, 0:kn], sm[:, 6:7], None, MUL))
        tk = V(v.scalar_tensor_tensor(W[:, 0:kn], s[:, 1, 0:kn], sm[:, 8:9], W[:, 0:kn], MUL, ADD))
        B_s.give(s, tk)
        it["W"], it["tW"] = W, tk

    def weights_turned(it):
        b = bank()
        T.w(it["tW"])
        for j in range(it["i"] + 1):
            m = pe.transpose(b[:, j * 128:j * 128 + 128], it["W"][:, j * 128:j * 128 + 128], ident)
        tk = T(m)
        B_w.give(it["W"], tk)
        wt, wtt = B_wt.take()
        A.w(wtt, tk)
        tk = A(a.copy(wt[:, 0:it["kn"]], b[:, 0:it["kn"]]))
        PS.give(b, tk)
        it["wt"], it["twt"] = wt, tk

    at_of = {}

    def values(it):
        sm, h, i = it["sm"], it["h"], it["i"]
        vv, tv = heads[h][2]
        if i == 0:
            at_of[h] = B_at.take()
        at, att_ = at_of[h]
        b = bank()
        T.w(it["twt"], tv)
        tk = T(mm_group(b[:, 0:128], lambda j: it["wt"][:, j * 128:j * 128 + 128], lambda j: vv[:, j, :], i + 1))
        B_wt.give(it["wt"], tk)
        if i == 3:
            B_v.give(vv, tk)
        A.w(tk, att_)
        tk = A(a.activation(at[:, i, :], b[:, 0:128], ACT.Square, scale=128.0 ** -0.5, accum_out=sm[:, 10:11]))
        it["tr"] = rstd(sm[:, 11:12], sm[:, 10:11], 1e-5, tk)
        it["b"] = b

    def scaled(it):
        at, att_ = at_of[it["h"]]
        V.w(it["tr"])
        tk = V(v.tensor_scalar(at[:, it["i"], :], it["b"][:, 0:128], it["sm"][:, 11:12], None, MUL))
        PS.give(it["b"], tk)
        B_st.give(it["sm"], tk)
        it["ta"] = tk

    def head_turned(h):
        at, att_ = at_of[h]
        b = bank()
        for i in range(4):
            T.w(items[h * 4 + i]["ta"])
            m = pe.transpose(b[:, i * 128:i * 128 + 128], at[:, i, :], ident)
        tk = T(m)
        B_at.give(at, tk)
        t_att[h] = evac(attT[:, h, :], b[:, :], col("subln_w"), after=tk)
        PS.give(b, t_att[h])

    def attention(n0, n1):
        for n in range(n0, n1):
            for lag, f in ((2, weights_turned), (3, values), (0, scores), (1, weights), (4, scaled)):
                if 0 <= n - lag < 32:
                    f(items[n - lag])
            if n - 5 >= 0 and (n - 5) % 4 == 3:
                head_turned((n - 5) // 4)
            yield

    run(dense_head(0))

    def dense_heads():
        for h in range(1, 8):
            yield from dense_head(h)

    interleave(dense_heads(), 49, attention(0, 28), 28)

    WT = Arena(WK.at, high)
    WS = Arena(work0, WK.at)
    wdt = sb("wdt", [128, 8, 32], stack=WT)
    dt_, da, sp1, sp2, sp3 = (sb(f"dt{i}", [128, NT, 32], stack=WT) for i in range(5))
    aexp = sb("aexp", [128, 32], stack=WT)
    ecum, etail, etot = (sb(f"ec{i}", [128, NT, 32], stack=WT) for i in range(3))
    U = [sb(f"u{i}", [128, 520], stack=WT) for i in range(2)]
    B_acc = bufs("acc", 2, [128, S], WT)

    def pair(name, shape):
        return Pool([sb(name + "0", shape, stack=WT), sb(name + "1", shape, stack=WS)])

    wdt_hi = nc.alloc_sbuf_tensor_at("wdh", [128, 8, 128], F32R, offset=WT.at)
    wdt_lo = nc.alloc_sbuf_tensor_at("wdl", [128, 8, 128], F32R, offset=WT.at + 4096)
    B_x = pair("xs", [128, NT, 256])
    B_z = pair("zs", [128, NT, 256])
    B_BT = pair("BT", [128, S])
    B_CT = pair("CT", [128, S])
    B_Bk = pair("Bk", [128, NT, 128])
    B_R = bufs("R", 2, [128, 4, 128], WS)
    B_E = bufs("E", 2, [128, 4, 128], WS)
    B_cb = bufs("cbm", 2, [128, 128], WS)
    B_xd = bufs("xd", 2, [128, 3, 256], WS)
    B_y = bufs("yy", 2, [128, 2, 256], WS)
    B_yn = bufs("yn", 2, [128, NT, 256], WS)
    B_sta = bufs("sta", 3, [128, 256], WS)
    B_so = bufs("so", 1, [128, 2, S], WS)
    l_so = Lane(sem("s_so"))
    t_spill = [None]
    B_st2 = bufs("st2", 4, [128, 4], WS)

    wl = Lane(sem("s_wdt"))
    t_wdt = wl(nc.gpsimd.dma_start(wdt[:, :, :], wview("w_in", 9216, 32)))
    for u in U:
        t_u0 = V(v.memset(u[:, 0:4], 0.0))
    B_u = Pool(U)

    def setup_ssd():
        b = bank()
        V.w(t_wdt)
        V(v.memset(wdt_hi[:, :, 32:128].bitcast(F32), 0.0))
        V(v.memset(wdt_lo[:, :, 32:128].bitcast(F32), 0.0))
        V(v.tensor_copy(wdt_hi[:, :, 0:32], wdt[:, :, :]))
        tk = V(v.tensor_tensor(wdt_lo[:, :, 0:32], wdt[:, :, :], wdt_hi[:, :, 0:32], SUB))
        T.w(tk)
        tk = T(mm3(b[:, :], lambda k: (wdt_hi[:, k, :], wdt_lo[:, k, :]), lambda k: (hTh[:, k, :], hTl[:, k, :]), 8))
        A.w(tk)
        raw, rt = B_acc.take()
        A.w(tk, rt)
        tk = A(a.copy(raw[0:32, :], b[0:32, :]))
        PS.give(b, tk)
        yield
        b = bank()
        T.w(tk)
        for tt in range(NT):
            m = pe.transpose(b[:, tt * 32:tt * 32 + 32], raw[0:32, tt * 128:tt * 128 + 128], ident[0:32, 0:32])
        tk = T(m)
        B_acc.give(raw, tk)
        V.w(tk)
        bc = lambda x: x.unsqueeze(1).to_broadcast([128, NT, 32])
        tk = V(v.tensor_tensor(sp1[:, :, :], b[:, 0:128].rearrange("p (a b) -> p a b", a=NT), bc(scv("dt_bias")), ADD))
        PS.give(b, tk)
        V(v.tensor_scalar(sp2[:, :, :], sp1[:, :, :], -1.0, None, MUL))
        tk = V(v.tensor_tensor(sp2[:, :, :], sp1[:, :, :], sp2[:, :, :], MIN))
        A.w(tk)
        tk = A(a.activation(sp2[:, :, :], sp2[:, :, :], ACT.Exp))
        tk2 = A(a.activation(aexp[:, :], scv("a_log"), ACT.Exp))
        V.w(tk, tk2)
        V(v.tensor_scalar(sp3[:, :, :], sp2[:, :, :], 2.0, None, ADD))
        V(v.reciprocal(sp3[:, :, :], sp3[:, :, :]))
        V(v.tensor_tensor(sp2[:, :, :], sp2[:, :, :], sp3[:, :, :], MUL))
        V(v.tensor_tensor(sp3[:, :, :], sp2[:, :, :], sp2[:, :, :], MUL))
        V(v.tensor_scalar(dt_[:, :, :], sp3[:, :, :], 2.0 / 17, 2.0 / 15, MUL, ADD))
        for c in (13, 11, 9, 7, 5, 3, 1):
            V(v.tensor_tensor(dt_[:, :, :], dt_[:, :, :], sp3[:, :, :], MUL))
            V(v.tensor_scalar(dt_[:, :, :], dt_[:, :, :], 2.0 / c, None, ADD))
        V(v.tensor_tensor(dt_[:, :, :], dt_[:, :, :], sp2[:, :, :], MUL))
        V(v.scalar_tensor_tensor(dt_[:, :, :], sp1[:, :, :], 0.0, dt_[:, :, :], MAX, ADD))
        tk = V(v.scalar_tensor_tensor(da[:, :, :], dt_[:, :, :], -1.0, bc(aexp[:, :]), MUL, MUL))
        G.w(tk)
        T.w(tk)
        yield
        b = bank()
        daf = da[:, :, :].rearrange("p a b -> p (a b)")
        pe.matmul(b[:, 0:128], cc("tri"), daf, start=True, stop=True)
        pe.matmul(b[:, 128:256], cc("gt"), daf, start=True, stop=True)
        tk = T(pe.matmul(b[:, 256:384], cc("ones"), daf, start=True, stop=True))
        A.w(tk)
        for i, dst in enumerate((ecum, etail, etot)):
            tk = A(a.activation(dst[:, :, :].rearrange("p a b -> p (a b)"), b[:, i * 128:i * 128 + 128], ACT.Exp))
        PS.give(b, tk)
        V.w(tk)
        G.w(tk)
        yield

    groups = {}

    def dense_group(gr):
        xs, xt = B_x.take()
        BT, BTt = B_BT.take()
        CT, CTt = B_CT.take()
        Bk, Bkt = B_Bk.take()
        zs, zt = B_z.take()
        pend = None

        def turn(p):
            src, tk, j = p
            b = bank()
            T.w(tk)
            for tt in range(NT):
                m = pe.transpose(b[:, tt * 128:tt * 128 + 128], src[:, tt * 128:tt * 128 + 128], ident)
            tk = T(m)
            if j != 2:
                B_acc.give(src, tk)
                A.w(tk, xt, zt)
                dst = xs[:, :, j * 128:j * 128 + 128] if j < 2 else zs[:, :, (j - 4) * 128:(j - 3) * 128]
                tk = A(a.copy(dst, b[:, :].rearrange("p (a b) -> p a b", a=NT)))
            else:
                A.w(tk, Bkt)
                tk = A(a.copy(Bk[:, :, :], b[:, :].rearrange("p (a b) -> p a b", a=NT)))
            PS.give(b, tk)
            return tk

        rec = {}
        for j in range(4):
            ch = (gr * 2, gr * 2 + 1, 16 + gr, 24 + gr)[j]
            b, tk, wi = yield from times_h()
            if j == 3:
                release(wi, tk)
            u, ut = B_u.take()
            A.w(ut, tk, t_u0)
            tk = A(a.copy(u[:, 4:516], b[:, :]))
            PS.give(b, tk)
            if j < 2:
                acc, at_ = B_acc.take()
            else:
                acc, at_ = (BT, BTt) if j == 2 else (CT, CTt)
            V.w(tk, at_)
            V(v.tensor_scalar(acc[:, :], u[:, 4:516], conv_col(3, ch), col("conv_b", ch), MUL, ADD))
            for kk in (2, 1, 0):
                tk = V(v.scalar_tensor_tensor(acc[:, :], u[:, 1 + kk:513 + kk], conv_col(kk, ch), acc[:, :], MUL, ADD))
            B_u.give(u, tk)
            A.w(tk)
            tk = A(a.activation(acc[:, :], acc[:, :], ACT.Silu))
            if j == 2:
                rec["BT"] = tk
            if j == 3:
                rec["CT"] = tk
            if pend is not None:
                rec[pend[2]] = turn(pend)
            pend = (acc, tk, j) if j < 3 else None
            yield
        for j in (4, 5):
            b, tk, wi = yield from times_h()
            if j == 5:
                release(wi, tk)
            acc, at_ = B_acc.take()
            A.w(tk, at_)
            tk = A(a.activation(acc[:, :], b[:, :], ACT.Silu))
            PS.give(b, tk)
            if pend is not None:
                rec[pend[2]] = turn(pend)
            pend = (acc, tk, j)
            yield
        rec["z"] = turn(pend)
        groups[gr] = (xs, BT, CT, Bk, zs, rec)

    def scan_group(gr):
        xs, BT, CT, Bk, zs, rec = groups[gr]
        yn, ynt = B_yn.take()
        its = [dict() for _ in range(4)]
        cur = {"s": None, "t": None}
        hs = slice(gr * 4, gr * 4 + 4)
        used = []

        def bc(x, n=64):
            return x.unsqueeze(2).to_broadcast([128, 4, n])

        def v4(x):
            return x.rearrange("p (r q) -> p r q", r=4)

        def ready(c):
            it = its[c]
            R, Rt = B_R.take()
            V.w(Rt)
            it["tR"] = V(v.tensor_tensor(R[:, :, :], cc("tri").unsqueeze(1).to_broadcast([128, 4, 128]),
                                         bc(da[:, c, hs], 128), MUL))
            it["R"] = R

        def inputs(c):
            it = its[c]
            xd, xdt = B_xd.take()
            G.w(xdt, rec[0], rec[1])
            G(g.tensor_tensor(v4(xd[:, 0, :]), v4(xs[:, c, :]), bc(dt_[:, c, hs]), MUL))
            G(g.tensor_tensor(v4(xd[:, 2, :]), v4(xs[:, c, :]), bc(scv("d_skip")[:, hs]), MUL))
            it["txd"] = G(g.tensor_tensor(v4(xd[:, 1, :]), v4(xd[:, 0, :]), bc(etail[:, c, hs]), MUL))
            it["xd"] = xd

        def decays(c):
            it = its[c]
            b = bank()
            T.w(rec["BT"], rec["CT"])
            ck = slice(c * 128, c * 128 + 128)
            tb = T(pe.matmul(b[:, 0:128], BT[:, ck], CT[:, ck], start=True, stop=True))
            b2 = bank()
            T.w(it["tR"])
            ts = T(pe.matmul(b2[:, :], cc("gt"), it["R"][:, :, :].rearrange("p a b -> p (a b)"), start=True, stop=True))
            B_R.give(it["R"], ts)
            cb, cbt = B_cb.take()
            V.w(cbt, tb)
            tc = V(v.tensor_tensor(cb[:, :], b[:, 0:128], cc("tri"), MUL))
            PS.give(b, tc)
            E, Et = B_E.take()
            A.w(Et, ts)
            it["te"] = A(a.activation(E[:, :, :].rearrange("p a b -> p (a b)"), b2[:, :], ACT.Exp))
            PS.give(b2, it["te"])
            it["E"], it["cb"], it["tc"] = E, cb, tc

        def mixing(c):
            it = its[c]
            E, cb = it["E"], it["cb"]
            V.w(it["te"], it["tc"])
            it["tm"] = V(v.tensor_tensor(E[:, :, :], E[:, :, :], cb[:, :].unsqueeze(1).to_broadcast([128, 4, 128]), MUL))
            B_cb.give(cb, it["tm"])

        def outputs(c):
            it = its[c]
            E, xd = it["E"], it["xd"]
            b = bank()
            ck = slice(c * 128, c * 128 + 128)
            if c > 0:
                T.w(cur["t"])
                pe.matmul(b[:, 256:512], CT[:, ck], cur["s"][:, :], start=True, stop=True)
            T.w(it["tm"], it["txd"])
            for r in range(4):
                m = pe.matmul(b[:, r * 64:r * 64 + 64], E[:, r, :], xd[:, 0, r * 64:r * 64 + 64], start=True, stop=True)
            ty = T(m)
            B_E.give(E, ty)
            if c < 3:
                b2 = bank()
                T.w(rec[2])
                ts = T(pe.matmul(b2[:, 0:256], Bk[:, c, :], xd[:, 1, :], start=True, stop=True))
                used.append(ts)
                new, nt = B_sta.take()
                V.w(nt, ts)
                if c == 0:
                    tk = V(v.tensor_copy(new[:, :], b2[:, 0:256]))
                else:
                    V.w(cur["t"])
                    V(v.tensor_tensor(v4(new[:, :]), v4(cur["s"][:, :]), bc(etot[:, c, hs]), MUL))
                    tk = V(v.tensor_tensor(new[:, :], new[:, :], b2[:, 0:256], ADD))
                PS.give(b2, tk)
                if c > 0:
                    B_sta.give(cur["s"], tk, ty)
                cur["s"], cur["t"] = new, tk
            else:
                B_sta.give(cur["s"], ty)
            used.append(ty)
            y, yt = B_y.take()
            V.w(yt, ty, it["txd"])
            V(v.tensor_tensor(y[:, 0, :], b[:, 0:256], xd[:, 2, :], ADD))
            if c > 0:
                V(v.tensor_tensor(v4(y[:, 1, :]), v4(b[:, 256:512]), bc(ecum[:, c, hs]), MUL))
                V(v.tensor_tensor(y[:, 0, :], y[:, 0, :], y[:, 1, :], ADD))
            PS.give(b, V.last())
            B_xd.give(xd, V.last(), ty, it["txd"])
            V.w(rec["z"])
            tk = V(v.tensor_tensor(y[:, 0, :], y[:, 0, :], zs[:, c, :], MUL))
            sm, smt = B_st2.take()
            A.w(tk, smt)
            tk = A(a.activation(y[:, 1, :], y[:, 0, :], ACT.Square, scale=1.0 / 16, accum_out=sm[:, 0:1]))
            it["tr"] = rstd(sm[:, 1:2], sm[:, 0:1], 1e-5, tk)
            it["y"], it["sm"] = y, sm

        def normed(c):
            it = its[c]
            V.w(it["tr"], ynt)
            tk = V(v.tensor_scalar(yn[:, c, :], it["y"][:, 0, :], it["sm"][:, 1:2], None, MUL))
            B_y.give(it["y"], tk)
            B_st2.give(it["sm"], tk)
            it["ty"] = tk

        so, sot = B_so.take()
        for n in range(8):
            for lag, f in ((3, outputs), (1, decays), (1, inputs), (0, ready), (2, mixing), (4, normed)):
                if 0 <= n - lag < 4:
                    f(n - lag)
            yield
        B_x.give(xs, its[3]["txd"])
        B_BT.give(BT, used[-1])
        B_CT.give(CT, used[-1])
        B_Bk.give(Bk, used[-1])
        B_z.give(zs, its[3]["ty"])
        for j in range(2):
            b = bank()
            for c in range(4):
                T.w(its[c]["ty"])
                m = pe.transpose(b[:, c * 128:c * 128 + 128], yn[:, c, j * 128:j * 128 + 128], ident)
            tk = T(m)
            if j == 1:
                B_yn.give(yn, tk)
            tk = evac(so[:, j, :], b[:, :], col("ssd_norm_w", gr * 2 + j), after=[tk, sot])
            PS.give(b, tk)
            SP.w(tk)
        t_spill[0] = l_so(nc.sync.dma_start(ssdd[gr * 256:gr * 256 + 256, :].rearrange("(j p) s -> p j s", p=128),
                                            so[:, :, :]))
        B_so.give(so, t_spill[0])
        yield

    def first():
        yield from setup_ssd()
        yield from dense_group(0)

    interleave(first(), 18, attention(28, 37), 9)
    fence()
    for gr in range(7):
        interleave(dense_group(gr + 1), 12, scan_group(gr), 8)
    run(scan_group(7))
    fence()

    WM = Arena(work0, high)
    X2 = sb("X2", [128, NT, D], stack=WM)
    mT = sb("mT", [128, 8, S], stack=WM)
    WH = Arena(WM.at, high - 16384)
    sga = sb("sga", [128, 4, S], stack=WM)
    B_m2 = bufs("m2", 2, [128, S], WM)
    B_sq = Pool([(sb(f"sq{i}", [128, 4, S], stack=WM), Lane(sem(f"s_sq{i}"))) for i in range(3)])
    assert WM.at <= high - 16384
    H2 = sb("H2", [128, NT, D], stack=WH)
    H2T = sb("H2T", [128, 8, S], stack=WH)
    lx = Lane(sem("s_x2"))
    t_x2 = lx(nc.gpsimd.dma_start(X2[:, :, :], t["x"].rearrange("a (n p) d -> p (a n) d", p=128)))
    WX = Arena(high - 16384, high)
    wrt = sb("wrt", [128, 8, 72], stack=WX)
    frow = sb("frow", [128, D], stack=WX)
    lw = Lane(sem("s_rt"))
    t_rt = lw(nc.gpsimd.dma_start(wrt[:, :, 0:8], wview("w_group_router", 0, 8)))
    t_rt = lw(nc.gpsimd.dma_start(wrt[:, :, 8:72], wview("w_expert_router", 0, 64)))
    t_rt = lw(nc.gpsimd.dma_start(frow[:, :], t["norm_ffn_w"].to_broadcast([128, D])))
    tm_ = [None] * 8

    quarters = []
    G.w(t_spill)

    def load_quarter(q):
        if q < 8:
            (x, lane), tk = B_sq.take()
            G.w(tk)
            src = ssdd[q % 4 * 512:q % 4 * 512 + 512, :].rearrange("(j p) s -> p j s", p=128)
            quarters.append((x, lane, lane(nc.gpsimd.dma_start(x[:, :, :], src))))

    for q in range(3):
        load_quarter(q)

    def gate_part(half, kind):
        for j in range(4):
            b, tk, wi = yield from times_h()
            A.w(tk, sg_free[j])
            sg_tok[j] = A(a.activation(sga[:, j, :], b[:, :], ACT.Sigmoid))
            PS.give(b, sg_tok[j])
            if j == 3:
                release(wi, tk)
            yield

    sg_free = [None] * 4
    sg_tok = [None] * 4

    def attn_part(half):
        state["taken"] = 25 + 5 * half
        w, wt, wi = take(8, 512)
        T.w(wt)
        for j in range(4):
            b = bank()
            tk = T(mm_group(b[:, :], lambda k: w[:, k, j * 128:j * 128 + 128], lambda k: attT[:, k, :], 8))
            f = half * 4 + j
            V.w(tk, sg_tok[j])
            tm_[f] = V(v.tensor_tensor(mT[:, f, :], b[:, :], sga[:, j, :], MUL))
            sg_free[j] = tm_[f]
            PS.give(b, tm_[f])
            yield
        release(wi, tk)

    def ssd_part(half):
        state["taken"] = 27 + 5 * half
        bs = [bank() for _ in range(4)]
        for q in range(4):
            if q % 2 == 0:
                w, wt, wi = take(8, 512)
                T.w(wt)
            x, lane, tq = quarters[half * 4 + q]
            T.w(tq)
            for j in range(4):
                js = slice(j * 128, j * 128 + 128)
                tk = T(mm_group(bs[j][:, :], lambda k: w[:, q % 2 * 4 + k, js], lambda k: x[:, k, :], 4,
                                start=q == 0, stop=q == 3))
                if q == 3:
                    f = half * 4 + j
                    m2, mt = B_m2.take()
                    V.w(tk, sg_tok[j], mt)
                    t1 = V(v.tensor_tensor(m2[:, :], bs[j][:, :], sga[:, j, :], MUL))
                    sg_free[j] = t1
                    PS.give(bs[j], t1)
                    tm_[f] = V(v.tensor_tensor(mT[:, f, :], mT[:, f, :], m2[:, :], ADD))
                    B_m2.give(m2, tm_[f])
            B_sq.give((x, lane), tk)
            load_quarter(half * 4 + q + 3)
            if q % 2:
                release(wi, tk)
            yield

    T.w(t_att)

    for gen in (gate_part(0, 0), attn_part(0), gate_part(0, 1), ssd_part(0)):
        run(gen)
    for gen in (gate_part(1, 0), attn_part(1), gate_part(1, 1), ssd_part(1)):
        run(gen)
    T.w(tm_)
    G.w(sg_free)
    A.w(sg_free, tm_)
    h2d = nc.dram_tensor("h2d", (S, D), F32, kind="Internal").ap()
    h2v = h2d.rearrange("(n p) d -> p n d", p=128)
    lh = Lane(sem("s_h2"))
    tx = [None] * NT
    t_h2, t_h2t, t_h2d = [None] * NT, [None] * NT, [None]

    def out_tile(w, half, tt):
        b = bank()
        tk = T(mm_group(b[:, :], lambda k: mT[:, k, tt * 128:tt * 128 + 128], lambda k: w[:, k, :], 8))
        V.w(tk, t_x2)
        xv = X2[:, tt, half * 512:half * 512 + 512]
        tx[tt] = V(v.tensor_tensor(xv, xv, b[:, :], ADD))
        PS.give(b, tx[tt])
        return tk

    def h2_tile(tt):
        tk = norm_start(H2[:, tt, :], X2, tt, tx[tt], 32)
        V.w(t_rt)
        t_h2[tt] = norm_end(H2, X2, tt, tk, 32, frow[:, :])
        G.w(t_h2[tt])
        t_h2d[0] = lh(nc.gpsimd.dma_start(h2v[:, tt, :], H2[:, tt, :]))

    def logits(tt):
        T.w(t_h2t[tt], t_rt)
        return T(mm_group(bl[:, tt * 72:tt * 72 + 72], lambda k: H2T[:, k, tt * 128:tt * 128 + 128],
                          lambda k: wrt[:, k, :], 8))

    state["taken"] = 34
    w, wt, wi = take(8, 512)
    T.w(wt)
    for tt in range(NT):
        tk = out_tile(w, 0, tt)
    release(wi, tk)
    w, wt, wi = take(8, 512)
    T.w(wt)
    bl = bank()
    for tt in range(NT + 2):
        if tt < NT:
            tk = out_tile(w, 1, tt)
            h2_tile(tt)
        if tt == NT - 1:
            release(wi, tk)
        if 0 <= tt - 1 < NT:
            t_h2t[tt - 1] = turn_tile(H2T, H2, tt - 1, t_h2[tt - 1])
        if 0 <= tt - 2 < NT:
            t_log = logits(tt - 2)
    fence()

    RA = Arena(region_a, region_a + 65536)
    WR = Arena(work0 + 16384, work0 + 32768)
    for i in range(4):
        ring.append(sb(f"ringx{i}", [128, 4096], stack=RA))
        rlane.append(Lane(sem(f"s_ringx{i}")))
        slots.append((RING + i, None))
        SP.w(V.last(), A.last(), T.last(), G.last())
        issue()
    EB = 64 + NOV
    sidx = sb("sidx", [128, EB], I32, stack=WR)
    gidx = sb("gidx", [128, EB], I32, stack=WR)
    wts = sb("wts", [128, NT, 2], stack=WR)
    work1 = WR.at
    L = sb("L", [128, NT, 72], stack=WR)
    ra = sb("ra", [128, NT, 64], stack=WR)
    rc = sb("rc", [128, 2, NT, 64], stack=WR)
    rb = sb("rb", [128, NT, 64], stack=WR)
    OO = sb("OO", [128, 2, NT, 64], stack=WR)
    O = [OO[:, k, :, :] for k in range(2)]
    PF = sb("PF", [128, NT, 64], stack=WR)
    AS = sb("AS", [128, NT, 64], stack=WR)
    s8 = sb("s8", [128, 12, NT, 8], stack=WR)
    s4 = sb("s4", [128, 16, NT], stack=WR)
    s2k = sb("s2k", [128, 8, 8], stack=WR)
    e64 = sb("e64", [128, 6, 64], stack=WR)
    oR = sb("oR", [128, 3, 128], stack=WR)
    oB = sb("oB", [128, 3, EB], stack=WR)
    ybuf = nc.dram_tensor("ybuf", (2 * S, D), F32, kind="Internal").ap()

    for i in range(2):
        ring.append(nc.alloc_sbuf_tensor_at(f"ringy{i}", [128, 4096], F32, offset=work0 + 38912 + i * 16384))
        rlane.append(Lane(sem(f"s_ringy{i}")))
        slots.append((RING + 4 + i, [t_log, V.last(), A.last(), t_h2d[0]]))
        issue()
    b, tk = bl, t_log
    V.w(tk)
    bv = b[:, 0:288].rearrange("p (a b) -> p a b", a=NT)
    V(v.tensor_tensor(L[:, :, 0:8], bv[:, :, 0:8], scv("b_group_router").unsqueeze(1).to_broadcast([128, NT, 8]), ADD))
    tk = V(v.tensor_tensor(L[:, :, 8:72], bv[:, :, 8:72],
                           scv("b_expert_router").unsqueeze(1).to_broadcast([128, NT, 64]), ADD))
    PS.give(b, tk)

    def up8(x):
        return x.unsqueeze(2).to_broadcast([128, NT, 8])

    iota8m = cc("iota8m").unsqueeze(1).to_broadcast([128, NT, 8])

    def first_max(src, mx, hot, tmp):
        V(v.tensor_reduce(mx, src, AX.X, MAX))
        V(v.tensor_tensor(hot, src, up8(mx), EQ))
        V(v.tensor_scalar(hot, hot, -1000.0, 1000.0, MUL, ADD))
        V(v.tensor_tensor(hot, hot, iota8m, ADD))
        V(v.tensor_reduce(tmp, hot, AX.X, MIN))
        return V(v.tensor_tensor(hot, iota8m, up8(tmp), EQ))

    gm, tmp, v1, v2, gate, w1c, w2c = (s4[:, i, :] for i in range(7))
    gh, es, h1, h2_, e2, ex = (s8[:, i, :, :] for i in range(6))
    first_max(L[:, :, 0:8], gm, gh, tmp)
    tk = V(v.tensor_tensor(ex, L[:, :, 0:8], up8(gm), SUB))
    A.w(tk)
    tk = A(a.activation(ex, ex, ACT.Exp))
    V.w(tk)
    V(v.tensor_reduce(gate, ex, AX.X, ADD))
    V(v.reciprocal(gate, gate))
    EL = L[:, :, 8:72].rearrange("p t (g j) -> p t g j", g=8)
    for tt in range(NT):
        V(v.tensor_tensor(ra[:, tt, :].rearrange("p (g j) -> p g j", g=8), EL[:, tt, :, :],
                          gh[:, tt, :].unsqueeze(2).to_broadcast([128, 8, 8]), MUL))
        V(v.tensor_reduce(es[:, tt, :], ra[:, tt, :].rearrange("p (g j) -> p j g", g=8), AX.X, ADD))
    first_max(es, v1, h1, tmp)
    V(v.scalar_tensor_tensor(e2, h1, -BIG, es, MUL, ADD))
    first_max(e2, v2, h2_, tmp)
    tk = V(v.tensor_tensor(w2c, v2, v1, SUB))
    A.w(tk)
    tk = A(a.activation(w2c, w2c, ACT.Exp))
    V.w(tk)
    V(v.tensor_scalar(w1c, w2c, 1.0, None, ADD))
    V(v.reciprocal(w1c, w1c))
    V(v.tensor_tensor(w1c, w1c, gate, MUL))
    V(v.tensor_tensor(w2c, w2c, w1c, MUL))
    V(v.tensor_copy(wts[:, :, 0], w1c))
    V(v.tensor_copy(wts[:, :, 1], w2c))
    for k, hot in ((0, h1), (1, h2_)):
        for tt in range(NT):
            V(v.tensor_tensor(O[k][:, tt, :].rearrange("p (g j) -> p g j", g=8),
                              gh[:, tt, :].unsqueeze(2).to_broadcast([128, 8, 8]),
                              hot[:, tt, :].unsqueeze(1).to_broadcast([128, 8, 8]), MUL))
    tk = V(v.tensor_tensor(AS[:, :, :], O[0][:, :, :], O[1][:, :, :], ADD))
    T.w(tk)
    V(v.tensor_copy(PF[:, 0, :], AS[:, 0, :]))
    for tt in range(1, NT):
        tk = V(v.tensor_tensor(PF[:, tt, :], PF[:, tt - 1, :], AS[:, tt, :], ADD))
    b = bank()
    asf = AS[:, :, :].rearrange("p a b -> p (a b)")
    pff = PF[:, :, :].rearrange("p a b -> p (a b)")
    pe.matmul(b[:, 0:64], cc("lt"), asf[:, 0:64], start=True, stop=True)
    pe.matmul(b[:, 64:256], cc("lt"), asf[:, 64:256], start=True, stop=False)
    T.w(tk)
    pe.matmul(b[:, 64:256], cc("ones"), pff[:, 0:192], start=False, stop=True)
    tk = T(pe.matmul(b[:, 256:320], cc("ones"), pff[:, 192:256], start=True, stop=True))
    V.w(tk)
    V(v.tensor_copy(rb[:, :, :].rearrange("p a b -> p (a b)"), b[:, 0:256]))
    cnt = e64[:, 0, :]
    tk = V(v.tensor_copy(cnt, b[:, 256:320]))
    PS.give(b, tk)
    nov = e64[:, 1, :]
    rcf = rc[:, :, :, :].rearrange("p a b c -> p (a b) c")
    steps = cc("ovid")[:, 0:8].unsqueeze(1)
    V(v.tensor_scalar(e64[:, 2, :], cnt, -float(CAP), 1.0 / 64, ADD, MUL))
    V(v.tensor_tensor(rcf.rearrange("p a b -> p (a b)").rearrange("p (e j) -> p e j", j=8),
                      e64[:, 2, :].unsqueeze(2).to_broadcast([128, 64, 8]), steps.to_broadcast([128, 64, 8]), GT))
    V(v.tensor_reduce(nov, rcf.rearrange("p a b -> p (a b)").rearrange("p (e j) -> p e j", j=8), AX.X, ADD))
    inc, alt = e64[:, 3, :], e64[:, 4, :]
    V(v.tensor_copy(inc, nov))
    d = 1
    while d < 64:
        V(v.tensor_copy(alt[:, 0:d], inc[:, 0:d]))
        V(v.tensor_tensor(alt[:, d:64], inc[:, d:64], inc[:, 0:64 - d], ADD))
        inc, alt = alt, inc
        d *= 2
    exc = e64[:, 5, :]
    V(v.tensor_tensor(exc, inc, nov, SUB))
    b = bank()
    oof = OO[:, :, :, :].rearrange("p a b c -> p (a b) c")
    rank, eid, ovs, over, hi, pos, blk, t8 = (s2k[:, i, :] for i in range(8))
    for k in range(2):
        V(v.tensor_tensor(rc[:, k, :, :], O[k], rb[:, :, :], MUL))
    V(v.tensor_reduce(rank, rcf, AX.X, ADD))
    for dst, other in ((eid, cc("iota64")), (ovs, exc)):
        V(v.tensor_tensor(rcf, oof, other.unsqueeze(1).to_broadcast([128, 8, 64]), MUL))
        V(v.tensor_reduce(dst, rcf, AX.X, ADD))
    V(v.tensor_scalar(over, rank, float(CAP), None, GE))
    V(v.tensor_scalar(t8, rank, -float(CAP), 1.0 / 64, ADD, MUL))
    r64 = rcf[:, :, 0:7]
    V(v.tensor_tensor(r64, t8.unsqueeze(2).to_broadcast([128, 8, 7]),
                      cc("ovid")[:, 1:8].unsqueeze(1).to_broadcast([128, 8, 7]), GE))
    V(v.tensor_reduce(hi, r64, AX.X, ADD))
    V(v.scalar_tensor_tensor(pos, over, -float(CAP), rank, MUL, ADD))
    V(v.scalar_tensor_tensor(pos, hi, -64.0, pos, MUL, ADD))
    V(v.tensor_tensor(ovs, ovs, hi, ADD))
    V(v.tensor_scalar(ovs, ovs, 64.0, None, ADD))
    V(v.tensor_tensor(ovs, ovs, eid, SUB))
    V(v.tensor_tensor(ovs, ovs, over, MUL))
    V(v.tensor_tensor(blk, eid, ovs, ADD))
    V(v.tensor_scalar(t8, blk, -64.0, None, ADD))
    t_r = [None] * 3
    for n in range(8):
        k, tt, r = n // NT, n % NT, n % 3
        aid = cc("aid1")[:, tt * 2 + k:tt * 2 + k + 1]
        V.w(t_r[r])
        V(v.tensor_scalar(oR[:, r, :], cc("iota64x2"), pos[:, n:n + 1], None, EQ))
        V(v.tensor_scalar(oB[:, r, 0:64], cc("iota64"), blk[:, n:n + 1], aid, EQ, MUL))
        tk = V(v.tensor_scalar(oB[:, r, 64:EB], cc("ovid")[:, 0:NOV], t8[:, n:n + 1], aid, EQ, MUL))
        T.w(tk)
        t_r[r] = T(pe.matmul(b[:, 0:EB], oR[:, r, :], oB[:, r, :], start=n == 0, stop=n == 7))
    V.w(t_r)
    tabf = oB[:, 0, :]
    tab2 = oB[:, 1, :]
    V(v.tensor_copy(tabf, b[:, 0:EB]))
    PS.give(b, V.last())
    V(v.tensor_scalar(tab2, tabf, 0.5, 5001.0, LE, MUL))
    V(v.tensor_tensor(tabf, tabf, tab2, ADD))
    V(v.tensor_scalar(tabf, tabf, -1.0, None, ADD))
    V(v.tensor_scalar(tab2, tabf, 2.0, cc("jcol"), MUL, ADD))
    V(v.tensor_copy(sidx[:, :], tab2))
    V(v.tensor_scalar(tab2, tabf, 512.0, -512.0, GE, MUL))
    V(v.tensor_tensor(tabf, tabf, tab2, ADD))
    V(v.tensor_scalar(tab2, tabf, 2.0, cc("jcol"), MUL, ADD))
    t_idx = V(v.tensor_copy(gidx[:, :], tab2))
    G.w(t_h2d, t_idx)
    V.w(t_h2d)
    V(v.tensor_copy(ovn[:, 15:16], inc[:, 63:64]))
    bigc = AS[:, :, :].rearrange("p a b -> p (a b)")
    for o0 in range(0, NOV, 4):
        n = min(4, NOV - o0)
        c4 = bigc[:, 0:n * 64].rearrange("p (a b) -> p a b", a=n)
        V(v.tensor_tensor(c4, inc.unsqueeze(1).to_broadcast([128, n, 64]),
                          cc("ovid")[:, o0:o0 + n].unsqueeze(2).to_broadcast([128, n, 64]), LE))
        V(v.tensor_reduce(st[:, 48 + o0:48 + o0 + n], c4, AX.X, ADD))
    V(v.tensor_scalar(st[:, 48:48 + NOV], st[:, 48:48 + NOV], 63.0, None, MIN))
    t_ovn = V(v.tensor_copy(ovn[:, 0:NOV], st[:, 48:48 + NOV]))
    fence()

    WE = Arena(work1, work0 + 38912)
    WF = Arena(high - 10240, high)
    nrow_ = sb("fnrow", [128, D], stack=WF)
    wuq = sb("wuq", [128, 2, 384], stack=WF)
    wukv = sb("wukv", [128, 512], stack=WF)
    mrow = sb("mrow", [128, 2, 96], stack=WF)
    lm = Lane(sem("s_mla"))
    t_ml = lm(nc.gpsimd.dma_start(wuq[:, :, :], wview("mla_w_uq_2", 0, 384)))
    t_ml = lm(nc.gpsimd.dma_start(wukv[:, :], t["mla_w_ukv_2"].rearrange("a p n -> (a p) n")))
    t_ml = lm(nc.gpsimd.dma_start(mrow[:, 0, :], t["mla_q_g_2"].to_broadcast([128, 96])))
    t_ml = lm(nc.gpsimd.dma_start(mrow[:, 1, :], t["mla_k_g_2"].to_broadcast([128, 96])))
    lf = Lane(sem("s_fn"))
    t_f = lf(nc.gpsimd.dma_start(nrow_[:, :], t["final_norm_w"].unsqueeze(0).to_broadcast([128, D])))
    h2r = h2d.rearrange("t (j c) -> (t j) c", j=2)
    ybr = ybuf.rearrange("t (j c) -> (t j) c", j=2)
    gxs = [sb(f"gx{i}", [128, 512], stack=WE) for i in range(3)]
    gxTs = [sb(f"gxT{i}", [128, 4, 128], stack=WE) for i in range(2)]
    sgs = [sb(f"sg{i}", [128, 256], stack=WE) for i in range(2)]
    hids = [sb(f"hid{i}", [128, 256], stack=WE) for i in range(2)]
    hidTs = [sb(f"hidT{i}", [128, 2, 128], stack=WE) for i in range(2)]
    ys = [sb(f"ys{i}", [128, 512], stack=WE) for i in range(2)]
    glane = [Lane(sem(f"s_gx{i}")) for i in range(3)]
    ylane = [Lane(sem(f"s_y{i}")) for i in range(2)]
    for x in gxs:
        t_gz = V(v.memset(x[:, :], 0.0))
    G.w(t_gz)

    def expert_run(n, col0, takew, give, glane, ylane, third=None):
        P_gx = Pool([(x, l) for x, l in zip(gxs, glane)])
        P_gxT, P_sg, P_hid, P_hidT = Pool(gxTs), Pool(sgs), Pool(hids), Pool(hidTs)
        P_y = Pool([(x, l) for x, l in zip(ys, ylane)])
        gath, its = {}, {}

        def gather(e):
            if e >= n:
                return
            (x, lane), tk = P_gx.take()
            G.w(tk)
            gath[e] = (x, lane, lane(g.indirect_dma_start(
                out=x[:, :], out_offset=None, in_=h2r[:, :],
                in_offset=bass.IndirectOffsetOnAxis(ap=gidx[:, col0 + e:col0 + e + 1].bitcast(U32), axis=0),
                bounds_check=2 * S - 1, oob_is_err=False)))

        def turn(e):
            if e >= n:
                return
            x, lane, tk = gath[e]
            T.w(tk)
            xT, xt = P_gxT.take()
            b = bank()
            for q in range(4):
                m = pe.transpose(b[:, q * 128:q * 128 + 128], x[:, q * 128:q * 128 + 128], ident)
            tk = T(m)
            V.w(tk, xt)
            t0 = V(v.tensor_copy(xT[:, :, :].rearrange("p a b -> p (a b)"), b[:, :]))
            PS.give(b, t0)
            P_gx.give((x, lane), tk)
            gather(e + 3)
            its[e] = (xT, [t0])

        def up(e):
            if e >= n:
                return
            xT, tks = its[e]
            T.w(tks)
            ps = []
            for j in range(2):
                w, wt, wi = takew(8, 512)
                T.w(wt)
                b = bank()
                for k in range(8):
                    for c in range(2):
                        m = pe.matmul(b[c * 64:c * 64 + 64, 0:256], xT[:, k % 4, k // 4 * 64:k // 4 * 64 + 64],
                                      w[:, k, c * 256:c * 256 + 256], start=k == 0, stop=k == 7)
                tk = T(m)
                give(wi, tk)
                ps.append((b, tk))
            P_gxT.give(xT, tk)
            s, stk = P_sg.take()
            h, htk = P_hid.take()
            A.w(ps[0][1], stk)
            tk = A(a.activation(s[:, :], ps[0][0][:, 0:256], ACT.Silu))
            PS.give(ps[0][0], tk)
            V.w(tk, ps[1][1], htk)
            tk = V(v.tensor_tensor(h[:, :], ps[1][0][:, 0:256], s[:, :], MUL))
            PS.give(ps[1][0], tk)
            P_sg.give(s, tk)
            its[e] = (h, tk)

        def down(e):
            if e < 0:
                return
            h, tk = its[e]
            T.w(tk)
            b = bank()
            for j in range(2):
                m = pe.transpose(b[:, j * 128:j * 128 + 128], h[:, j * 128:j * 128 + 128], ident)
            tk = T(m)
            P_hid.give(h, tk)
            hT_, ht = P_hidT.take()
            V.w(tk, ht)
            tk = V(v.tensor_copy(hT_[:, :, :].rearrange("p a b -> p (a b)"), b[:, 0:256]))
            PS.give(b, tk)
            T.w(tk)
            w, wt, wi = takew(4, 1024)
            T.w(wt)
            (y, lane), yt = P_y.take()
            b = bank()
            for k in range(4):
                for c in range(2):
                    m = pe.matmul(b[c * 64:c * 64 + 64, :], hT_[:, k % 2, k // 2 * 64:k // 2 * 64 + 64],
                                  w[:, k, c * 512:c * 512 + 512], start=k == 0, stop=k == 3)
            tk = T(m)
            A.w(tk, yt)
            tks = A(a.copy(y[:, :], b[:, :]))
            PS.give(b, tks)
            give(wi, tk)
            P_hidT.give(hT_, tk)
            G.w(tks)
            tk = lane(g.indirect_dma_start(
                out=ybr[:, :],
                out_offset=bass.IndirectOffsetOnAxis(ap=sidx[:, col0 + e:col0 + e + 1].bitcast(U32), axis=0),
                in_=y[:, :], in_offset=None, bounds_check=4 * S - 1, oob_is_err=False))
            P_y.give((y, lane), tk)

        for e in range(3):
            gather(e)
        turn(0)
        for e in range(n + 1):
            if e == 2 and third is not None:
                third()
            up(e)
            turn(e + 1)
            down(e - 1)
        return [(lane.sem, lane.n) for lane in list(glane) + list(ylane)]

    ov_reg = []

    def read_overflow():
        for e in (V, A, T, G, SP):
            e.w(t_ovn)
        ov_reg.append(nc.values_load(ovn[0:1, 15:16], min_val=0, max_val=NOV))

    t_y = expert_run(64, 0, take, release, glane, ylane, read_overflow)

    for e in (V, A, T, G, SP):
        e.w(t_y)
    fence()
    SP.w(V.last(), A.last(), T.last(), G.last())
    ovr = ov_reg[0]
    saved = (V, A, T, G, SP, PS)
    with nc.If(ovr > 0):
        V = Engine(nc.vector, sem("s_dve2"))
        A = Engine(nc.scalar, sem("s_act2"))
        T = Engine(nc.tensor, sem("s_pe2"), serial=False)
        G = Engine(nc.gpsimd, sem("s_pool2"))
        SP = Engine(nc.sync, sem("s_sp2"))
        PS = Pool(banks)
        ob = ring[RING:RING + 1]
        olane = Lane(sem("s_ob"))
        ostate = {"n": 0, "free": None}

        def otake(k, n):
            i = ostate["n"]
            ostate["n"] = i + 1
            order = []
            for e in range(NOV + 1):
                if e < NOV:
                    order += [("w_expert_gate", e), ("w_expert_up", e)]
                if e > 0:
                    order.append(("w_expert_down", e - 1))
            name, e = order[i]
            SP.w(ostate["free"])
            er = nc.sync.value_load(ovn[0:1, e:e + 1], min_val=0, max_val=63)
            src = t[name].rearrange("a e (k p) n -> p (a e) k n", p=128)[:, bass.ds(er, 1), :, :]
            dst = ob[0][:, 0:k * n].rearrange("p (e k n) -> p e k n", k=k, e=1)
            tk = olane(nc.sync.dma_start(dst, src))
            return ob[0][:, 0:k * n].rearrange("p (k n) -> p k n", k=k), tk, i

        def ogive(i, tk):
            ostate["free"] = [tk]

        gl2 = [Lane(sem(f"s_gz{i}")) for i in range(3)]
        yl2 = [Lane(sem(f"s_yz{i}")) for i in range(2)]
        ty2 = expert_run(NOV, 64, otake, ogive, gl2, yl2)
        for e in (V, A, T, G, SP):
            e.w(ty2)
        fence()
        SP.w(V.last(), A.last(), T.last(), G.last())
    V, A, T, G, SP, PS = saved
    PS = Pool(banks)
    A.w(V(v.memset(st[:, 20:21], 0.0)))
    A(a.copy(st[:, 21:22], st[:, 20:21]))
    T(pe.matmul(banks[0][:, 0:1], ident, ident[:, 0:1], start=True, stop=True))
    G(g.memset(st[:, 23:24], 0.0))
    fence()

    WC = Arena(work1, high)
    Y = [sb(f"Y{k}", [128, NT, D], stack=WC) for k in range(2)]
    ly = [Lane(sem(f"s_cy{k}")) for k in range(NT)]
    t_c = []
    for tt in range(NT):
        for k in range(2):
            tk = ly[tt](nc.gpsimd.dma_start(Y[k][:, tt, :], ybuf[k * S + tt * 128:k * S + tt * 128 + 128, :]))
        t_c.append(tk)
    state["limit"] = len(chunks)
    SP.w(t_c[1])
    issue()
    SP.w(t_c[3])
    issue()
    issue()
    A1 = sb("A1", [128, NT, D], stack=Arena(region_a, region_a + 65536))
    RB = Arena(region_a + 16384, region_a + 65536)
    g1_at = RB.take([128, 4096])
    G1 = [nc.alloc_sbuf_tensor_at("G1h", [128, 8, S], F32R, offset=g1_at), None]
    qlT = sb("qlT", [128, 2, S], stack=RB)
    kvT = sb("kvT", [128, S], stack=RB)
    ss2 = sb("ss2", [128, NT, 24], stack=RB)
    rs2 = sb("rs2", [128, NT, 24], stack=RB)
    mh2 = sb("mh2", [128, NT, 24], stack=RB)
    sm3 = sb("sm3", [128, 4, 16], stack=RB)
    stm = sb("stm", [128, 16, 8], stack=RB)
    RT = Arena(RB.at, region_a + 65536)
    G1[1] = sb("G1l", [128, 8, S], F32R, stack=RT)
    h2b = [sb(f"h2b{i}", [128, 1024], F32R, stack=RT) for i in range(2)]
    h2b += [nc.alloc_sbuf_tensor_at(f"h2b{i + 2}", [128, 1024], F32R, offset=region_a + i * 4096) for i in range(2)]
    B_h2 = Pool(h2b[0:2])
    B_t1 = bufs("t1_", 2, [128, S], Arena(work0 + 57344, high))

    def turn_split(dst, src, tt, tok, name, pool):
        T.w(tok)
        parts = []
        for i in range(2):
            b = bank()
            for k in range(4):
                m = pe.transpose(b[:, k * 128:k * 128 + 128], src[:, tt, (i * 4 + k) * 128:(i * 4 + k) * 128 + 128], ident)
            tk = T(m)
            r = rows_at[name] + i * 4
            u, ut = pool.take()
            uv = u[:, :].rearrange("p (k c) -> p k c", k=4)
            V.w(tk, ut)
            tk = V(v.tensor_tensor(uv, b[:, :].rearrange("p (k c) -> p k c", k=4),
                                   vcol[:, r:r + 4].unsqueeze(2).to_broadcast([128, 4, 128]), MUL))
            PS.give(b, tk)
            d = slice(i * 4, i * 4 + 4), slice(tt * 128, tt * 128 + 128)
            A.w(tk)
            parts.append((u, uv, d, A(a.copy(dst[0][:, d[0], d[1]], uv))))
        outs = []
        for u, uv, d, tk in parts:
            V.w(tk)
            tk = V(v.tensor_tensor(dst[1][:, d[0], d[1]], uv, dst[0][:, d[0], d[1]], SUB))
            pool.give(u, tk)
            outs.append(tk)
        return outs

    seq2 = [(c, q) for c in range(5) for q in range(4)]
    ready2, half2 = [], []

    def split2():
        if half2:
            blk = half2.pop(0)
            V.w(blk["th"], slot_tok[blk["i"]])
            blk["tok"] = V(v.tensor_tensor(blk["lo"], blk["raw"], blk["hi"], SUB))
            ready2.append(blk)
        if seq2 and n_moe_end + seq2[0][0] in slot_of and B_h2.free:
            c, q = seq2.pop(0)
            i, n = n_moe_end + c, min(512, 2464 - c * 512)
            r = slot_of[i]
            hb, ht = B_h2.take()
            cs = slice(q * 2 * n, q * 2 * n + 2 * n)
            raw, lo = ring[r][:, cs], rview[r][:, cs]
            A.w(slot_tok[i], ht)
            half2.append({"i": i, "hb": hb, "hi": hb[:, 0:2 * n], "raw": raw, "lo": lo, "n": n,
                          "th": A(a.copy(hb[:, 0:2 * n], raw))})
            return True
        return False

    V.w(t_f)
    r1, r2, t_x3, tn = {}, {}, [], []
    t_h = []
    for n in range(NT + 3):
        if n < NT:
            V.w(t_c[n])
            for k in range(2):
                tk = V(v.scalar_tensor_tensor(X2[:, n, :], Y[k][:, n, :], wts[:, n, k:k + 1], X2[:, n, :], MUL, ADD))
            r1[n] = norm_start(A1[:, n, :], X2, n, tk, 64)
        if 0 <= n - 1 < NT:
            t_x3.append(norm_end(X2, X2, n - 1, r1[n - 1], 64, nrow_[:, :]))
            r2[n - 1] = norm_start(A1[:, n - 1, :], X2, n - 1, t_x3[-1], 72)
        if 0 <= n - 2 < NT:
            tn.append(norm_end(A1, X2, n - 2, r2[n - 2], 72))
        if n == 3:
            split2()
            split2()
        if 0 <= n - 3 < NT:
            t_h += turn_split(G1, A1, n - 3, tn[n - 3], "attn_norm_g_2", B_t1)
        if n - 3 in (0, 1):
            B_h2.give(h2b[n - 1], T.last())
    fence()

    WB = Arena(work0 + 16384, high)
    P2 = sb("P2", [128, NT, 2464], stack=WB)
    QT = sb("QT", [128, 11, S], stack=WB)
    RT = Arena(RB.at, region_a + 65536)
    vm = sb("vm", [128, NT, 256], stack=RT)
    B_QK = bufs("QK", 2, [128, 8, 96], RT)
    lsq = A1[:, 2, :]
    t_mh = V(v.memset(mh2[:, :, :], -0.5))
    T.w(t_h)
    A.w(t_h)
    SEG = ((0, 8), (1184, 8), (1952, 6))
    done2 = []

    def project(c0, after={}):
        bs = [bank() for _ in range(NT)]
        for q in range(4):
            while not ready2:
                split2()
            blk = ready2.pop(0)
            while len(ready2) + len(half2) < 3 and split2():
                pass
            n = blk["n"]
            vh, vl = (x.rearrange("p (k n) -> p k n", k=2) for x in (blk["hi"], blk["lo"]))
            T.w(blk["tok"])
            for tt in range(NT):
                tk = T(mm3(bs[tt][:, 0:n], lambda k: (G1[0][:, 2 * q + k, tt * 128:tt * 128 + 128],
                                                      G1[1][:, 2 * q + k, tt * 128:tt * 128 + 128]),
                           lambda k: (vh[:, k, :], vl[:, k, :]), 2, start=q == 0, stop=q == 3))
                if q == 3:
                    tk2 = evac(P2[:, tt, c0:c0 + n], bs[tt][:, 0:n], after=tk)
                    PS.give(bs[tt], tk2)
                    done2.append(tk2)
            B_h2.give(blk["hb"], tk)
            for f in after.get(q, ()):
                f()
        release(blk["i"], tk)

    def heads_view(tt, c0, n):
        return P2[:, tt, c0:c0 + n * 64].rearrange("p (h c) -> p h c", h=n)

    def root(cols, scale):
        tk = V(v.tensor_scalar(ss2[:, :, cols], ss2[:, :, cols], scale, 1e-6, MUL, ADD))
        G.w(tk, t_mh)
        tk = G(g.tensor_tensor(rs2[:, :, cols], ss2[:, :, cols], mh2[:, :, cols], ALU.pow))
        V.w(tk)

    def heads_squares(si, tiles):
        c0, n = SEG[si]
        o = si * 8
        for tt in tiles:
            sq = P2[:, tt, 768:1152] if si == 2 else A1[:, 3, :]
            V(v.tensor_tensor(sq[:, 0:n * 64], P2[:, tt, c0:c0 + n * 64], P2[:, tt, c0:c0 + n * 64], MUL))
            V(v.tensor_reduce(ss2[:, tt, o:o + n], sq[:, 0:n * 64].rearrange("p (h c) -> p h c", h=n), AX.X, ADD))

    def heads_root(si):
        cols = slice(si * 8, si * 8 + SEG[si][1])
        tk = V(v.tensor_scalar(ss2[:, :, cols], ss2[:, :, cols], 1.0 / 64, 1e-6, MUL, ADD))
        G.w(tk, t_mh)
        return G(g.tensor_tensor(rs2[:, :, cols], ss2[:, :, cols], mh2[:, :, cols], ALU.pow))

    def heads_scaled(si, tt, tk):
        c0, n = SEG[si]
        o = si * 8
        V.w(tk)
        hv, oo, nn = heads_view(tt, c0, n), o, n
        if si == 2:
            sq = P2[:, tt, 768:1152]
            V(v.tensor_scalar(sq[:, 0:64], hv[:, 1, :], rs2[:, tt, o + 1:o + 2], None, MUL))
            V(v.tensor_scalar(hv[:, 1, :], hv[:, 2, :], rs2[:, tt, o + 2:o + 3], None, MUL))
            V(v.tensor_copy(hv[:, 2, :], sq[:, 0:64]))
            V(v.tensor_scalar(hv[:, 0, :], hv[:, 0, :], rs2[:, tt, o:o + 1], None, MUL))
            hv, oo, nn = hv[:, 3:6, :], o + 3, 3
        return V(v.tensor_tensor(hv, hv, rs2[:, tt, oo:oo + nn].unsqueeze(2).to_broadcast([128, nn, 64]), MUL))

    def latent_squares():
        A.w(done2, t_h)
        for tt in range(NT):
            A(a.activation(lsq[:, 0:256], P2[:, tt, 768:1024], ACT.Square, scale=0.5, accum_out=ss2[:, tt, 22:23]))
            tk = A(a.activation(lsq[:, 256:384], P2[:, tt, 1024:1152], ACT.Square, scale=0.5 ** 0.5,
                                accum_out=ss2[:, tt, 23:24]))
        norm["ls"] = tk

    def latent_root():
        V.w(norm["ls"])
        tk = V(v.tensor_scalar(ss2[:, :, 22:24], ss2[:, :, 22:24], 1.0 / 64, 1e-6, MUL, ADD))
        G.w(tk, t_mh)
        norm["lr"] = G(g.tensor_tensor(rs2[:, :, 22:24], ss2[:, :, 22:24], mh2[:, :, 22:24], ALU.pow))

    def latent_scaled():
        V.w(norm["lr"], done2)
        for tt in range(NT):
            V(v.tensor_scalar(P2[:, tt, 768:1024], P2[:, tt, 768:1024], rs2[:, tt, 22:23], None, MUL))
            nl.append(V(v.tensor_scalar(P2[:, tt, 1024:1152], P2[:, tt, 1024:1152], rs2[:, tt, 23:24], None, MUL)))

    def turn4(dst, src, scol, toks):
        b = bank()
        for tt in range(NT):
            T.w(toks[tt])
            m = pe.transpose(b[:, tt * 128:tt * 128 + 128], src(tt), ident)
        tk = T(m)
        tk = evac(dst, b[:, :], scol, after=tk)
        PS.give(b, tk)
        return tk

    t_l, t_qt = [], []

    def turn_heads(base, c0, names, toks):
        for i, name in enumerate(names):
            t_qt.append(turn4(QT[:, base + i, :], lambda tt: P2[:, tt, c0 + i * 128:c0 + i * 128 + 128], col(name), toks))

    norm, nl, n0, n1 = {}, [], [], []

    def squares(si, *tiles):
        def f():
            V.w(done2, t_h)
            heads_squares(si, tiles)
            if tiles[-1] == NT - 1:
                norm[si] = heads_root(si)
        return f

    def scaled(si, toks, *tiles):
        def f():
            for tt in tiles:
                toks.append(heads_scaled(si, tt, norm[si]))
        return f

    def turned_latents():
        for k in range(2):
            t_l.append(turn4(qlT[:, k, :], lambda tt: P2[:, tt, 768 + k * 128:896 + k * 128], col("mla_qlat_g_2", k), nl))
        t_l.append(turn4(kvT[:, :], lambda tt: P2[:, tt, 1024:1152], col("mla_kvlat_g_2"), nl))

    MOBA = (0, 0, ("moba_q_g_2", "moba_q_g_2", "moba_k_g_2", "moba_k_g_2"))
    DIL = (4, 1184, ("dil_q_g_2", "dil_q_g_2", "dil_k_g_2", "dil_k_g_2"))
    project(0)
    project(512, {0: [squares(0, 0, 1)], 1: [squares(0, 2, 3)], 2: [scaled(0, n0, 0, 1)], 3: [scaled(0, n0, 2, 3)]})
    project(1024, {1: [lambda: turn_heads(*MOBA, n0)]})
    project(1536, {0: [latent_squares], 1: [latent_root], 2: [latent_scaled]})
    project(2048, {0: [turned_latents, squares(1, 0, 1)], 1: [squares(1, 2, 3)], 2: [scaled(1, n1, 0, 1)],
                   3: [scaled(1, n1, 2, 3)]})
    t_v2 = list(done2)
    t_qt4 = t_qt[3]

    QM = nc.alloc_sbuf_tensor_at("QM", [128, 8, S], F32, offset=g1_at)
    t_qm = []

    def mla_heads():
        T.w(t_l, t_ml)
        V.w(t_ml)
        for tt in range(NT):
            ts = slice(tt * 128, tt * 128 + 128)
            bq = bank()
            t1 = T(mm_group(bq[:, 0:384], lambda k: qlT[:, k, ts], lambda k: wuq[:, k, :], 2))
            bk = bank()
            t2 = T(pe.matmul(bk[:, :], kvT[:, ts], wukv[:, :], start=True, stop=True))
            yield
            QK, qt = B_QK.take()
            A.w(t1, t2, qt)
            tk = A(a.copy(QK[:, 0:4, :], bq[:, 0:384].rearrange("p (h c) -> p h c", h=4)))
            PS.give(bq, tk)
            kv = bk[:, :].rearrange("p (h c) -> p h c", h=4)
            A(a.copy(QK[:, 4:8, 0:64], kv[:, :, 0:64]))
            tk = A(a.copy(vm[:, tt, :].rearrange("p (h c) -> p h c", h=4), kv[:, :, 64:128]))
            PS.give(bk, tk)
            V.w(tk, qt)
            tk = V(v.tensor_copy(QK[:, 4:8, 64:96], P2[:, tt, 1152:1184].unsqueeze(1).to_broadcast([128, 4, 32])))
            T_ = P2[:, tt, 0:512]
            V.w(t_qt4)
            V(v.tensor_tensor(T_[:, 0:480].rearrange("p (h c) -> p h c", h=5), QK[:, 0:5, :], QK[:, 0:5, :], MUL))
            V(v.tensor_reduce(sm3[:, tt, 0:5], T_[:, 0:480].rearrange("p (h c) -> p h c", h=5), AX.X, ADD))
            V(v.tensor_tensor(T_[:, 0:288].rearrange("p (h c) -> p h c", h=3), QK[:, 5:8, :], QK[:, 5:8, :], MUL))
            V(v.tensor_reduce(sm3[:, tt, 5:8], T_[:, 0:288].rearrange("p (h c) -> p h c", h=3), AX.X, ADD))
            tk = V(v.tensor_scalar(sm3[:, tt, 0:8], sm3[:, tt, 0:8], 1.0 / 96, 1e-6, MUL, ADD))
            G.w(tk)
            tk = G(g.tensor_tensor(sm3[:, tt, 8:16], sm3[:, tt, 0:8], mh2[:, 0, 0:8], ALU.pow))
            yield
            V.w(tk)
            V(v.tensor_tensor(QK[:, :, :], QK[:, :, :], sm3[:, tt, 8:16].unsqueeze(2).to_broadcast([128, 8, 96]), MUL))
            for i in range(2):
                V(v.tensor_tensor(QK[:, i * 4:i * 4 + 4, :], QK[:, i * 4:i * 4 + 4, :],
                                  mrow[:, i, :].unsqueeze(1).to_broadcast([128, 4, 96]), MUL))
            cs = cc("rcos")[:, tt * 16:tt * 16 + 16].unsqueeze(1).to_broadcast([128, 8, 16])
            sn = cc("rsin")[:, tt * 16:tt * 16 + 16].unsqueeze(1).to_broadcast([128, 8, 16])
            x1, x2 = QK[:, :, 64:80], QK[:, :, 80:96]
            u1, u2, u3 = (T_[:, i * 128:i * 128 + 128].rearrange("p (h c) -> p h c", h=8) for i in range(3))
            V(v.tensor_tensor(u1, x1, cs, MUL))
            V(v.tensor_tensor(u2, x2, sn, MUL))
            V(v.tensor_tensor(u3, x1, sn, MUL))
            V(v.tensor_tensor(x1, u1, u2, SUB))
            V(v.tensor_tensor(u1, x2, cs, MUL))
            tk = V(v.tensor_tensor(x2, u1, u3, ADD))
            yield
            T.w(tk)
            for i in range(2):
                b = bank()
                for j in range(4):
                    m = pe.transpose(b[0:96, j * 128:j * 128 + 128], QK[:, i * 4 + j, :], ident)
                tk = T(m)
                tk2 = evac(QM[0:96, i * 4:i * 4 + 4, ts], b[0:96, :].rearrange("p (h c) -> p h c", h=4), after=tk)
                PS.give(b, tk2)
                t_qm.append(tk2)
            B_QK.give(QK, tk)
            yield

    mixed = A1
    B_bi = [(sb(f"bi{i}", [128, S], stack=RT), Lane(sem(f"s_bi{i}"))) for i in range(2)]
    P_bi = Pool(B_bi)
    B_s2 = bufs("s2_", 3, [128, S], RT)
    B_t2 = bufs("t2_", 2, [128, S], RT)
    order = [(0, h) for h in range(4)] + [(2, h) for h in range(4)] + [(3, h) for h in range(4)] + [(1, h) for h in range(4)]
    biases = {}

    def load_bias(n):
        if n < 12:
            (x, lane), tk = P_bi.take()
            G.w(tk)
            biases[n] = (x, lane, lane(nc.gpsimd.dma_start(x[:, :], t["biases"][n])))

    G.w(T.last())
    load_bias(0)
    load_bias(1)
    state["taken"] = n_moe_end + 5
    items = []
    for hn, (mx, h) in enumerate(order):
        for i in range(4):
            items.append({"m": mx, "h": h, "i": i, "hn": hn, "n": len(items)})

    def q_k_v(mx, h):
        r = slice((h % 2) * 64, (h % 2) * 64 + 64)
        if mx == 0:
            return QT[r, h // 2, :], QT[r, 2 + h // 2, :], lambda j: P2[:, j, 512 + h * 64:576 + h * 64]
        if mx == 2:
            return QT[r, 4 + h // 2, :], QT[r, 6 + h // 2, :], lambda j: P2[:, j, 1696 + h * 64:1760 + h * 64]
        if mx == 3:
            r = slice((h // 2) * 64, (h // 2) * 64 + 64)
            return QT[r, 8 + h % 2, :], QT[r, 10, :], lambda j: P2[:, j, 2336 + (h // 2) * 64:2400 + (h // 2) * 64]
        return QM[0:96, h, :], QM[0:96, 4 + h, :], lambda j: vm[:, j, h * 64:h * 64 + 64]

    def a1(it):
        i, mx = it["i"], it["m"]
        q, k_, _ = q_k_v(mx, it["h"])
        j0 = max(0, i - 1) if mx == 3 else 0
        kn = (i + 1 - j0) * 128
        it["j0"], it["kn"] = j0, kn
        b = bank()
        tk = T(pe.matmul(b[:, 0:kn], q[:, i * 128:i * 128 + 128], k_[:, j0 * 128:(i + 1) * 128], start=True, stop=True))
        s, stk = B_s2.take()
        sm = stm[:, it["n"] % 16, :]
        if it["n"] >= 16:
            V.w(items[it["n"] - 16]["done"])
        V.w(tk, stk)
        if mx == 1:
            bias, scale = cc("causal"), 96.0 ** -0.5
        else:
            x, lane, bt = biases[it["hn"]]
            V.w(bt)
            bias, scale = x[:, :], 1.0
        tk = V(v.tensor_tensor_reduce(s[:, 0:kn], b[:, 0:kn], bias[:, 512 - kn:512], 1.0, -3e38, ADD, MAX, sm[:, 0:1]))
        PS.give(b, tk)
        if mx != 1 and i == 3:
            P_bi.give((x, lane), tk)
            load_bias(it["hn"] + 2)
        if mx == 3:
            V(v.tensor_tensor(sm[:, 0:1], sm[:, 0:1], scv("swa_sinks_2")[:, it["h"]:it["h"] + 1], MAX))
        tk = V(v.tensor_scalar(sm[:, 1:2], sm[:, 0:1], -scale, None, MUL))
        A.w(tk)
        tk = A(a.activation(s[:, 0:kn], s[:, 0:kn], ACT.Exp, scale=scale, bias=sm[:, 1:2], accum_out=sm[:, 2:3]))
        it["s"], it["ts"] = s, tk
        if mx == 3:
            tk = A(a.activation(sm[:, 3:4], scv("swa_sinks_2")[:, it["h"]:it["h"] + 1], ACT.Exp, bias=sm[:, 1:2]))
            it["te"] = tk

    def a2(it):
        nb = it["kn"] // 128
        s = it["s"]
        sm = stm[:, it["n"] % 16, :]
        b = bank()
        T.w(it["ts"])
        for j in range(nb):
            m = pe.transpose(b[:, j * 128:j * 128 + 128], s[:, j * 128:j * 128 + 128], ident)
        tk = T(m)
        B_s2.give(s, tk)
        wt, wtt = B_t2.take()
        V.w(it["ts"])
        if it["m"] == 3:
            V.w(it["te"])
            V(v.tensor_tensor(sm[:, 2:3], sm[:, 2:3], sm[:, 3:4], ADD))
        V(v.reciprocal(sm[:, 4:5], sm[:, 2:3]))
        it["trc"] = V.last()
        A.w(tk, wtt)
        tk = A(a.copy(wt[:, 0:it["kn"]], b[:, 0:it["kn"]]))
        PS.give(b, tk)
        it["wt"], it["twt"] = wt, tk

    def a3(it):
        _, _, vv = q_k_v(it["m"], it["h"])
        b = bank()
        T.w(it["twt"])
        tk = T(mm_group(b[:, 0:64], lambda j: it["wt"][:, j * 128:j * 128 + 128], lambda j: vv(it["j0"] + j),
                        it["kn"] // 128))
        B_t2.give(it["wt"], tk)
        A.w(tk, it["trc"])
        c0 = it["m"] * 256 + it["h"] * 64
        tk = A(a.activation(mixed[:, it["i"], c0:c0 + 64], b[:, 0:64], ACT.Copy, scale=stm[:, it["n"] % 16, 4:5]))
        it["done"] = tk
        PS.give(b, tk)

    gn = {}

    def group_squares(m_, junk=None):
        A.w(t_l, gn.get("n2"))
        for tt in range(NT):
            j_ = P2[:, tt, 768:1024] if junk is None else junk[:, tt, 0:256]
            gn["t"] = A(a.activation(j_, mixed[:, tt, m_ * 256:m_ * 256 + 256], ACT.Square,
                                     scale=1.0 / 16, accum_out=ss2[:, tt, m_:m_ + 1]))

    def group_root(m_):
        V.w(gn["t"])
        tk = V(v.tensor_scalar(ss2[:, :, m_:m_ + 1], ss2[:, :, m_:m_ + 1], 1e-6, None, ADD))
        G.w(tk)
        gn["r"] = G(g.tensor_tensor(rs2[:, :, m_:m_ + 1], ss2[:, :, m_:m_ + 1], mh2[:, :, m_:m_ + 1], ALU.pow))

    def group_scaled(m_):
        V.w(gn["r"])
        for tt in range(NT):
            mv = mixed[:, tt, m_ * 256:m_ * 256 + 256]
            tk = V(v.tensor_scalar(mv, mv, rs2[:, tt, m_:m_ + 1], None, MUL))
        return tk

    def attention2(n0, n1):
        for n in range(n0, n1):
            if n == 32:
                T.w(t_qt)
            if n == 48:
                T.w(t_qm)
            for lag, f in ((2, a2), (3, a3), (0, a1)):
                if 0 <= n - lag < len(items):
                    f(items[n - lag])
            for lag, f in ((4, group_squares), (5, group_root), (6, group_scaled)):
                if n > 16 and n % 16 == lag:
                    f(order[(n - 16) // 16 * 4][0])
            yield

    T.w(t_qt, t_v2)
    mla = mla_heads()

    def with_mla(n0, n1):
        for n in range(n0, n1):
            if n % 2 == 0:
                next(mla, None)
            run(attention2(n, n + 1))

    with_mla(0, 8)
    turn_heads(*DIL, n1)
    with_mla(8, 14)
    T.w(t_qt)
    with_mla(14, 22)
    V.w(t_l)
    n2 = []
    heads_squares(2, (0, 1))
    with_mla(22, 23)
    heads_squares(2, (2, 3))
    tk2 = heads_root(2)
    with_mla(23, 25)
    for tt in range(NT):
        n2.append(heads_scaled(2, tt, tk2))
        with_mla(25 + tt, 26 + tt)
    gn["n2"] = n2
    for r in range(2):
        t_qt.append(turn4(QT[:, 8 + r, :], lambda tt: P2[:, tt, 1952 + r * 128:2080 + r * 128], col("swa_q_g_2"), n2))
    t_qt.append(turn4(QT[:, 10, :], lambda tt: P2[:, tt, 2208:2336], col("swa_k_g_2"), n2))
    with_mla(29, 45)
    run(mla)
    run(attention2(45, 67))
    fence()
    WN = Arena(work0 + 16384, high)
    B_wh = Pool([sb(f"whi{i}", [128, 4096], F32R, stack=WN) for i in range(2)])
    H3 = [sb(f"H3{i}", [128, 8, S], F32R, stack=WN) for i in "hl"]
    B_r = bufs("relu", 2, [128, S], WN)
    B_r.give(cc("causal"), V.last())
    RC = Arena(region_a + 16384, region_a + 65536)
    MT = [sb(f"MT{i}", [128, 8, S], F32R, stack=RC) for i in "hl"]
    N3 = sb("N3", [128, NT, D], stack=RC)
    plan = [(8, 512)] * 2 + ([(8, 512)] * 4 + [(4, 1024)] * 4) * 2
    at = {"n": 0}

    def following():
        at["n"] += 1
        return prepare(*plan[at["n"] - 1], B_wh) if at["n"] <= len(plan) else None

    group_squares(order[12][0], N3)
    group_root(order[12][0])
    nxt = following()
    split_part(nxt, 0)
    t_m = {}
    t_n2 = None
    K_ORDER = (0, 1, 4, 5, 6, 7, 2, 3)
    for n, k in enumerate(K_ORDER):
        if n in (2, 4, 6):
            split_part(nxt, n // 2)
        if n == 4:
            t_n2 = group_scaled(order[12][0])
        b = bank()
        for tt in range(NT):
            T.w(t_n2)
            m = pe.transpose(b[:, tt * 128:tt * 128 + 128], mixed[:, tt, k * 128:k * 128 + 128], ident)
        tk = T(m)
        A.w(tk)
        tk = A(a.activation(MT[0][:, k, :], b[:, :], ACT.Copy, scale=col("group_out_g_2", k)))
        V.w(tk)
        tk = V(v.scalar_tensor_tensor(MT[1][:, k, :], b[:, :], col("group_out_g_2", k), MT[0][:, k, :], MUL, SUB))
        PS.give(b, tk)
        t_m[k] = tk

    def pair_of(x, k, c):
        return x[0][:, k, c], x[1][:, k, c]

    def wpair(rec, k, c):
        return rec["vh"][:, k, c], rec["vl"][:, k, c]

    def tk128(tt):
        return slice(tt * 128, tt * 128 + 128)

    tx = [None] * NT
    t_n3, t_h = [None] * NT, []
    for half in range(2):
        rec, nxt = nxt, following()
        for tt in range(NT + half):
            if tt < NT:
                split_part(nxt, tt)
                b = bank()
                for n, k in enumerate(K_ORDER):
                    T.w(t_m[k], rec["tok"][k // 2])
                    tk = T(mm3(b[:, :], lambda _: pair_of(MT, k, tk128(tt)), lambda _: wpair(rec, k, slice(0, 512)), 1,
                               start=n == 0, stop=n == 7))
                V.w(tk)
                xv = X2[:, tt, half * 512:half * 512 + 512]
                tx[tt] = V(v.tensor_tensor(xv, xv, b[:, :], ADD))
                PS.give(b, tx[tt])
                if tt == NT - 1:
                    retire(rec, tk)
                if half:
                    t_n3[tt] = norm_end(N3, X2, tt, norm_start(N3[:, tt, :], X2, tt, tx[tt], 80), 80)
            if half and tt:
                t_h += turn_split(H3, N3, tt - 1, t_n3[tt - 1], "mlp_norm_g_2", B_r)
    fence()

    UA = Arena(region_a, region_a + 65536)
    UU = [sb(f"UU{i}", [128, 16, S], F32R, stack=UA) for i in "hl"]
    T.w(t_h)
    lo_ = Lane(sem("s_out"))
    ov = out.rearrange("a (n p) d -> p (a n) d", p=128)
    t_down = [None] * 4
    for part in range(2):
        t_u = []
        squares = []

        def rest():
            f, u, tk = squares.pop(0)
            A.w(tk, t_down[f // 4])
            tk = A(a.copy(UU[0][:, f, :], u[:, :]))
            V.w(tk, t_down[f // 4])
            tk = V(v.tensor_tensor(UU[1][:, f, :], u[:, :], UU[0][:, f, :], SUB))
            B_r.give(u, tk)
            t_u.append(tk)

        for c in range(4):
            rec, nxt = nxt, following()
            T.w(rec["tok"])
            for j in range(4):
                split_part(nxt, j)
                b = bank()
                tk = T(mm3(b[:, :], lambda k: wpair(rec, k, tk128(j)), lambda k: pair_of(H3, k, slice(0, S)), 8))
                r, rt = B_r.take()
                A.w(tk, rt)
                tr = A(a.activation(r[:, :], b[:, :], ACT.Relu))
                PS.give(b, tr)
                V.w(tr)
                tu = V(v.tensor_tensor(r[:, :], r[:, :], r[:, :], MUL))
                squares.append((c * 4 + j, r, tu))
                if len(squares) == 2:
                    rest()
            retire(rec, tk)
        rest()
        acc8 = [bank() for _ in range(8)]
        tk8 = [None] * 8
        for c in range(4):
            rec, nxt = nxt, following()
            T.w(rec["tok"], t_u[c * 4:c * 4 + 4])
            for i in range(8):
                tt, half = i // 2, i % 2
                if i < 4:
                    split_part(nxt, i)
                tk8[i] = T(mm3(acc8[i][:, :], lambda k: pair_of(UU, c * 4 + k, tk128(tt)),
                               lambda k: wpair(rec, k, slice(half * 512, half * 512 + 512)), 4, start=c == 0, stop=c == 3))
            t_down[c] = tk8[7]
            retire(rec, tk8[7])
        for i in range(8):
            tt, half = i // 2, i % 2
            xv = X2[:, tt, half * 512:half * 512 + 512]
            V.w(tk8[i])
            tk = V(v.tensor_tensor(xv, xv, acc8[i][:, :], ADD))
            PS.give(acc8[i], tk)
            if part:
                SP.w(tk)
                t_out = lo_(nc.sync.dma_start(ov[:, tt, half * 512:half * 512 + 512], xv))
    SP.w(t_out)


NAMES = ["x", "positions", "norm_mix_w", "w_in", "conv_w", "conv_b", "dt_bias", "a_log", "d_skip", "ssd_norm_w",
         "lambda_q1", "lambda_k1", "lambda_q2", "lambda_k2", "subln_w", "w_branch_attn", "w_branch_ssd", "w_out",
         "norm_ffn_w", "w_group_router", "b_group_router", "w_expert_router", "b_expert_router", "w_expert_gate",
         "w_expert_up", "w_expert_down", "final_norm_w", "attn_norm_g_2", "w_in_2", "moba_q_g_2", "moba_k_g_2",
         "mla_qlat_g_2", "mla_kvlat_g_2", "mla_w_uq_2", "mla_w_ukv_2", "mla_q_g_2", "mla_k_g_2", "dil_q_g_2",
         "dil_k_g_2", "swa_q_g_2", "swa_k_g_2", "swa_sinks_2", "group_out_g_2", "w_o_2", "mlp_norm_g_2", "w_up_2",
         "w_down_2"]


def kernel(**inputs):
    import concourse.bacc as bacc
    from concourse.bass_utils import run_bass_kernel_spmd

    nc = bacc.Bacc("TRN2", target_bir_lowering=False, num_devices=1)
    consts, biases = constants()
    arrays, t = {}, {}
    for name, value in [("consts", consts), ("biases", biases)] + [(n, inputs[n]) for n in NAMES]:
        value = np.ascontiguousarray(value)
        arrays["in_" + name] = value
        t[name] = nc.dram_tensor("in_" + name, value.shape, mybir.dt.from_np(value.dtype), kind="ExternalInput").ap()
    out = nc.dram_tensor("out_0", (1, S, D), F32, kind="ExternalOutput").ap()
    build(nc, t, out)
    result = run_bass_kernel_spmd(nc, [arrays], core_ids=[0])
    return result.results[0]["out_0"]
```
